# Optimizing a Trainium2 kernel written in Bass

```python
import math
import jax, jax.numpy as jnp
from jax import lax
import numpy as np

D_MODEL = 1024
BATCH = 1
SEQ = 256
DEPTH = 1

MEM_LEN = 256
POOL_WINDOWS = (2, 4, 8, 16)
N_POOL_GROUPS = 4
D_POOL = D_MODEL
POOL_GROUP = D_POOL // N_POOL_GROUPS
D_LRU = D_MODEL
N_LRU_HEADS = 4
LRU_BLOCK = D_LRU // N_LRU_HEADS
CONV_WIDTH = 4
RG_C = 8.0
N_XATTN_HEADS = 4
XATTN_HEAD_DIM = D_MODEL // N_XATTN_HEADS
N_EXPERTS = 32
TOP_K = 4
D_EXPERT = D_MODEL
SWIGLU_LIMIT = 7.0
SWIGLU_ALPHA = 1.702
EXPERT_BLOCK = 256
RMS_EPS = 1e-6
OFF_POOL = 0
OFF_LRU_X = OFF_POOL + D_POOL
OFF_LRU_Y = OFF_LRU_X + D_LRU
OFF_GATE_A = OFF_LRU_Y + D_LRU
OFF_GATE_B = OFF_GATE_A + D_MODEL
D_IN_TOTAL = OFF_GATE_B + D_MODEL

kernel_name = "hybrid_pool_rglru_xattn_moe"

def rms_norm(x, g):
    xf = x.astype(jnp.float32)
    y = xf * lax.rsqrt(jnp.mean(xf * xf, axis=-1, keepdims=True) + RMS_EPS)
    return (y * g.astype(jnp.float32)).astype(x.dtype)

def pool_mixer(u, w_group, scale):
    B_, S_, _ = u.shape
    uf = u.astype(jnp.float32)
    cs0 = jnp.pad(jnp.cumsum(uf, axis=1), ((0, 0), (1, 0), (0, 0)))
    t = jnp.arange(S_)
    outs = []
    for gi, w in enumerate(POOL_WINDOWS):
        lo, hi = gi * POOL_GROUP, (gi + 1) * POOL_GROUP
        c = cs0[:, :, lo:hi]
        lagged = jnp.pad(c[:, :S_ - w + 1], ((0, 0), (w - 1, 0), (0, 0)))
        cnt = jnp.minimum(t + 1, w).astype(jnp.float32)[None, :, None]
        outs.append((c[:, 1:] - lagged) / cnt - uf[:, :, lo:hi])
    p = jnp.stack(outs, axis=2).astype(u.dtype)
    p = jnp.einsum('bsgi,gij->bsgj', p, w_group).reshape(B_, S_, D_POOL)
    return p * scale

def causal_depthwise_conv(u, conv_w, conv_b):
    C = u.shape[-1]
    out = lax.conv_general_dilated(
        u, conv_w[:, None, :].astype(u.dtype), window_strides=(1,),
        padding=[(CONV_WIDTH - 1, 0)], dimension_numbers=('NWC', 'WIO', 'NWC'),
        feature_group_count=C)
    return out + conv_b

def rg_lru(xr, w_a, b_a, w_x, b_x, lam):
    B_, S_, C = xr.shape
    xh = xr.reshape(B_, S_, N_LRU_HEADS, LRU_BLOCK)
    r = jax.nn.sigmoid(jnp.einsum('bshi,hij->bshj', xh, w_a).reshape(B_, S_, C) + b_a).astype(jnp.float32)
    i = jax.nn.sigmoid(jnp.einsum('bshi,hij->bshj', xh, w_x).reshape(B_, S_, C) + b_x).astype(jnp.float32)
    log_a = RG_C * r * jax.nn.log_sigmoid(lam.astype(jnp.float32))
    a = jnp.exp(log_a)
    mult = jnp.sqrt(jnp.maximum(1.0 - jnp.exp(2.0 * log_a), 0.0))
    mult = jnp.where((jnp.arange(S_) == 0)[None, :, None], 1.0, mult)
    b = mult * i * xr.astype(jnp.float32)

    def combine(left, right):
        a1, b1 = left
        a2, b2 = right
        return a1 * a2, a2 * b1 + b2

    _, hs = lax.associative_scan(combine, (a, b), axis=1)
    return hs.astype(xr.dtype)

def hybrid_mixer(h, w_in, w_pool_group, pool_scale, w_pool_proj, conv_w, conv_b,
                 lru_w_a, lru_b_a, lru_w_x, lru_b_x, lru_lambda, w_lru_proj, w_mix_out):
    z = h @ w_in
    u_pool = z[..., OFF_POOL:OFF_LRU_X]
    u_lru = z[..., OFF_LRU_X:OFF_LRU_Y]
    u_gelu = z[..., OFF_LRU_Y:OFF_GATE_A]
    g_a = z[..., OFF_GATE_A:OFF_GATE_B]
    g_b = z[..., OFF_GATE_B:D_IN_TOTAL]
    y_a = pool_mixer(u_pool, w_pool_group, pool_scale) @ w_pool_proj
    xr = causal_depthwise_conv(u_lru, conv_w, conv_b)
    hr = rg_lru(xr, lru_w_a, lru_b_a, lru_w_x, lru_b_x, lru_lambda)
    y_b = (hr * jax.nn.gelu(u_gelu)) @ w_lru_proj
    m = jax.nn.sigmoid(g_a) * y_a + jax.nn.sigmoid(g_b) * y_b
    return m @ w_mix_out

def cross_attention(hq, memn, w_q, w_kv, w_o):
    B_, S_, _ = hq.shape
    M = memn.shape[1]
    q = (hq @ w_q).reshape(B_, S_, N_XATTN_HEADS, XATTN_HEAD_DIM)
    kv = (memn @ w_kv).reshape(B_, M, 2, N_XATTN_HEADS, XATTN_HEAD_DIM)
    k, v = kv[:, :, 0], kv[:, :, 1]
    s = jnp.einsum('bqhd,bkhd->bhqk', q, k).astype(jnp.float32) * (XATTN_HEAD_DIM ** -0.5)
    p = jax.nn.softmax(s, axis=-1).astype(v.dtype)
    o = jnp.einsum('bhqk,bkhd->bqhd', p, v).reshape(B_, S_, D_MODEL)
    return o @ w_o

def clamped_swiglu(hgu):
    g, u = hgu[..., :D_EXPERT], hgu[..., D_EXPERT:]
    g = jnp.minimum(g, SWIGLU_LIMIT)
    u = jnp.clip(u, -SWIGLU_LIMIT, SWIGLU_LIMIT)
    return (u + 1.0) * (g * jax.nn.sigmoid(SWIGLU_ALPHA * g))

def moe(xn, w_router, b_router, w_gate_up, b_gate_up, w_down, b_down):
    T = xn.shape[0]
    A = T * TOP_K
    logits = (xn @ w_router + b_router).astype(jnp.float32)
    top_val, top_idx = lax.top_k(logits, TOP_K)
    gates = jax.nn.softmax(top_val, axis=-1)
    flat_e = top_idx.reshape(-1).astype(jnp.int32)
    flat_tok = jnp.arange(A, dtype=jnp.int32) // TOP_K
    flat_g = gates.reshape(-1)
    order = jnp.argsort(flat_e)
    s_e, s_tok, s_g = flat_e[order], flat_tok[order], flat_g[order]
    counts = jnp.bincount(flat_e, length=N_EXPERTS).astype(jnp.int32)
    padded = (counts + EXPERT_BLOCK - 1) // EXPERT_BLOCK * EXPERT_BLOCK
    start = jnp.cumsum(counts) - counts
    pend = jnp.cumsum(padded)
    pstart = pend - padded
    dest = pstart[s_e] + (jnp.arange(A, dtype=jnp.int32) - start[s_e])
    n_blocks = -(-(A + N_EXPERTS * (EXPERT_BLOCK - 1)) // EXPERT_BLOCK)
    P = n_blocks * EXPERT_BLOCK
    tok_buf = jnp.zeros((P,), jnp.int32).at[dest].set(s_tok)
    gate_buf = jnp.zeros((P,), xn.dtype).at[dest].set(s_g.astype(xn.dtype))
    block_start = jnp.arange(n_blocks, dtype=jnp.int32) * EXPERT_BLOCK
    block_e = jnp.minimum(jnp.searchsorted(pend, block_start, side='right'), N_EXPERTS - 1)

    def expert_block(args):
        tok, e = args
        xb = xn[tok]
        hact = clamped_swiglu(xb @ w_gate_up[e] + b_gate_up[e])
        return hact @ w_down[e] + b_down[e]

    out = lax.map(expert_block, (tok_buf.reshape(n_blocks, EXPERT_BLOCK), block_e))
    out = out.reshape(P, D_MODEL) * gate_buf[:, None]
    return jnp.zeros_like(xn).at[tok_buf].add(out)

def setup_inputs(seed: int = 0) -> dict:
    key = jax.random.key(seed)
    ks = jax.random.split(key, 32)

    def nrm(k, shape, fan_in):
        return jax.random.normal(k, shape, jnp.float32) * (fan_in ** -0.5)

    def gain(k, shape):
        return 1.0 + 0.05 * jax.random.normal(k, shape, jnp.float32)

    def small(k, shape):
        return 0.01 * jax.random.normal(k, shape, jnp.float32)

    L = DEPTH
    a_init = jax.random.uniform(ks[11], (L, D_LRU), jnp.float32, minval=0.9, maxval=0.999)
    s_init = a_init ** (1.0 / RG_C)
    lru_lambda = jnp.log(s_init) - jnp.log1p(-s_init)
    return {
        "x": jax.random.normal(ks[0], (BATCH, SEQ, D_MODEL), jnp.float32),
        "mem": jax.random.normal(ks[1], (BATCH, MEM_LEN, D_MODEL), jnp.float32),
        "norm_mix": gain(ks[2], (L, D_MODEL)),
        "w_in": nrm(ks[3], (L, D_MODEL, D_IN_TOTAL), D_MODEL),
        "w_pool_group": nrm(ks[4], (L, N_POOL_GROUPS, POOL_GROUP, POOL_GROUP), POOL_GROUP),
        "pool_scale": gain(ks[5], (L, D_POOL)),
        "w_pool_proj": nrm(ks[6], (L, D_POOL, D_MODEL), D_POOL),
        "conv_w": nrm(ks[7], (L, CONV_WIDTH, D_LRU), CONV_WIDTH),
        "conv_b": small(ks[8], (L, D_LRU)),
        "lru_w_a": nrm(ks[9], (L, N_LRU_HEADS, LRU_BLOCK, LRU_BLOCK), LRU_BLOCK),
        "lru_b_a": small(ks[10], (L, D_LRU)),
        "lru_w_x": nrm(ks[12], (L, N_LRU_HEADS, LRU_BLOCK, LRU_BLOCK), LRU_BLOCK),
        "lru_b_x": small(ks[13], (L, D_LRU)),
        "lru_lambda": lru_lambda,
        "w_lru_proj": nrm(ks[14], (L, D_LRU, D_MODEL), D_LRU),
        "w_mix_out": nrm(ks[15], (L, D_MODEL, D_MODEL), D_MODEL),
        "norm_xattn": gain(ks[16], (L, D_MODEL)),
        "norm_mem": gain(ks[17], (L, D_MODEL)),
        "w_q": nrm(ks[18], (L, D_MODEL, D_MODEL), D_MODEL),
        "w_kv": nrm(ks[19], (L, D_MODEL, 2 * D_MODEL), D_MODEL),
        "w_o": nrm(ks[20], (L, D_MODEL, D_MODEL), D_MODEL),
        "norm_moe": gain(ks[21], (L, D_MODEL)),
        "w_router": nrm(ks[22], (L, D_MODEL, N_EXPERTS), D_MODEL),
        "b_router": small(ks[23], (L, N_EXPERTS)),
        "w_gate_up": nrm(ks[24], (L, N_EXPERTS, D_MODEL, 2 * D_EXPERT), D_MODEL),
        "b_gate_up": small(ks[25], (L, N_EXPERTS, 2 * D_EXPERT)),
        "w_down": nrm(ks[26], (L, N_EXPERTS, D_EXPERT, D_MODEL), D_EXPERT),
        "b_down": small(ks[27], (L, N_EXPERTS, D_MODEL)),
        "norm_final": gain(ks[28], (D_MODEL,)),
    }

def reference(x, mem, norm_mix, w_in, w_pool_group, pool_scale, w_pool_proj, conv_w, conv_b,
              lru_w_a, lru_b_a, lru_w_x, lru_b_x, lru_lambda, w_lru_proj, w_mix_out,
              norm_xattn, norm_mem, w_q, w_kv, w_o, norm_moe, w_router, b_router,
              w_gate_up, b_gate_up, w_down, b_down, norm_final):
    B_, S_, D_ = x.shape
    for l in range(DEPTH):
        x = x + hybrid_mixer(rms_norm(x, norm_mix[l]), w_in[l], w_pool_group[l], pool_scale[l],
                             w_pool_proj[l], conv_w[l], conv_b[l], lru_w_a[l], lru_b_a[l],
                             lru_w_x[l], lru_b_x[l], lru_lambda[l], w_lru_proj[l], w_mix_out[l])
        memn = rms_norm(mem, norm_mem[l])
        x = x + cross_attention(rms_norm(x, norm_xattn[l]), memn, w_q[l], w_kv[l], w_o[l])
        xn = rms_norm(x, norm_moe[l]).reshape(B_ * S_, D_)
        x = x + moe(xn, w_router[l], b_router[l], w_gate_up[l], b_gate_up[l],
                    w_down[l], b_down[l]).reshape(B_, S_, D_)
    return rms_norm(x, norm_final)


_drawn_inputs = setup_inputs


def setup_inputs(seed=0):
    import zlib

    import numpy as np

    out = dict(_drawn_inputs(seed))
    spreads = {}
    factors = {'lru_b_a': 27.382, 'lru_b_x': 21.569, 'norm_xattn': 8.0, 'b_gate_up': 8.0, 'b_down': 8.0}
    for name, (base, spread) in spreads.items():
        noise = np.random.default_rng([zlib.crc32(name.encode()), seed]).standard_normal(out[name].shape)
        drawn = base * np.exp(spread * noise) if base else spread * noise
        out[name] = __import__('jax').numpy.asarray(drawn.astype(out[name].dtype))
    for name, factor in factors.items():
        out[name] = (out[name] * factor).astype(out[name].dtype)
    return out
```

```python
from contextlib import ExitStack

import concourse.bass as bass
from concourse import mybir

F32 = mybir.dt.float32
F32R = mybir.dt.float32r
BF16 = mybir.dt.bfloat16
I32 = mybir.dt.int32
U32 = mybir.dt.uint32
ALU = mybir.AluOpType
ACT = mybir.ActivationFunctionType
AX = mybir.AxisListType

P = 128
D = 1024
KT = D // P
T = 256
TT = T // P
HEADS = 4
HD = D // HEADS
WINDOWS = (2, 4, 8, 16)
PAD = max(WINDOWS)
CONV = 4
EPS = 1e-6
EXPERTS = 32
TOPK = 4
LIMIT = 7.0
ALPHA = 1.702
CHUNK = 2048
BANK = 512

SLOTS = 64
ROUNDS = T // SLOTS
GU_CHUNKS = KT
DN_CHUNKS = KT // 2
PER_EXPERT = GU_CHUNKS + DN_CHUNKS
RAW = 6
SPL = 4
BLOCKS = EXPERTS + 1
SPLIT = 3 * BANK

COLS = ["norm_mix", "norm_mem", "norm_xattn", "norm_moe", "pool_scale", "conv_b", "lru_b_a", "lru_b_x",
        "lru_lambda", "conv_w"]
COL = {name: KT * i for i, name in enumerate(COLS)}
NCOL = KT * (len(COLS) - 1 + CONV)

CONST = {}
_at = 0
for _name, _n in (("ident", P), ("fold", SLOTS), ("before", P), ("ones", P), ("iota", T), ("inv", len(WINDOWS) * PAD)):
    CONST[_name] = (_at, _at + _n)
    _at += _n
NCONST = _at

DENSE = {}
_at = 0
for _name, _n in (("k", 4), ("v", 4), ("lrux", 4), ("pool", 4), ("ra", 1), ("rx", 1), ("grp", 1), ("gelu", 4),
                  ("ga", 4), ("gb", 4), ("pp", 4), ("lp", 4), ("mix", 4), ("q", 4), ("o", 4)):
    DENSE[_name] = _at
    _at += _n
NDENSE = _at

UNIT, EVAC = {}, []
for _name, _n, _eng in (("memT", 4, "dve"), ("k", 4, "dve"), ("v", 4, "act"), ("xT", 4, "dve"), ("lrux", 4, "dve"),
                        ("pool", 4, "act"), ("ra", 4, "act"), ("rx", 4, "act"), ("grp", 4, "dve"),
                        ("gelu", 4, "act"), ("ga", 4, "act"), ("gb", 4, "act"), ("pp", 4, "dve"), ("lp", 4, "dve"),
                        ("mix", 4, "dve"), ("x1T", 4, "dve"), ("q", 4, "dve"), ("score", 4, "act"), ("pT", 4, "act"),
                        ("oT", 4, "dve"), ("o", 4, "dve"), ("xnT", 4, "dve"), ("logit", 1, "dve"), ("rank", 1, "dve"),
                        ("gT", 1, "dve"), ("bd", 4, "dve")):
    UNIT[_name] = len(EVAC)
    EVAC += [_eng] * _n
NUNIT = len(EVAC)


def evacuated(unit):
    return EVAC[unit], EVAC[: unit + 1].count(EVAC[unit])


TOKEN_MAJOR = ("v", "mix", "o")
CHUNKS_0 = len(TOKEN_MAJOR) * (KT // 2 - 1)


def dense_used():
    used, partial = [], 0
    names = list(DENSE)
    for i, name in enumerate(names):
        count = (DENSE[names[i + 1]] if i + 1 < len(names) else NDENSE) - DENSE[name]
        for j in range(count):
            if name in TOKEN_MAJOR and j < count - 1:
                partial += 1
                used.append(("chunk_used", partial))
            elif name in TOKEN_MAJOR or count == 1:
                used.append(("unit_done", UNIT[name] + 4))
            else:
                used.append(("unit_done", UNIT[name] + j + 1))
    return used


def build(nc, x, mem, cols, consts, dense, bgu, b_router, w_router, norm_final, w_gate_up, w_down, b_down, out):
    ctx = ExitStack()
    sb = lambda name, shape, dt=F32: ctx.enter_context(nc.sbuf_tensor(name, shape, dt))
    sem = lambda name: ctx.enter_context(nc.semaphore(name))
    with ctx:
        scratch = nc.dram_tensor("expert_rows", (BLOCKS * SLOTS, D), F32, kind="Internal").ap()

        raw = sb("raw", [P, RAW, CHUNK])
        whi = sb("whi", [P, SPL, SPLIT], F32R)
        wlo = sb("wlo", [P, SPL, SPLIT], F32R)
        xpair = sb("xpair", [P, KT, 2 * SLOTS], F32R)
        hpair = sb("hpair", [P, KT, 2 * SLOTS], F32R)
        res = sb("res", [P, TT, D])
        cst = sb("cst", [P, NCONST])
        col = sb("col", [P, NCOL])
        bgu_sb = sb("bgu_sb", [P, EXPERTS, 2 * KT])
        wide = KT * (PAD + T)
        plain = KT * T
        s0, s2, s3, s4, s7, s8, s9 = (sb(f"s{i}", [P, plain]) for i in (0, 2, 3, 4, 7, 8, 9))
        s1, s5, s6 = (sb(f"s{i}", [P, wide]) for i in (1, 5, 6))
        ps = ctx.enter_context(nc.psum_tensor("ps", [P, 8, BANK], F32))

        feat = lambda s: s[:, 0:plain].rearrange("p (k t) -> p k t", t=T)
        rows = lambda s: s[:, 0:plain].rearrange("p (t d) -> p t d", d=D)
        padded = lambda s: s[:, 0:wide].rearrange("p (k t) -> p k t", t=PAD + T)
        c_ = lambda name: cst[:, CONST[name][0]:CONST[name][1]]
        p_ = lambda name, k: col[:, COL[name] + k:COL[name] + k + 1]
        ident, fold, iota = c_("ident"), c_("fold"), c_("iota")

        mem_rows, mem_f, k_f, v_rows = rows(s0), feat(s1), feat(s2), rows(s3)
        xs_rows, h_f = rows(s7), feat(s4)
        u_lru, xr_f = padded(s1), feat(s0)
        u_pool, win_a, win_b, pool_f = padded(s5), padded(s1), padded(s6), feat(s7)
        r_f, i_f, a_f, b_f = feat(s8), feat(s6), feat(s1), feat(s5)
        hs_f, gelu_f, gtmp_f = feat(s8), feat(s9), feat(s0)
        siga_f, sigb_f, m_f = feat(s6), feat(s1), feat(s5)
        xn_rows, xn_f, q_f, o_f = rows(s0), feat(s4), feat(s6), feat(s8)
        prob = s1[:, 0:plain].rearrange("p (h q m) -> p h q m", h=HEADS, q=TT)
        probT = s5[:, 0:plain].rearrange("p (h m q) -> p h m q", h=HEADS, m=TT)
        half = [s[:, :].bitcast(BF16) for s in (s2, s3)]
        n16 = TT * D
        xpart = [v.rearrange("p (t d) -> p t d", d=D)
                 for v in (half[0][:, 0:n16], half[0][:, n16:2 * n16], half[1][:, 0:n16])]
        onehot = half[1][:, n16:n16 + TT * SLOTS].rearrange("p (t c) -> p t c", c=SLOTS)
        rest_rows = rows(s8)
        gated = s5[:, 0:2 * D]
        x32, h32 = (s6[:, i * D:(i + 1) * D].rearrange("p (k c) -> p k c", c=2 * SLOTS) for i in range(2))
        gate, up, sig, lin = (s8[:, BANK * i:BANK * (i + 1)].rearrange("p (k c) -> p k c", c=SLOTS) for i in range(4))
        dlow, drow = s7[0:SLOTS, 0:D], s7[0:SLOTS, D:2 * D]
        router_w = s9[:, 0:KT * EXPERTS].rearrange("p (k e) -> p k e", e=EXPERTS)
        router_b = s9[:, KT * EXPERTS:(KT + 1) * EXPERTS]
        bdown_sb = s9[0:EXPERTS, BANK:BANK + D]
        fin_g = s4[:, 0:D]
        gather = [s[:, D * i:D * (i + 1)] for s in (s0, s1, s5, s8) for i in range(2)]

        router = sb("router", [P, 1000])
        at = [0]

        def carve(n):
            at[0] += n
            assert at[0] <= 1000
            return router[:, at[0] - n:at[0]]

        ssum, root, rstd = carve(10), carve(10), carve(10)
        smax, snegm, ssm, srec = carve(8), carve(8), carve(8), carve(8)
        lam_mag, lam_y, lam_s, lam_z, lam_p, lam_c = (carve(KT) for _ in range(6))
        logit, pick, rankp, gmat, rowid, roundid, tmp = (carve(TT * EXPERTS).rearrange("p (t e) -> p t e", e=EXPERTS)
                                                for _ in range(7))
        rank_or_no = carve(TT * BLOCKS).rearrange("p (t e) -> p t e", e=BLOCKS)
        top8, idxf = carve(8 * TT), carve(8 * TT)
        gates, gsum, grec, negtop = carve(TOPK * TT), carve(TT), carve(TT), carve(TT)
        slotf, chosen_round, weight = carve(TOPK * TT), carve(TOPK * TT), carve(TOPK * TT)
        cntmax, nround = carve(1), carve(1)
        idx8 = sb("idx8", [P, 8 * TT], U32)
        sloti = sb("sloti", [P, TOPK * TT], I32)
        pick16 = sb("pick16", [P, TT, EXPERTS], BF16)
        mat16 = sb("mat16", [P, 2, P], BF16)
        nround_i = sb("nround_i", [P, 1], I32)
        gT = sb("gT", [EXPERTS, T])

        loaded = [sem(f"loaded{i}") for i in range(RAW)]
        names = """in_x in_mem in_cst in_router in_fin
            chunk_used unit_done freed_dve freed_act squared rooted normed dve_seq act_seq
            lam_abs lam_exp pads_zero xr_done pool_done decay_done inner_done mult_done scan_done
            gelu_arg gelu_sig yb_done m_done rowmax prob_done part_hi part_rest
            gate_in gate_exp picked gmat_done logits_read route_done
            onehot_ready sel_done x_ready xhi_ready xlo_ready whi_ready wlo_ready gated_out turned
            gate_biased up_biased gate_ready up_ready lin_ready sig_ready h_ready hhi_ready hlo_ready
            dlow_out drow_ready stored drow_free weighed summed fin_sum fin_sq fin_root fin_rec result written""".split()
        S = {n: sem(n) for n in names}
        gathered = [sem(f"gathered{i}") for i in range(TT * TOPK)]
        freed = {"dve": S["freed_dve"], "act": S["freed_act"]}

        block = ctx.enter_context(nc.Block())

        PER_ROUND = PER_EXPERT * EXPERTS

        def number(r, e, i):
            return r * PER_ROUND + e * PER_EXPERT + (CHUNKS_0 - DN_CHUNKS + i)

        def place(i):
            return NDENSE - DN_CHUNKS + i

        def fills(r, e, i):
            return r * (PER_ROUND // RAW) + e * (PER_EXPERT // RAW) + (place(i) // RAW + 1)

        def needed_rounds(eng):
            eng.wait_ge(S["route_done"], 1)
            return eng.value_load(nround_i[0:1, 0:1], min_val=1, max_val=ROUNDS)

        @block.sync
        def _(sp):
            sp.dma_start(mem_rows, mem.rearrange("(t p) d -> p t d", p=P)).then_inc(S["in_mem"], 16)
            sp.dma_start(res[:], x.rearrange("(t p) d -> p t d", p=P)).then_inc(S["in_x"], 16)
            used = dense_used()
            for n in range(NDENSE):
                if n >= RAW:
                    name, count = used[n - RAW]
                    sp.wait_ge(S[name], count)
                sp.dma_start(raw[:, n % RAW, :], dense[n]).then_inc(loaded[n % RAW], 16)

            def gate_up_chunk(r, e, i, k):
                sp.wait_ge(S["chunk_used"], number(r, e, i) - (RAW - 1))
                sp.dma_start(raw[:, place(i) % RAW, :], w_gate_up[bass.ds(e * D + k * P, P), :])\
                    .then_inc(loaded[place(i) % RAW], 16)

            def down_chunk(r, e, i, k):
                sp.wait_ge(S["chunk_used"], number(r, e, i) - (RAW - 1))
                rows2 = w_down[bass.ds((e - 1) * D + k * 2 * P, 2 * P), :]
                sp.dma_start(raw[:, place(i) % RAW, :].rearrange("p (f d) -> p f d", d=D),
                             rows2.rearrange("(f p) d -> p f d", p=P)).then_inc(loaded[place(i) % RAW], 16)

            for k in range(RAW):
                name, count = used[NDENSE - RAW + k]
                sp.wait_ge(S[name], count)
                sp.dma_start(raw[:, (NDENSE + k) % RAW, :], w_gate_up[k * P:(k + 1) * P, :])\
                    .then_inc(loaded[(NDENSE + k) % RAW], 16)
            n = needed_rounds(sp)
            with sp.Fori(0, n) as r:
                for k in range(RAW, GU_CHUNKS):
                    gate_up_chunk(r, 0, DN_CHUNKS + k, k)
                with sp.Fori(1, EXPERTS) as e:
                    for k in range(GU_CHUNKS):
                        gate_up_chunk(r, e, k, k)
                    for k in range(DN_CHUNKS):
                        down_chunk(r, e, GU_CHUNKS + k, k)
                for k in range(DN_CHUNKS):
                    down_chunk(r, EXPERTS, k, k)
                with sp.If(r + 1 < n):
                    for k in range(RAW):
                        gate_up_chunk(r + 1, 0, DN_CHUNKS + k, k)
            for t in range(TT):
                sp.wait_ge(S["result"], t + 1)
                sp.dma_start(out[t * P:(t + 1) * P, :], res[:, t, :]).then_inc(S["written"], 16)
            sp.wait_ge(S["written"], 16 * TT)

        @block.gpsimd
        def _(pool):
            pool.wait_ge(S["yb_done"], 1)
            pool.dma_start(router_w, w_router.rearrange("(k p) e -> p k e", p=P)).then_inc(S["in_router"], 16)
            pool.dma_start(router_b, b_router).then_inc(S["in_router"], 16)
            pool.dma_start(bdown_sb, b_down).then_inc(S["in_router"], 16)
            pool.wait_ge(S["logits_read"], 1)
            pool.dma_start(fin_g, norm_final).then_inc(S["in_fin"], 16)
            pool.sem_inc(S["drow_free"], 1)
            n = needed_rounds(pool)
            with pool.Fori(0, n) as r:
                with pool.Fori(0, BLOCKS) as k:
                    done = r * BLOCKS + k + 1
                    pool.wait_ge(S["drow_ready"], done + 1)
                    pool.dma_start(scratch[bass.ds(k * SLOTS, SLOTS), :], drow)\
                        .then_inc(S["stored"], 16)
                    pool.wait_ge(S["stored"], done * 16)
                    pool.sem_inc(S["drow_free"], 1)
                for j in range(TT * TOPK):
                    pool.indirect_dma_start(gather[j], None, scratch,
                                            bass.IndirectOffsetOnAxis(ap=sloti[:, j:j + 1], axis=0))\
                        .then_inc(gathered[j], 16)
                for j in range(TT * TOPK):
                    pool.wait_ge(gathered[j], (r + 1) * 16)

        @block.scalar
        def _(act):
            act.dma_start(cst[:], consts).then_inc(S["in_cst"], 16)
            act.dma_start(col[:], cols).then_inc(S["in_cst"], 16)
            act.dma_start(bgu_sb[:], bgu).then_inc(S["in_cst"], 16)
            act.wait_ge(S["in_cst"], 48)

            def squares(n, src, junk):
                for t in range(TT):
                    nc.scalar.activation(junk[:, t, :], src[:, t, :], ACT.Square,
                                         accum_out=ssum[:, 2 * n + t:2 * n + t + 1]).then_inc(S["squared"], 1)
                act.wait_ge(S["squared"], 2 * n + 2)
                nc.scalar.activation(root[:, 2 * n:2 * n + 2], ssum[:, 2 * n:2 * n + 2], ACT.Sqrt,
                                     scale=1.0 / D, bias=EPS).then_inc(S["rooted"], 1)

            def units(name, n, fn):
                for j in range(n):
                    u = UNIT[name] + j
                    act.wait_ge(S["unit_done"], u + 1)
                    fn(j, ps[:, u % 8, :])

            two = lambda b: b.rearrange("p (k t) -> p k t", t=T)

            act.wait_ge(S["in_mem"], 16)
            squares(0, mem_rows, rows(s4))
            act.wait_ge(S["in_x"], 16)
            squares(1, res, xs_rows)
            act.wait_ge(S["lam_abs"], 1)
            nc.scalar.activation(lam_y, lam_mag, ACT.Exp, scale=-1.0).then_inc(S["lam_exp"], 1)

            units("v", 4, lambda j, b: nc.scalar.activation(
                v_rows[:, j // 2, (j % 2) * BANK:(j % 2 + 1) * BANK], b, ACT.Copy).then_inc(S["freed_act"], 1))
            act.wait_ge(S["pads_zero"], 1)
            units("pool", 4, lambda j, b: nc.scalar.activation(
                u_pool[:, 2 * j:2 * j + 2, PAD:], two(b), ACT.Copy).then_inc(S["freed_act"], 1))

            def logistic_gate(dst, bias):
                def fn(j, b):
                    for k in (2 * j, 2 * j + 1):
                        ins = nc.scalar.activation(dst[:, k, :], b[:, (k % 2) * T:(k % 2 + 1) * T], ACT.Sigmoid,
                                                   bias=p_(bias, k))
                        ins.then_inc(S["freed_act"] if k % 2 else S["act_seq"], 1)
                return fn
            units("ra", 4, logistic_gate(r_f, "lru_b_a"))
            act.wait_ge(S["pool_done"], 1)
            units("rx", 4, logistic_gate(i_f, "lru_b_x"))
            act.wait_ge(S["freed_act"], evacuated(UNIT["ra"] + 3)[1])
            act.wait_ge(S["act_seq"], 8)
            for k in range(KT):
                nc.scalar.activation(a_f[:, k, :], r_f[:, k, :], ACT.Exp, scale=lam_c[:, k:k + 1])\
                    .then_inc(S["decay_done"], 1)
                nc.scalar.activation(b_f[:, k, :], r_f[:, k, :], ACT.Tanh, scale=lam_c[:, k:k + 1])\
                    .then_inc(S["decay_done"], 1)
            units("gelu", 4, lambda j, b: nc.scalar.activation(
                gelu_f[:, 2 * j:2 * j + 2, :], two(b), ACT.Copy).then_inc(S["freed_act"], 1))
            act.wait_ge(S["inner_done"], 1)
            nc.scalar.activation(b_f, b_f, ACT.Sqrt, scale=-1.0).then_inc(S["mult_done"], 1)
            act.wait_ge(S["scan_done"], KT)
            units("ga", 4, lambda j, b: nc.scalar.activation(
                siga_f[:, 2 * j:2 * j + 2, :], two(b), ACT.Sigmoid).then_inc(S["freed_act"], 1))
            act.wait_ge(S["gelu_arg"], 1)
            nc.scalar.activation(gtmp_f, gtmp_f, ACT.Sigmoid, scale=2.0 * 0.7978845608028654)\
                .then_inc(S["gelu_sig"], 1)
            units("gb", 4, lambda j, b: nc.scalar.activation(
                sigb_f[:, 2 * j:2 * j + 2, :], two(b), ACT.Sigmoid).then_inc(S["freed_act"], 1))
            act.wait_ge(S["freed_dve"], evacuated(UNIT["mix"] + 3)[1])
            squares(2, res, xn_rows)

            def exps(j, b):
                act.wait_ge(S["rowmax"], j + 1)
                for q in range(TT):
                    ins = nc.scalar.activation(prob[:, j, q, :], b[:, q * T:(q + 1) * T], ACT.Exp, scale=HD ** -0.5,
                                               bias=snegm[:, 2 * j + q:2 * j + q + 1],
                                               accum_out=ssm[:, 2 * j + q:2 * j + q + 1])
                    ins.then_inc(S["freed_act"] if q else S["act_seq"], 1)
            units("score", 4, exps)
            units("pT", 4, lambda j, b: nc.scalar.activation(
                probT[:, j, :, :], b.rearrange("p (m q) -> p m q", q=T), ACT.Copy).then_inc(S["freed_act"], 1))
            act.wait_ge(S["freed_dve"], evacuated(UNIT["o"] + 3)[1])
            squares(3, res, xn_rows)
            act.wait_ge(S["normed"], 8)
            nc.scalar.activation(xpart[0], xn_rows, ACT.Copy).then_inc(S["part_hi"], 1)
            for n in (1, 2):
                act.wait_ge(S["part_rest"], n)
                nc.scalar.activation(xpart[n], rest_rows, ACT.Copy).then_inc(S["part_hi"], 1)
            act.wait_ge(S["gate_in"], 1)
            for t in range(TT):
                nc.scalar.activation(gates[:, TOPK * t:TOPK * (t + 1)], top8[:, 8 * t:8 * t + TOPK], ACT.Exp,
                                     bias=negtop[:, t:t + 1], accum_out=gsum[:, t:t + 1]).then_inc(S["gate_exp"], 1)
            act.preload_act_table(ACT.Sigmoid)

            def split(r, e, i):
                act.wait_ge(loaded[place(i) % RAW], fills(r, e, i) * 16)
                act.wait_ge(S["chunk_used"], number(r, e, i) - (SPL - 1))
                nc.scalar.activation(whi[:, place(i) % SPL, :], raw[:, place(i) % RAW, 0:SPLIT], ACT.Copy)\
                    .then_inc(S["whi_ready"], 1)

            def x_high(r, e):
                act.wait_ge(S["x_ready"], r * BLOCKS + e + 1)
                nc.scalar.activation(xpair[:, :, 0:SLOTS], x32[:, :, 0:SLOTS], ACT.Copy).then_inc(S["xhi_ready"], 1)

            def rows_out(r, e, i):
                act.wait_ge(S["chunk_used"], number(r, e, i))
                for b in range(4):
                    nc.scalar.activation(gated[:, b * BANK:(b + 1) * BANK], ps[:, b, :], ACT.Copy)\
                        .then_inc(S["gated_out"], 1)

            def low_rows(r, e, k):
                act.wait_ge(S["chunk_used"], number(r, e, 0))
                act.wait_ge(S["drow_ready"], r * BLOCKS + k + 1)
                nc.scalar.activation(dlow, ps[SLOTS:2 * SLOTS, 4:6, :].rearrange("p b n -> p (b n)"), ACT.Copy)\
                    .then_inc(S["dlow_out"], 1)

            def gate_sigmoid(count):
                act.wait_ge(S["gate_ready"], count)
                nc.scalar.activation(sig, gate, ACT.Sigmoid, scale=ALPHA).then_inc(S["sig_ready"], 1)

            def h_high(count):
                act.wait_ge(S["h_ready"], count)
                nc.scalar.activation(hpair[:, :, 0:SLOTS], h32[:, :, 0:SLOTS], ACT.Copy).then_inc(S["hhi_ready"], 1)

            act.sem_inc(S["gated_out"], 4)
            n = needed_rounds(act)
            with act.Fori(0, n) as r:
                x_high(r, 0)
                for i in range(DN_CHUNKS, PER_EXPERT - 1):
                    split(r, 0, i)
                split(r, 0, PER_EXPERT - 1)
                rows_out(r, 0, PER_EXPERT)
                x_high(r, 1)
                with act.Fori(1, EXPERTS) as e:
                    done = r * EXPERTS + e
                    for i in range(PER_EXPERT):
                        if i == 4:
                            low_rows(r, e, e - 1)
                        if i == 5:
                            gate_sigmoid(done)
                        if i == 6:
                            h_high(done)
                        if i == 11:
                            rows_out(r, e, GU_CHUNKS)
                            x_high(r, e + 1)
                        split(r, e, i)
                low_rows(r, EXPERTS, EXPERTS - 1)
                gate_sigmoid((r + 1) * EXPERTS)
                for i in range(DN_CHUNKS):
                    split(r, EXPERTS, i)
                    if i == 0:
                        h_high((r + 1) * EXPERTS)
                act.wait_ge(S["chunk_used"], number(r, EXPERTS, DN_CHUNKS))
                low_rows(r, EXPERTS, EXPERTS)
            for t in range(TT):
                act.wait_ge(S["fin_sum"], 1)
                nc.scalar.activation(xs_rows[:, t, :], res[:, t, :], ACT.Square,
                                     accum_out=ssum[:, 8 + t:9 + t]).then_inc(S["fin_sq"], 1)
                act.wait_ge(S["fin_sq"], t + 1)
                nc.scalar.activation(root[:, 8 + t:9 + t], ssum[:, 8 + t:9 + t], ACT.Sqrt, scale=1.0 / D,
                                     bias=EPS).then_inc(S["fin_root"], 1)

        @block.vector
        def _(dve):
            V = nc.vector
            seq = [0]

            def link(ins):
                seq[0] += 1
                ins.then_inc(S["dve_seq"], 1)
                dve.wait_ge(S["dve_seq"], seq[0])

            def units(name, n, fn):
                for j in range(n):
                    u = UNIT[name] + j
                    dve.wait_ge(S["unit_done"], u + 1)
                    fn(j, ps[:, u % 8, :])

            two = lambda b: b.rearrange("p (k t) -> p k t", t=T)

            def normalise(n, src, dst):
                dve.wait_ge(S["rooted"], n + 1)
                link(V.reciprocal(rstd[:, 2 * n:2 * n + 2], root[:, 2 * n:2 * n + 2]))
                for t in range(TT):
                    V.tensor_scalar(dst[:, t, :], src[:, t, :], rstd[:, 2 * n + t:2 * n + t + 1], None, ALU.mult)\
                        .then_inc(S["normed"], 1)

            def gained(dst, gain):
                def fn(j, b):
                    V.tensor_scalar(dst[:, 2 * j, :], b[:, 0:T], p_(gain, 2 * j), None, ALU.mult)\
                        .then_inc(S["dve_seq"], 1)
                    seq[0] += 1
                    V.tensor_scalar(dst[:, 2 * j + 1, :], b[:, T:2 * T], p_(gain, 2 * j + 1), None, ALU.mult)\
                        .then_inc(S["freed_dve"], 1)
                return fn

            def copied(dst):
                return lambda j, b: V.tensor_copy(dst[:, 2 * j:2 * j + 2, :], two(b)).then_inc(S["freed_dve"], 1)

            dve.wait_ge(S["in_cst"], 48)
            lam0 = col[:, COL["lru_lambda"]:COL["lru_lambda"] + KT]
            link(V.scalar_tensor_tensor(lam_mag, lam0, -1.0, lam0, ALU.mult, ALU.max))
            dve.sem_inc(S["lam_abs"], 1)
            V.memset(u_pool[:, :, 0:PAD], 0.0).then_inc(S["pads_zero"], 1)
            V.tensor_copy(mat16[:, :, :], cst[:, CONST["before"][0]:CONST["ones"][1]].rearrange(
                "p (a b) -> p a b", a=2)).then_inc(S["dve_seq"], 1)
            seq[0] += 1
            normalise(0, mem_rows, mem_rows)
            normalise(1, res, xs_rows)
            dve.wait_ge(S["lam_exp"], 1)
            link(V.tensor_scalar(lam_s, lam_y, 2.0, None, ALU.add))
            link(V.reciprocal(lam_s, lam_s))
            link(V.tensor_tensor(lam_s, lam_s, lam_y, ALU.mult))
            link(V.tensor_tensor(lam_z, lam_s, lam_s, ALU.mult))
            link(V.tensor_scalar(lam_p, lam_z, 1.0 / 19, None, ALU.mult))
            for odd in range(17, 1, -2):
                link(V.scalar_tensor_tensor(lam_p, lam_p, 1.0 / odd, lam_z, ALU.add, ALU.mult))
            link(V.scalar_tensor_tensor(lam_p, lam_p, 1.0, lam_s, ALU.add, ALU.mult))
            link(V.tensor_scalar(lam_z, lam0, 0.0, 8.0, ALU.min, ALU.mult))
            link(V.scalar_tensor_tensor(lam_c, lam_p, -16.0, lam_z, ALU.mult, ALU.add))

            units("memT", 4, gained(mem_f, "norm_mem"))
            units("k", 4, copied(k_f))
            units("xT", 4, gained(h_f, "norm_mix"))
            link(V.memset(u_lru[:, :, 0:PAD], 0.0))
            units("lrux", 4, lambda j, b: V.tensor_copy(
                u_lru[:, 2 * j:2 * j + 2, PAD:], two(b)).then_inc(S["freed_dve"], 1))
            dve.wait_ge(S["freed_dve"], evacuated(UNIT["lrux"] + 3)[1])
            for tap in range(CONV):
                shift = PAD - (CONV - 1) + tap
                for k in range(KT):
                    w = col[:, COL["conv_w"] + KT * tap + k:COL["conv_w"] + KT * tap + k + 1]
                    if tap == 0:
                        ins = V.tensor_scalar(xr_f[:, k, :], u_lru[:, k, shift:shift + T], w, p_("conv_b", k),
                                              ALU.mult, ALU.add)
                    else:
                        ins = V.scalar_tensor_tensor(xr_f[:, k, :], u_lru[:, k, shift:shift + T], w, xr_f[:, k, :],
                                                     ALU.mult, ALU.add)
                    if tap == CONV - 1:
                        ins.then_inc(S["xr_done"], 1)
                    else:
                        ins.then_inc(S["dve_seq"], 1)
                        seq[0] += 1
                if tap < CONV - 1:
                    dve.wait_ge(S["dve_seq"], seq[0])
            dve.wait_ge(S["xr_done"], KT)
            dve.wait_ge(S["freed_act"], evacuated(UNIT["pool"] + 3)[1])
            end = PAD + T
            link(V.tensor_tensor(win_a[:, 0:8, 2:end], u_pool[:, 0:8, 2:end], u_pool[:, 0:8, 1:end - 1], ALU.add))
            link(V.tensor_tensor(win_b[:, 2:8, 4:end], win_a[:, 2:8, 4:end], win_a[:, 2:8, 2:end - 2], ALU.add))
            link(V.tensor_tensor(win_a[:, 4:8, 8:end], win_b[:, 4:8, 8:end], win_b[:, 4:8, 4:end - 4], ALU.add))
            link(V.tensor_tensor(win_b[:, 6:8, 16:end], win_a[:, 6:8, 16:end], win_a[:, 6:8, 8:end - 8], ALU.add))
            for g, w in enumerate(WINDOWS):
                src = (win_a, win_b)[g % 2]
                early = src[:, 2 * g:2 * g + 2, PAD:2 * PAD]
                inv = c_("inv")[:, PAD * g:PAD * (g + 1)].unsqueeze(1).broadcast_to([P, 2, PAD])
                link(V.tensor_tensor(early, early, inv, ALU.mult))
                link(V.scalar_tensor_tensor(pool_f[:, 2 * g:2 * g + 2, :], src[:, 2 * g:2 * g + 2, PAD:], 1.0 / w,
                                            u_pool[:, 2 * g:2 * g + 2, PAD:], ALU.mult, ALU.subtract))
            dve.sem_inc(S["pool_done"], 1)

            def scaled(j, b):
                for k in (2 * j, 2 * j + 1):
                    V.tensor_scalar(pool_f[:, k, :], b[:, (k % 2) * T:(k % 2 + 1) * T], p_("pool_scale", k), None,
                                    ALU.mult).then_inc(S["freed_dve"] if k % 2 else S["dve_seq"], 1)
                seq[0] += 1
            units("grp", 4, scaled)

            dve.wait_ge(S["decay_done"], 2 * KT)
            link(V.tensor_tensor(r_f, a_f, a_f, ALU.mult))
            link(V.scalar_tensor_tensor(b_f, r_f, 1.0, b_f, ALU.add, ALU.mult))
            V.tensor_scalar(b_f, b_f, 0.0, None, ALU.min).then_inc(S["inner_done"], 1)
            dve.wait_ge(S["freed_act"], evacuated(UNIT["rx"] + 3)[1])
            dve.wait_ge(S["mult_done"], 1)
            link(V.memset(b_f[:, :, 0:1], 1.0))
            link(V.tensor_tensor(b_f, b_f, i_f, ALU.mult))
            link(V.tensor_tensor(b_f, b_f, xr_f, ALU.mult))
            for k in range(KT):
                V.tensor_tensor_scan(hs_f[:, k, :], a_f[:, k, :], b_f[:, k, :], 0.0, ALU.mult, ALU.add)\
                    .then_inc(S["scan_done"], 1)
            dve.wait_ge(S["freed_act"], evacuated(UNIT["gelu"] + 3)[1])
            link(V.tensor_tensor(gtmp_f, gelu_f, gelu_f, ALU.mult))
            link(V.tensor_scalar(gtmp_f, gtmp_f, 0.044715, 1.0, ALU.mult, ALU.add))
            V.tensor_tensor(gtmp_f, gtmp_f, gelu_f, ALU.mult).then_inc(S["gelu_arg"], 1)
            dve.wait_ge(S["scan_done"], KT)
            link(V.tensor_tensor(hs_f, hs_f, gelu_f, ALU.mult))
            dve.wait_ge(S["gelu_sig"], 1)
            V.tensor_tensor(hs_f, hs_f, gtmp_f, ALU.mult).then_inc(S["yb_done"], 1)
            dve.wait_ge(S["freed_act"], evacuated(UNIT["gb"] + 3)[1])
            units("pp", 4, lambda j, b: V.tensor_tensor(
                m_f[:, 2 * j:2 * j + 2, :], siga_f[:, 2 * j:2 * j + 2, :], two(b), ALU.mult)
                .then_inc(S["freed_dve"], 1))

            def merge(j, b):
                t2 = sigb_f[:, 2 * j:2 * j + 2, :]
                V.tensor_tensor(t2, t2, two(b), ALU.mult).then_inc(S["freed_dve"], 1)
                dve.wait_ge(S["freed_dve"], evacuated(UNIT["lp"] + j)[1])
                V.tensor_tensor(m_f[:, 2 * j:2 * j + 2, :], m_f[:, 2 * j:2 * j + 2, :], t2, ALU.add)\
                    .then_inc(S["m_done"], 1)
            units("lp", 4, merge)

            def onto_residual(j, b):
                part = res[:, j // 2, (j % 2) * BANK:(j % 2 + 1) * BANK]
                V.tensor_tensor(part, part, b, ALU.add).then_inc(S["freed_dve"], 1)
            units("mix", 4, onto_residual)
            normalise(2, res, xn_rows)
            units("x1T", 4, gained(xn_f, "norm_xattn"))
            units("q", 4, copied(q_f))

            def maxima(j, b):
                link(V.tensor_reduce(smax[:, 2 * j:2 * j + 2], two(b), AX.X, ALU.max))
                V.tensor_scalar(snegm[:, 2 * j:2 * j + 2], smax[:, 2 * j:2 * j + 2], -(HD ** -0.5), None, ALU.mult)\
                    .then_inc(S["rowmax"], 1)
            units("score", 4, maxima)
            for j in range(HEADS):
                dve.wait_ge(S["freed_act"], evacuated(UNIT["score"] + j)[1])
                dve.wait_ge(S["act_seq"], 8 + j + 1)
                link(V.reciprocal(srec[:, 2 * j:2 * j + 2], ssm[:, 2 * j:2 * j + 2]))
                for q in range(TT):
                    V.tensor_scalar(prob[:, j, q, :], prob[:, j, q, :], srec[:, 2 * j + q:2 * j + q + 1], None,
                                    ALU.mult).then_inc(S["prob_done"], 1)
            units("oT", 4, copied(o_f))
            units("o", 4, onto_residual)
            normalise(3, res, xn_rows)
            units("xnT", 4, gained(xn_f, "norm_moe"))
            for n in range(2):
                dve.wait_ge(S["part_hi"], n + 1)
                V.tensor_tensor(rest_rows, (xn_rows, rest_rows)[n], xpart[n], ALU.subtract)\
                    .then_inc(S["part_rest"], 1)

            dve.wait_ge(S["in_router"], 48)
            u = UNIT["logit"]
            dve.wait_ge(S["unit_done"], u + 1)
            bias = router_b.unsqueeze(1).broadcast_to([P, TT, EXPERTS])
            V.tensor_tensor(logit, ps[:, u % 8, 0:TT * EXPERTS].rearrange("p (t e) -> p t e", e=EXPERTS), bias, ALU.add)\
                .then_inc(S["freed_dve"], 1)
            dve.wait_ge(S["freed_dve"], evacuated(u)[1])
            dve.sem_inc(S["logits_read"], 1)
            tops = lambda v, t, j: v[:, 8 * t + j:8 * t + j + 1]
            for t in range(TT):
                link(V.max(top8[:, 8 * t:8 * t + 8], logit[:, t, :]))
                link(V.max_index(idx8[:, 8 * t:8 * t + 8], top8[:, 8 * t:8 * t + 8], logit[:, t, :]))
                link(V.tensor_scalar(negtop[:, t:t + 1], tops(top8, t, 0), -1.0, None, ALU.mult))
            dve.sem_inc(S["gate_in"], 1)
            link(V.tensor_copy(idxf, idx8[:]))
            places = iota[:, 0:EXPERTS]
            for t in range(TT):
                link(V.tensor_scalar(pick[:, t, :], places, tops(idxf, t, 0), None, ALU.is_equal))
                for j in range(1, TOPK):
                    link(V.scalar_tensor_tensor(pick[:, t, :], places, tops(idxf, t, j), pick[:, t, :], ALU.is_equal,
                                                ALU.add))
            V.tensor_copy(pick16[:], pick).then_inc(S["picked"], 1)
            dve.wait_ge(S["gate_exp"], TT)
            link(V.reciprocal(grec, gsum))
            for t in range(TT):
                mine = gates[:, TOPK * t:TOPK * (t + 1)]
                link(V.tensor_scalar(mine, mine, grec[:, t:t + 1], None, ALU.mult))
                for j in range(TOPK):
                    g = gates[:, TOPK * t + j:TOPK * t + j + 1]
                    dst = gmat[:, t, :] if j == 0 else tmp[:, t, :]
                    link(V.tensor_scalar(dst, places, tops(idxf, t, j), g, ALU.is_equal, ALU.mult))
                    if j:
                        link(V.tensor_tensor(gmat[:, t, :], gmat[:, t, :], tmp[:, t, :], ALU.add))
            dve.sem_inc(S["gmat_done"], 1)
            u = UNIT["rank"]
            dve.wait_ge(S["unit_done"], u + 1)
            got = ps[:, u % 8, 0:3 * EXPERTS].rearrange("p (t e) -> p t e", e=EXPERTS)
            link(V.tensor_copy(rankp, got[:, 0:TT, :]))
            V.tensor_reduce(cntmax, got[:, TT, :], AX.X, ALU.max).then_inc(S["freed_dve"], 1)
            dve.wait_ge(S["freed_dve"], evacuated(u)[1])
            link(V.tensor_scalar(nround, cntmax, float(SLOTS), 1.0, ALU.is_gt, ALU.add))
            for n in range(2, ROUNDS):
                link(V.scalar_tensor_tensor(nround, cntmax, float(SLOTS * n), nround, ALU.is_gt, ALU.add))
            link(V.tensor_copy(nround_i[:], nround))
            link(V.memset(rank_or_no, 0.0))
            link(V.scalar_tensor_tensor(rank_or_no[:, :, 0:EXPERTS], rankp, 1.0, pick, ALU.add, ALU.mult))
            link(V.tensor_scalar(rank_or_no, rank_or_no, -1.0, None, ALU.add))
            dve.sem_inc(S["route_done"], 1)
            link(V.tensor_scalar(rowid, places.unsqueeze(1).broadcast_to([P, TT, EXPERTS]), float(SLOTS), float(SLOTS),
                                 ALU.mult, ALU.add))
            link(V.tensor_tensor(rowid, rowid, rankp, ALU.add))
            link(V.tensor_scalar(roundid, rankp, float(SLOTS), None, ALU.is_ge))
            for n in range(2, ROUNDS):
                link(V.scalar_tensor_tensor(roundid, rankp, float(SLOTS * n), roundid, ALU.is_ge, ALU.add))
            link(V.scalar_tensor_tensor(rowid, roundid, -float(SLOTS), rowid, ALU.mult, ALU.add))
            for dst, table in ((slotf, rowid), (chosen_round, roundid)):
                for t in range(TT):
                    for j in range(TOPK):
                        link(V.scalar_tensor_tensor(tmp[:, t, :], places, tops(idxf, t, j), table[:, t, :],
                                                    ALU.is_equal, ALU.mult,
                                                    accum_out=dst[:, TOPK * t + j:TOPK * t + j + 1]))
            link(V.tensor_copy(sloti[:], slotf))
            u = UNIT["gT"]
            dve.wait_ge(S["unit_done"], u + 1)
            V.tensor_copy(gT[:], ps[0:EXPERTS, u % 8, 0:T]).then_inc(S["freed_dve"], 1)
            units("bd", 4, onto_residual)

            def split(r, e, i):
                dve.wait_ge(S["whi_ready"], number(r, e, i) - (CHUNKS_0 - 1))
                V.tensor_tensor(wlo[:, place(i) % SPL, :], raw[:, place(i) % RAW, 0:SPLIT],
                                whi[:, place(i) % SPL, :].bitcast(F32), ALU.subtract).then_inc(S["wlo_ready"], 1)

            def select(r, e):
                for t in range(TT):
                    V.tensor_scalar(onehot[:, t, :], iota[:, bass.ds(r * SLOTS, SLOTS)],
                                    rank_or_no[:, t, bass.ds(e, 1)], None, ALU.is_equal)\
                        .then_inc(S["onehot_ready"], 1)

            gain = col[:, COL["norm_moe"]:COL["norm_moe"] + KT].unsqueeze(2).broadcast_to([P, KT, SLOTS])

            def x_whole(r, e):
                dve.wait_ge(S["sel_done"], r * BLOCKS + e + 1)
                V.tensor_tensor(x32[:, :, 0:SLOTS], ps[:, 6, :].rearrange("p (k c) -> p k c", c=SLOTS), gain,
                                ALU.mult).then_inc(S["x_ready"], 1)

            def x_low(r, e):
                dve.wait_ge(S["xhi_ready"], r * BLOCKS + e + 1)
                V.tensor_tensor(xpair[:, :, SLOTS:], x32[:, :, 0:SLOTS], xpair[:, :, 0:SLOTS].bitcast(F32),
                                ALU.subtract).then_inc(S["xlo_ready"], 1)

            def add_bias(r, e, count):
                dve.wait_ge(S["turned"], count)
                for n, (dst, name) in enumerate(((gate, "gate_biased"), (up, "up_biased"))):
                    b = bgu_sb[:, bass.ds(e, 1), KT * n:KT * (n + 1)].rearrange("p o k -> p (o k)").unsqueeze(2)
                    V.tensor_tensor(dst, ps[:, 6 + n, :].rearrange("p (k c) -> p k c", c=SLOTS),
                                    b.broadcast_to([P, KT, SLOTS]), ALU.add).then_inc(S[name], 1)
                dve.wait_ge(S["gate_biased"], count)
                V.tensor_scalar(gate, gate, LIMIT, None, ALU.min).then_inc(S["gate_ready"], 1)

            def swiglu(count):
                dve.wait_ge(S["up_biased"], count)
                V.tensor_scalar(up, up, LIMIT, -LIMIT, ALU.min, ALU.max).then_inc(S["up_ready"], 1)
                dve.wait_ge(S["up_ready"], count)
                dve.wait_ge(S["gate_ready"], count)
                V.scalar_tensor_tensor(lin, up, 1.0, gate, ALU.add, ALU.mult).then_inc(S["lin_ready"], 1)
                dve.wait_ge(S["lin_ready"], count)
                dve.wait_ge(S["sig_ready"], count)
                V.tensor_tensor(h32[:, :, 0:SLOTS], sig, lin, ALU.mult).then_inc(S["h_ready"], 1)

            def h_low(count):
                dve.wait_ge(S["hhi_ready"], count)
                V.tensor_tensor(hpair[:, :, SLOTS:], h32[:, :, 0:SLOTS], hpair[:, :, 0:SLOTS].bitcast(F32),
                                ALU.subtract).then_inc(S["hlo_ready"], 1)

            def sum_rows(r, k):
                dve.wait_ge(S["dlow_out"], r * BLOCKS + k + 1)
                dve.wait_ge(S["drow_free"], r * BLOCKS + k + 1)
                V.tensor_tensor(drow, ps[0:SLOTS, 4:6, :].rearrange("p b n -> p (b n)"), dlow, ALU.add)\
                    .then_inc(S["drow_ready"], 1)

            link(V.memset(x32[:, :, SLOTS:], 0.0))
            link(V.memset(h32[:, :, SLOTS:], 0.0))
            dve.sem_inc(S["drow_ready"], 1)
            n = needed_rounds(dve)
            with dve.Fori(0, n) as r:
                select(r, 0)
                x_whole(r, 0)
                x_low(r, 0)
                for i in range(DN_CHUNKS, PER_EXPERT):
                    if i == DN_CHUNKS + 1:
                        dve.wait_ge(S["sel_done"], r * BLOCKS + 1)
                        select(r, 1)
                    split(r, 0, i)
                dve.wait_ge(S["chunk_used"], number(r, 0, PER_EXPERT))
                x_whole(r, 1)
                x_low(r, 1)
                with dve.Fori(1, EXPERTS) as e:
                    done = r * EXPERTS + e
                    for i in range(PER_EXPERT):
                        if i == 4:
                            add_bias(r, e - 1, done)
                        if i == 5:
                            swiglu(done)
                        if i == 6:
                            sum_rows(r, e - 1)
                        if i == 7:
                            h_low(done)
                            dve.wait_ge(S["sel_done"], r * BLOCKS + e + 1)
                            select(r, e + 1)
                        if i == 11:
                            dve.wait_ge(S["chunk_used"], number(r, e, GU_CHUNKS))
                            x_whole(r, e + 1)
                        split(r, e, i)
                    x_low(r, e + 1)
                add_bias(r, EXPERTS - 1, (r + 1) * EXPERTS)
                split(r, EXPERTS, 0)
                swiglu((r + 1) * EXPERTS)
                sum_rows(r, EXPERTS - 1)
                split(r, EXPERTS, 1)
                h_low((r + 1) * EXPERTS)
                split(r, EXPERTS, 2)
                split(r, EXPERTS, 3)
                sum_rows(r, EXPERTS)
                V.scalar_tensor_tensor(weight, chosen_round, iota[:, bass.ds(r, 1)], gates, ALU.is_equal, ALU.mult)\
                    .then_inc(S["weighed"], 1)
                dve.wait_ge(S["weighed"], r + 1)
                for j in range(TOPK):
                    for t in range(TT):
                        i = TOPK * t + j
                        dve.wait_ge(gathered[i], (r + 1) * 16)
                        if j:
                            dve.wait_ge(S["summed"], r * (TT * TOPK) + (TT * (j - 1) + t + 1))
                        V.scalar_tensor_tensor(res[:, t, :], gather[i], weight[:, i:i + 1], res[:, t, :], ALU.mult,
                                               ALU.add).then_inc(S["summed"], 1)
                dve.wait_ge(S["summed"], (r + 1) * (TT * TOPK))
            dve.sem_inc(S["fin_sum"], 1)
            dve.wait_ge(S["in_fin"], 16)
            for t in range(TT):
                dve.wait_ge(S["fin_root"], t + 1)
                link(V.reciprocal(rstd[:, 8 + t:9 + t], root[:, 8 + t:9 + t]))
                V.scalar_tensor_tensor(res[:, t, :], res[:, t, :], rstd[:, 8 + t:9 + t], fin_g, ALU.mult, ALU.mult)\
                    .then_inc(S["result"], 1)

        @block.tensor
        def _(pe):
            def begin(u):
                if u >= 8:
                    eng, count = evacuated(u - 8)
                    pe.wait_ge(freed[eng], count)
                return ps[:, u % 8, :]

            def chunk(name, j):
                n = DENSE[name] + j
                pe.wait_ge(loaded[n % RAW], 16 * (n // RAW + 1))
                return raw[:, n % RAW, :]

            def transposed(name, src):
                for j in range(KT // 2):
                    b = begin(UNIT[name] + j)
                    for k in (2 * j, 2 * j + 1):
                        for t in range(TT):
                            at = (k % 2) * T + t * P
                            last = nc.tensor.transpose(b[:, at:at + P], src[:, t, k * P:(k + 1) * P], ident)
                    last.then_inc(S["unit_done"], 1)

            def feature_major(name, act_f):
                for j in range(KT // 2):
                    w = chunk(name, j).rearrange("p (k n) -> p k n", n=2 * P)
                    b = begin(UNIT[name] + j)
                    for n in range(2):
                        for k in range(KT):
                            last = nc.tensor.matmul(b[:, n * T:(n + 1) * T], w[:, k, n * P:(n + 1) * P],
                                                    act_f[:, k, :], start=k == 0, stop=k == KT - 1)
                    last.then_inc(S["unit_done"], 1)

            def token_major(name, act_f):
                banks = [begin(UNIT[name] + i) for i in range(4)]
                for j in range(KT // 2):
                    w = chunk(name, j).rearrange("p (k n) -> p k n", n=D)
                    for kk in range(2):
                        k = 2 * j + kk
                        for i, b in enumerate(banks):
                            t, h = i // 2, i % 2
                            last = nc.tensor.matmul(b, act_f[:, k, t * P:(t + 1) * P], w[:, kk, h * BANK:(h + 1) * BANK],
                                                    start=k == 0, stop=k == KT - 1)
                            if k == KT - 1:
                                last.then_inc(S["unit_done"], 1)
                    if j < KT // 2 - 1:
                        last.then_inc(S["chunk_used"], 1)

            def per_head(name, act_f):
                w = chunk(name, 0).rearrange("p (h k n) -> p h k n", h=HEADS, k=2)
                for h in range(HEADS):
                    b = begin(UNIT[name] + h)
                    for n in range(2):
                        for k in range(2):
                            last = nc.tensor.matmul(b[:, n * T:(n + 1) * T], w[:, h, k, n * P:(n + 1) * P],
                                                    act_f[:, 2 * h + k, :], start=k == 0, stop=k == 1)
                    last.then_inc(S["unit_done"], 1)

            pe.wait_ge(S["in_cst"], 48)
            pe.wait_ge(S["normed"], 2)
            transposed("memT", mem_rows)
            pe.wait_ge(S["freed_dve"], evacuated(UNIT["memT"] + 3)[1])
            feature_major("k", mem_f)
            token_major("v", mem_f)
            pe.wait_ge(S["normed"], 4)
            transposed("xT", xs_rows)
            pe.wait_ge(S["freed_dve"], evacuated(UNIT["xT"] + 3)[1])
            feature_major("lrux", h_f)
            feature_major("pool", h_f)
            pe.wait_ge(S["xr_done"], KT)
            per_head("ra", xr_f)
            per_head("rx", xr_f)
            pe.wait_ge(S["pool_done"], 1)
            per_head("grp", pool_f)
            for name in ("gelu", "ga", "gb"):
                feature_major(name, h_f)
            pe.wait_ge(S["freed_dve"], evacuated(UNIT["grp"] + 3)[1])
            feature_major("pp", pool_f)
            pe.wait_ge(S["yb_done"], 1)
            feature_major("lp", hs_f)
            pe.wait_ge(S["m_done"], 4)
            token_major("mix", m_f)
            pe.wait_ge(S["normed"], 6)
            transposed("x1T", xn_rows)
            pe.wait_ge(S["freed_dve"], evacuated(UNIT["x1T"] + 3)[1])
            feature_major("q", xn_f)
            pe.wait_ge(S["freed_dve"], evacuated(UNIT["q"] + 3)[1])
            for h in range(HEADS):
                b = begin(UNIT["score"] + h)
                for q in range(TT):
                    for k in range(2):
                        last = nc.tensor.matmul(b[:, q * T:(q + 1) * T], q_f[:, 2 * h + k, q * P:(q + 1) * P],
                                                k_f[:, 2 * h + k, :], start=k == 0, stop=k == 1)
                last.then_inc(S["unit_done"], 1)
            for h in range(HEADS):
                pe.wait_ge(S["prob_done"], TT * (h + 1))
                b = begin(UNIT["pT"] + h)
                for m in range(TT):
                    for q in range(TT):
                        at = m * T + q * P
                        last = nc.tensor.transpose(b[:, at:at + P], prob[:, h, q, m * P:(m + 1) * P], ident)
                last.then_inc(S["unit_done"], 1)
            for h in range(HEADS):
                pe.wait_ge(S["freed_act"], evacuated(UNIT["pT"] + h)[1])
                b = begin(UNIT["oT"] + h)
                for n in range(2):
                    for m in range(TT):
                        at = h * HD + n * P
                        last = nc.tensor.matmul(b[:, n * T:(n + 1) * T], v_rows[:, m, at:at + P], probT[:, h, m, :],
                                                start=m == 0, stop=m == TT - 1)
                last.then_inc(S["unit_done"], 1)
            pe.wait_ge(S["freed_dve"], evacuated(UNIT["oT"] + 3)[1])
            token_major("o", o_f)
            pe.wait_ge(S["normed"], 8)
            transposed("xnT", xn_rows)
            pe.wait_ge(S["in_router"], 48)
            pe.wait_ge(S["freed_dve"], evacuated(UNIT["xnT"] + 3)[1])
            b = begin(UNIT["logit"])
            for t in range(TT):
                for k in range(KT):
                    last = nc.tensor.matmul(b[:, t * EXPERTS:(t + 1) * EXPERTS], xn_f[:, k, t * P:(t + 1) * P],
                                            router_w[:, k, :], start=k == 0, stop=k == KT - 1)
            last.then_inc(S["unit_done"], 1)
            pe.wait_ge(S["picked"], 1)
            b = begin(UNIT["rank"])
            lower, whole = mat16[:, 0, :], mat16[:, 1, :]
            for n, terms in enumerate((((lower, 0),), ((whole, 0), (lower, 1)), ((whole, 0), (whole, 1)))):
                for i, (m, t) in enumerate(terms):
                    last = nc.tensor.matmul(b[:, n * EXPERTS:(n + 1) * EXPERTS], m, pick16[:, t, :], start=i == 0,
                                            stop=i == len(terms) - 1)
            last.then_inc(S["unit_done"], 1)
            pe.wait_ge(S["gmat_done"], 1)
            b = begin(UNIT["gT"])
            for t in range(TT):
                last = nc.tensor.transpose(b[0:EXPERTS, t * P:(t + 1) * P], gmat[:, t, :], ident)
            last.then_inc(S["unit_done"], 1)
            pe.wait_ge(S["freed_dve"], evacuated(UNIT["gT"])[1])
            for i in range(4):
                b = begin(UNIT["bd"] + i)
                t, h = i // 2, i % 2
                nc.tensor.matmul(b, gT[:, t * P:(t + 1) * P], bdown_sb[:, h * BANK:(h + 1) * BANK], start=True,
                                 stop=True).then_inc(S["unit_done"], 1)

            def chunk_products(r, e, i, pair, whole32, tiles, bank, opens, closes):
                n = number(r, e, i) - CHUNKS_0
                pe.wait_ge(loaded[place(i) % RAW], fills(r, e, i) * 16)
                pe.wait_ge(S["whi_ready"], n + 1)
                pe.wait_ge(S["wlo_ready"], n + 1)
                for b in range(4):
                    out_ = ps[:, bank(b), :]
                    start, stop = b < opens, b >= 4 - closes
                    k = tiles[b]
                    if b < 3:
                        cut = slice(b * BANK, (b + 1) * BANK)
                        nc.tensor.matmul(out_, pair[:, k, :], whi[:, place(i) % SPL, cut], start=start, stop=False)
                        ins = nc.tensor.matmul(out_, pair[:, k, :], wlo[:, place(i) % SPL, cut], start=False, stop=stop)
                    else:
                        ins = nc.tensor.matmul(out_, whole32[:, k, :], raw[:, place(i) % RAW, SPLIT:], start=start,
                                               stop=stop)
                ins.then_inc(S["chunk_used"], 1)

            def gate_up(r, e, i, k):
                chunk_products(r, e, i, xpair, x32, [k] * 4, lambda b: b, 4 * (k == 0), 4 * (k == KT - 1))

            def down(r, e, i, j):
                chunk_products(r, e, i, hpair, h32, [2 * j, 2 * j, 2 * j + 1, 2 * j + 1], lambda b: 4 + b % 2,
                               2 * (j == 0), 2 * (j == DN_CHUNKS - 1))

            def select(r, e):
                pe.wait_ge(S["onehot_ready"], (r * BLOCKS + e + 1) * TT)
                for k in range(KT):
                    for n in range(3):
                        for t in range(TT):
                            last = nc.tensor.matmul(ps[:, 6, k * SLOTS:(k + 1) * SLOTS],
                                                    xpart[n][:, t, k * P:(k + 1) * P], onehot[:, t, :],
                                                    start=n == 0 and t == 0, stop=n == 2 and t == TT - 1)
                last.then_inc(S["sel_done"], 1)

            def input_ready(r, e):
                pe.wait_ge(S["x_ready"], r * BLOCKS + e + 1)
                pe.wait_ge(S["xhi_ready"], r * BLOCKS + e + 1)
                pe.wait_ge(S["xlo_ready"], r * BLOCKS + e + 1)
                pe.wait_ge(S["gated_out"], (r * EXPERTS + e) * 4 + 4)

            def hidden_ready(r, e, count):
                pe.wait_ge(S["h_ready"], count)
                pe.wait_ge(S["hhi_ready"], count)
                pe.wait_ge(S["hlo_ready"], count)
                pe.wait_ge(S["drow_ready"], r * BLOCKS + e + 1)

            def turn(r, e):
                pe.wait_ge(S["gated_out"], (r * EXPERTS + e) * 4 + 8)
                pe.wait_ge(S["x_ready"], r * BLOCKS + e + 2)
                for j in range(2 * KT):
                    last = nc.tensor.matmul(ps[:, 6 + j // KT, (j % KT) * SLOTS:(j % KT + 1) * SLOTS],
                                            gated[:, j * P:(j + 1) * P], fold, start=True, stop=True)
                last.then_inc(S["turned"], 1)

            pe.wait_ge(S["freed_dve"], evacuated(NUNIT - 1)[1])
            pe.wait_ge(S["part_hi"], 3)
            n = needed_rounds(pe)
            with pe.Fori(0, n) as r:
                select(r, 0)
                input_ready(r, 0)
                for k in range(GU_CHUNKS):
                    gate_up(r, 0, DN_CHUNKS + k, k)
                select(r, 1)
                turn(r, 0)
                with pe.Fori(1, EXPERTS) as e:
                    done = r * EXPERTS + e
                    input_ready(r, e)
                    for k in range(GU_CHUNKS):
                        gate_up(r, e, k, k)
                    pe.wait_ge(S["up_biased"], done)
                    select(r, e + 1)
                    hidden_ready(r, e, done)
                    for j in range(DN_CHUNKS):
                        down(r, e, GU_CHUNKS + j, j)
                    turn(r, e)
                hidden_ready(r, EXPERTS, (r + 1) * EXPERTS)
                for j in range(DN_CHUNKS):
                    down(r, EXPERTS, j, j)


INPUTS = ("x", "mem", "cols", "consts", "dense", "bgu", "b_router", "w_router", "norm_final", "w_gate_up", "w_down",
          "b_down")


def kernel(x, mem, norm_mix, w_in, w_pool_group, pool_scale, w_pool_proj, conv_w, conv_b, lru_w_a, lru_b_a, lru_w_x,
           lru_b_x, lru_lambda, w_lru_proj, w_mix_out, norm_xattn, norm_mem, w_q, w_kv, w_o, norm_moe, w_router,
           b_router, w_gate_up, b_gate_up, w_down, b_down, norm_final):
    import numpy as np
    import concourse.bacc as bacc
    from concourse.bass_utils import run_bass_kernel_spmd

    a = {k: np.asarray(v) for k, v in locals().items() if k not in ("np", "bacc", "run_bass_kernel_spmd")}
    one = lambda name: a[name][0]
    tiles = lambda v: v.reshape(-1, P).T
    cols = np.concatenate([tiles(one(n)) for n in COLS[:-1]] + [tiles(one("conv_w").reshape(-1))], 1)
    consts = np.zeros((P, NCONST), np.float32)
    part = lambda name: consts[:, CONST[name][0]:CONST[name][1]]
    part("ident")[:] = np.eye(P)
    part("fold")[:] = np.concatenate([np.eye(SLOTS)] * 2)
    part("before")[:] = np.triu(np.ones((P, P)), 1)
    part("ones")[:] = 1
    part("iota")[:] = np.arange(T)
    part("inv")[:] = np.concatenate([w / np.minimum(np.arange(PAD) + 1, w) for w in WINDOWS])

    def by_columns(w):
        return w.reshape(KT, P, -1, 2 * P).transpose(2, 1, 0, 3).reshape(-1, P, CHUNK)

    def by_rows(w):
        return w.reshape(KT // 2, 2, P, D).transpose(0, 2, 1, 3).reshape(-1, P, CHUNK)

    def by_heads(w):
        return w.reshape(HEADS, 2, P, HD).transpose(2, 0, 1, 3).reshape(1, P, CHUNK)

    w_in_ = one("w_in")
    kv = one("w_kv")
    section = lambda i: by_columns(w_in_[:, i * D:(i + 1) * D])
    stages = {"k": by_columns(kv[:, :D]), "v": by_rows(kv[:, D:]), "lrux": section(1), "pool": section(0),
              "ra": by_heads(one("lru_w_a")), "rx": by_heads(one("lru_w_x")), "grp": by_heads(one("w_pool_group")),
              "gelu": section(2), "ga": section(3), "gb": section(4), "pp": by_columns(one("w_pool_proj")),
              "lp": by_columns(one("w_lru_proj")), "mix": by_rows(one("w_mix_out")), "q": by_columns(one("w_q")),
              "o": by_rows(one("w_o"))}
    dense = np.concatenate([stages[n] for n in DENSE], 0)
    arrays = {"x": a["x"][0], "mem": a["mem"][0], "cols": cols, "consts": consts, "dense": dense,
              "bgu": one("b_gate_up").reshape(EXPERTS, 2 * KT, P).transpose(2, 0, 1),
              "b_router": np.broadcast_to(one("b_router"), (P, EXPERTS)), "w_router": one("w_router"),
              "norm_final": np.broadcast_to(a["norm_final"], (P, D)),
              "w_gate_up": one("w_gate_up").reshape(EXPERTS * D, 2 * D), "w_down": one("w_down").reshape(EXPERTS * D, D),
              "b_down": one("b_down")}
    arrays = {k: np.ascontiguousarray(arrays[k]) for k in INPUTS}
    nc = bacc.Bacc("TRN2", target_bir_lowering=False, num_devices=1)
    args = {k: nc.dram_tensor(f"in_{k}", v.shape, mybir.dt.from_np(v.dtype), kind="ExternalInput").ap()
            for k, v in arrays.items()}
    args["out"] = nc.dram_tensor("out", (T, D), F32, kind="ExternalOutput").ap()
    build(nc, **args)
    r = run_bass_kernel_spmd(nc, [{f"in_{k}": v for k, v in arrays.items()}], core_ids=[0])
    return r.results[0]["out"].reshape(1, T, D)
```

```python
from contextlib import ExitStack

import concourse.bass as bass
from concourse import mybir

F32 = mybir.dt.float32
F32R = mybir.dt.float32r
BF16 = mybir.dt.bfloat16
I32 = mybir.dt.int32
U32 = mybir.dt.uint32
ALU = mybir.AluOpType
ACT = mybir.ActivationFunctionType
AX = mybir.AxisListType

P = 128
D = 1024
KT = D // P
T = 256
TT = T // P
HEADS = 4
HD = D // HEADS
WINDOWS = (2, 4, 8, 16)
PAD = max(WINDOWS)
CONV = 4
EPS = 1e-6
EXPERTS = 32
TOPK = 4
LIMIT = 7.0
ALPHA = 1.702
CHUNK = 2048
BANK = 512

SLOTS = 64
ROUNDS = T // SLOTS
GU_CHUNKS = KT
DN_CHUNKS = KT // 2
PER_EXPERT = GU_CHUNKS + DN_CHUNKS
RAW = 6
SPL = 4
BLOCKS = EXPERTS + 1
SPLIT = 3 * BANK
DSPL = SPL * SPLIT // CHUNK

COLS = ["norm_mix", "norm_mem", "norm_xattn", "norm_moe", "pool_scale", "conv_b", "lru_b_a", "lru_b_x",
        "lru_lambda", "conv_w"]
COL = {name: KT * i for i, name in enumerate(COLS)}
NCOL = KT * (len(COLS) - 1 + CONV)

CONST = {}
_at = 0
for _name, _n in (("ident", P), ("fold", SLOTS), ("before", P), ("ones", P), ("iota", T), ("inv", len(WINDOWS) * PAD)):
    CONST[_name] = (_at, _at + _n)
    _at += _n
NCONST = _at

DENSE = {}
_at = 0
for _name, _n in (("k", 4), ("v", 4), ("lrux", 4), ("pool", 4), ("ra", 1), ("rx", 1), ("grp", 1), ("gelu", 4),
                  ("ga", 4), ("gb", 4), ("pp", 4), ("lp", 4), ("mix", 4), ("q", 4), ("o", 4)):
    DENSE[_name] = _at
    _at += _n
NDENSE = _at

PER_HEAD = ("ra", "rx", "grp")
SPLIT_CHUNKS = [n for n in range(NDENSE) if n not in [DENSE[name] for name in PER_HEAD]]

OPERANDS = ("mem", "h", "pool", "lru", "merged", "xn", "attn")

UNIT, EVAC = {}, []
for _name, _n, _eng in (("memT", 4, "lo"), ("k", 4, "dve"), ("v", 4, "act"), ("xT", 4, "lo"), ("lrux", 4, "dve"),
                        ("pool", 4, "act"), ("ra", 4, "act"), ("rx", 4, "act"), ("grp", 4, "dve"),
                        ("gelu", 4, "act"), ("ga", 4, "act"), ("gb", 4, "act"), ("pp", 4, "dve"), ("lp", 4, "dve"),
                        ("mix", 4, "dve"), ("x1T", 4, "lo"), ("q", 4, "dve"), ("score", 4, "act"), ("pT", 4, "act"),
                        ("oT", 4, "lo"), ("o", 4, "dve"), ("xnT", 4, "dve"), ("logit", 1, "dve"), ("rank", 1, "dve"),
                        ("gT", 1, "dve"), ("bd", 4, "dve")):
    UNIT[_name] = len(EVAC)
    EVAC += [_eng] * _n
NUNIT = len(EVAC)


def evacuated(unit):
    if EVAC[unit] == "lo":
        for name, operand in (("memT", "mem"), ("xT", "h"), ("x1T", "xn"), ("oT", "attn")):
            if 0 <= unit - UNIT[name] < 4:
                return "lo", split_tiles(operand, 2 * (unit - UNIT[name]) + 1)
    return EVAC[unit], EVAC[: unit + 1].count(EVAC[unit])


def split_tiles(operand, k):
    return KT * OPERANDS.index(operand) + k + 1


TOKEN_MAJOR = ("v", "mix", "o")
CHUNKS_0 = len(TOKEN_MAJOR) * (KT // 2 - 1)


def dense_used():
    used, partial = [], 0
    names = list(DENSE)
    for i, name in enumerate(names):
        count = (DENSE[names[i + 1]] if i + 1 < len(names) else NDENSE) - DENSE[name]
        for j in range(count):
            if name in TOKEN_MAJOR and j < count - 1:
                partial += 1
                used.append(("chunk_used", partial))
            elif name in TOKEN_MAJOR or count == 1:
                used.append(("unit_done", UNIT[name] + 4))
            else:
                used.append(("unit_done", UNIT[name] + j + 1))
    return used


USED = dense_used()


def build(nc, x, mem, cols, consts, dense, bgu, b_router, w_router, norm_final, w_gate_up, w_down, b_down, out):
    ctx = ExitStack()
    sb = lambda name, shape, dt=F32: ctx.enter_context(nc.sbuf_tensor(name, shape, dt))
    sem = lambda name: ctx.enter_context(nc.semaphore(name))
    with ctx:
        scratch = nc.dram_tensor("expert_rows", (BLOCKS * SLOTS, D), F32, kind="Internal").ap()

        raw = sb("raw", [P, RAW, CHUNK])
        whi_all = sb("whi", [P, SPL * SPLIT], F32R)
        wlo_all = sb("wlo", [P, SPL * SPLIT], F32R)
        whi, wlo = (w[:, :].rearrange("p (s c) -> p s c", c=SPLIT) for w in (whi_all, wlo_all))
        dense_hi, dense_lo = (w[:, :].rearrange("p (s c) -> p s c", c=CHUNK) for w in (whi_all, wlo_all))
        act_hi_all = sb("act_hi", [P, KT * T], F32R)
        act_lo_all = sb("act_lo", [P, KT * T], F32R)
        act_hi, act_lo = (a[:, :].rearrange("p (k t) -> p k t", t=T) for a in (act_hi_all, act_lo_all))
        pair = lambda i: act_lo_all[:, i * D:(i + 1) * D].rearrange("p (k c) -> p k c", c=2 * SLOTS)
        xpair, hpair = pair(0), pair(1)
        res = sb("res", [P, TT, D])
        cst = sb("cst", [P, NCONST])
        col = sb("col", [P, NCOL])
        bgu_sb = sb("bgu_sb", [P, EXPERTS, 2 * KT])
        wide = KT * (PAD + T)
        plain = KT * T
        s0, s2, s3, s7, s8, s9 = (sb(f"s{i}", [P, plain]) for i in (0, 2, 3, 7, 8, 9))
        s1, s5, s6 = (sb(f"s{i}", [P, wide]) for i in (1, 5, 6))
        ps = ctx.enter_context(nc.psum_tensor("ps", [P, 8, BANK], F32))

        feat = lambda s: s[:, 0:plain].rearrange("p (k t) -> p k t", t=T)
        rows = lambda s: s[:, 0:plain].rearrange("p (t d) -> p t d", d=D)
        padded = lambda s: s[:, 0:wide].rearrange("p (k t) -> p k t", t=PAD + T)
        c_ = lambda name: cst[:, CONST[name][0]:CONST[name][1]]
        p_ = lambda name, k: col[:, COL[name] + k:COL[name] + k + 1]
        ident, fold, iota = c_("ident"), c_("fold"), c_("iota")

        mem_rows, k_f, v_rows = rows(s0), feat(s2), rows(s3)
        xs_rows = rows(s7)
        u_lru, xr_f = padded(s1), feat(s0)
        u_pool, win_a, win_b, pool_f = padded(s5), padded(s1), padded(s6), feat(s7)
        r_f, i_f, a_f, b_f = feat(s8), feat(s6), feat(s1), feat(s5)
        hs_f, gelu_f, gtmp_f = feat(s8), feat(s9), feat(s0)
        siga_f, sigb_f, m_f = feat(s6), feat(s1), feat(s5)
        xn_rows, q_f = rows(s0), feat(s6)
        xn_f = feat(s6)
        prob = s1[:, 0:plain].rearrange("p (h q m) -> p h q m", h=HEADS, q=TT)
        probT = s5[:, 0:plain].rearrange("p (h m q) -> p h m q", h=HEADS, m=TT)
        half = [s[:, :].bitcast(BF16) for s in (s2, s3)]
        n16 = TT * D
        xpart = [v.rearrange("p (t d) -> p t d", d=D)
                 for v in (half[0][:, 0:n16], half[0][:, n16:2 * n16], half[1][:, 0:n16])]
        onehot = half[1][:, n16:n16 + TT * SLOTS].rearrange("p (t c) -> p t c", c=SLOTS)
        rest_rows = rows(s8)
        gated = s5[:, 0:2 * D]
        x32, h32 = (s6[:, i * D:(i + 1) * D].rearrange("p (k c) -> p k c", c=2 * SLOTS) for i in range(2))
        gate, up, sig, lin = (s8[:, BANK * i:BANK * (i + 1)].rearrange("p (k c) -> p k c", c=SLOTS) for i in range(4))
        dlow, drow = s7[0:SLOTS, 0:D], s7[0:SLOTS, D:2 * D]
        router_w = s9[:, 0:KT * EXPERTS].rearrange("p (k e) -> p k e", e=EXPERTS)
        router_b = s9[:, KT * EXPERTS:(KT + 1) * EXPERTS]
        bdown_sb = s9[0:EXPERTS, BANK:BANK + D]
        fin_g = s9[:, 0:D]
        gather = [s[:, D * i:D * (i + 1)] for s in (s0, s1, s5, s8) for i in range(2)]

        router = sb("router", [P, 1000])
        at = [0]

        def carve(n):
            at[0] += n
            assert at[0] <= 1000
            return router[:, at[0] - n:at[0]]

        ssum, root, rstd = carve(10), carve(10), carve(10)
        smax, snegm, ssm, srec = carve(8), carve(8), carve(8), carve(8)
        lam_mag, lam_y, lam_s, lam_z, lam_p, lam_c = (carve(KT) for _ in range(6))
        logit, pick, rankp, gmat, rowid, roundid, tmp = (carve(TT * EXPERTS).rearrange("p (t e) -> p t e", e=EXPERTS)
                                                for _ in range(7))
        rank_or_no = carve(TT * BLOCKS).rearrange("p (t e) -> p t e", e=BLOCKS)
        top8, idxf = carve(8 * TT), carve(8 * TT)
        gates, gsum, grec, negtop = carve(TOPK * TT), carve(TT), carve(TT), carve(TT)
        slotf, chosen_round, weight = carve(TOPK * TT), carve(TOPK * TT), carve(TOPK * TT)
        cntmax, nround = carve(1), carve(1)
        idx8 = sb("idx8", [P, 8 * TT], U32)
        sloti = sb("sloti", [P, TOPK * TT], I32)
        pick16 = sb("pick16", [P, TT, EXPERTS], BF16)
        mat16 = sb("mat16", [P, 2, P], BF16)
        nround_i = sb("nround_i", [P, 1], I32)
        gT = sb("gT", [EXPERTS, T])

        loaded = [sem(f"loaded{i}") for i in range(RAW)]
        names = """in_x in_mem in_cst in_bgu in_router in_fin
            dense_hi_ready dense_lo_ready hi_done lo_done
            chunk_used unit_done freed_dve freed_act squared rooted normed dve_seq act_seq
            lam_abs lam_exp pads_zero xr_done pool_done decay_done inner_done mult_done scan_done
            gelu_arg gelu_sig yb_done m_done lam_done rowmax prob_done part_hi part_rest
            gate_in gate_exp picked gmat_done  route_done
            onehot_ready sel_done x_ready xhi_ready xlo_ready whi_ready wlo_ready gated_out turned
            gate_biased up_biased gate_ready up_ready lin_ready sig_ready h_ready hhi_ready hlo_ready
            dlow_out drow_ready stored drow_free weighed summed fin_sum fin_sq fin_root fin_rec result written""".split()
        S = {n: sem(n) for n in names}
        gathered = [sem(f"gathered{i}") for i in range(TT * TOPK)]
        freed = {"dve": S["freed_dve"], "act": S["freed_act"], "lo": S["lo_done"]}

        block = ctx.enter_context(nc.Block())

        PER_ROUND = PER_EXPERT * EXPERTS

        def number(r, e, i):
            return r * PER_ROUND + e * PER_EXPERT + (CHUNKS_0 - DN_CHUNKS + i)

        def place(i):
            return NDENSE - DN_CHUNKS + i

        def fills(r, e, i):
            return r * (PER_ROUND // RAW) + e * (PER_EXPERT // RAW) + (place(i) // RAW + 1)

        def needed_rounds(eng):
            eng.wait_ge(S["route_done"], 1)
            return eng.value_load(nround_i[0:1, 0:1], min_val=1, max_val=ROUNDS)

        @block.sync
        def _(sp):
            sp.dma_start(mem_rows, mem.rearrange("(t p) d -> p t d", p=P)).then_inc(S["in_mem"], 16)
            used = USED
            for n in range(NDENSE):
                if n >= RAW:
                    name, count = used[n - RAW]
                    sp.wait_ge(S[name], count)
                sp.dma_start(raw[:, n % RAW, :], dense[n]).then_inc(loaded[n % RAW], 16)
                if n == 1:
                    sp.dma_start(res[:], x.rearrange("(t p) d -> p t d", p=P)).then_inc(S["in_x"], 16)

            def gate_up_chunk(r, e, i, k):
                sp.wait_ge(S["chunk_used"], number(r, e, i) - (RAW - 1))
                sp.dma_start(raw[:, place(i) % RAW, :], w_gate_up[bass.ds(e * D + k * P, P), :])\
                    .then_inc(loaded[place(i) % RAW], 16)

            def down_chunk(r, e, i, k):
                sp.wait_ge(S["chunk_used"], number(r, e, i) - (RAW - 1))
                rows2 = w_down[bass.ds((e - 1) * D + k * 2 * P, 2 * P), :]
                sp.dma_start(raw[:, place(i) % RAW, :].rearrange("p (f d) -> p f d", d=D),
                             rows2.rearrange("(f p) d -> p f d", p=P)).then_inc(loaded[place(i) % RAW], 16)

            for k in range(RAW):
                name, count = used[NDENSE - RAW + k]
                sp.wait_ge(S[name], count)
                sp.dma_start(raw[:, (NDENSE + k) % RAW, :], w_gate_up[k * P:(k + 1) * P, :])\
                    .then_inc(loaded[(NDENSE + k) % RAW], 16)
            n = needed_rounds(sp)
            with sp.Fori(0, n) as r:
                for k in range(RAW, GU_CHUNKS):
                    gate_up_chunk(r, 0, DN_CHUNKS + k, k)
                with sp.Fori(1, EXPERTS) as e:
                    for k in range(GU_CHUNKS):
                        gate_up_chunk(r, e, k, k)
                    for k in range(DN_CHUNKS):
                        down_chunk(r, e, GU_CHUNKS + k, k)
                for k in range(DN_CHUNKS):
                    down_chunk(r, EXPERTS, k, k)
                with sp.If(r + 1 < n):
                    for k in range(RAW):
                        gate_up_chunk(r + 1, 0, DN_CHUNKS + k, k)
            for t in range(TT):
                sp.wait_ge(S["result"], t + 1)
                sp.dma_start(out[t * P:(t + 1) * P, :], res[:, t, :]).then_inc(S["written"], 16)
            sp.wait_ge(S["written"], 16 * TT)

        @block.gpsimd
        def _(pool):
            pool.dma_start(bgu_sb[:], bgu).then_inc(S["in_bgu"], 16)
            for m, n in enumerate(SPLIT_CHUNKS):
                pool.wait_ge(S["dense_hi_ready"], m + 1)
                nc.gpsimd.tensor_tensor(dense_lo[:, m % DSPL, :], raw[:, n % RAW, :],
                                        dense_hi[:, m % DSPL, :].bitcast(F32), ALU.subtract)\
                    .then_inc(S["dense_lo_ready"], 1)
            pool.wait_ge(S["yb_done"], 1)
            pool.dma_start(router_w, w_router.rearrange("(k p) e -> p k e", p=P)).then_inc(S["in_router"], 16)
            pool.dma_start(router_b, b_router).then_inc(S["in_router"], 16)
            pool.dma_start(bdown_sb, b_down).then_inc(S["in_router"], 16)
            pool.wait_ge(S["freed_dve"], evacuated(NUNIT - 1)[1])
            pool.dma_start(fin_g, norm_final).then_inc(S["in_fin"], 16)
            pool.sem_inc(S["drow_free"], 1)
            n = needed_rounds(pool)
            with pool.Fori(0, n) as r:
                with pool.Fori(0, BLOCKS) as k:
                    done = r * BLOCKS + k + 1
                    pool.wait_ge(S["drow_ready"], done + 1)
                    pool.dma_start(scratch[bass.ds(k * SLOTS, SLOTS), :], drow)\
                        .then_inc(S["stored"], 16)
                    pool.wait_ge(S["stored"], done * 16)
                    pool.sem_inc(S["drow_free"], 1)
                for j in range(TT * TOPK):
                    pool.indirect_dma_start(gather[j], None, scratch,
                                            bass.IndirectOffsetOnAxis(ap=sloti[:, j:j + 1], axis=0))\
                        .then_inc(gathered[j], 16)
                for j in range(TT * TOPK):
                    pool.wait_ge(gathered[j], (r + 1) * 16)

        @block.scalar
        def _(act):
            act.dma_start(cst[:], consts).then_inc(S["in_cst"], 16)
            act.dma_start(col[:], cols).then_inc(S["in_cst"], 16)

            def squares(n, src, junk):
                for t in range(TT):
                    nc.scalar.activation(junk[:, t, :], src[:, t, :], ACT.Square,
                                         accum_out=ssum[:, 2 * n + t:2 * n + t + 1]).then_inc(S["squared"], 1)
                act.wait_ge(S["squared"], 2 * n + 2)
                nc.scalar.activation(root[:, 2 * n:2 * n + 2], ssum[:, 2 * n:2 * n + 2], ACT.Sqrt,
                                     scale=1.0 / D, bias=EPS).then_inc(S["rooted"], 1)

            def units(name, n, fn):
                for j in range(n):
                    u = UNIT[name] + j
                    act.wait_ge(S["unit_done"], u + 1)
                    fn(j, ps[:, u % 8, :])

            two = lambda b: b.rearrange("p (k t) -> p k t", t=T)

            next_split = [0]

            def weights_after(name, j):
                while next_split[0] < len(SPLIT_CHUNKS):
                    m = next_split[0]
                    if m >= DSPL:
                        if SPLIT_CHUNKS[m - DSPL] > DENSE[name] + j:
                            break
                        who, count = USED[SPLIT_CHUNKS[m - DSPL]]
                        act.wait_ge(S[who], count)
                    elif m > j + DSPL:
                        break
                    n = SPLIT_CHUNKS[m]
                    act.wait_ge(loaded[n % RAW], 16 * (n // RAW + 1))
                    nc.scalar.activation(dense_hi[:, m % DSPL, :], raw[:, n % RAW, :], ACT.Copy)\
                        .then_inc(S["dense_hi_ready"], 1)
                    next_split[0] += 1

            def high_from_psum(name, gain):
                def fn(j, b):
                    for k in (2 * j, 2 * j + 1):
                        nc.scalar.activation(act_hi[:, k, :], b[:, (k % 2) * T:(k % 2 + 1) * T], ACT.Copy,
                                             scale=p_(gain, k) if gain else 1.0).then_inc(S["hi_done"], 1)
                units(name, 4, fn)

            def high_of(src, j):
                nc.scalar.activation(act_hi[:, 2 * j:2 * j + 2, :], src[:, 2 * j:2 * j + 2, :], ACT.Copy)\
                    .then_inc(S["hi_done"], 2)

            def evacuate(name, j, fn):
                u = UNIT[name] + j
                act.wait_ge(S["unit_done"], u + 1)
                fn(j, ps[:, u % 8, :])

            act.wait_ge(S["in_mem"], 16)
            squares(0, mem_rows, rows(s9))
            weights_after("k", -3)
            act.wait_ge(S["in_cst"], 32)
            high_from_psum("memT", "norm_mem")
            weights_after("k", 0)
            act.wait_ge(S["in_x"], 16)
            squares(1, res, xs_rows)
            act.wait_ge(S["lam_abs"], 1)
            nc.scalar.activation(lam_y, lam_mag, ACT.Exp, scale=-1.0).then_inc(S["lam_exp"], 1)
            weights_after("k", 3)
            weights_after("v", 2)
            units("v", 4, lambda j, b: nc.scalar.activation(
                v_rows[:, j // 2, (j % 2) * BANK:(j % 2 + 1) * BANK], b, ACT.Copy).then_inc(S["freed_act"], 1))
            high_from_psum("xT", "norm_mix")
            weights_after("v", 3)
            weights_after("lrux", 3)
            act.wait_ge(S["pads_zero"], 1)
            for j in range(4):
                evacuate("pool", j, lambda j, b: nc.scalar.activation(
                    u_pool[:, 2 * j:2 * j + 2, PAD:], two(b), ACT.Copy).then_inc(S["freed_act"], 1))
                weights_after("pool", j)

            def logistic_gate(dst, bias):
                def fn(j, b):
                    for k in (2 * j, 2 * j + 1):
                        ins = nc.scalar.activation(dst[:, k, :], b[:, (k % 2) * T:(k % 2 + 1) * T], ACT.Sigmoid,
                                                   bias=p_(bias, k))
                        ins.then_inc(S["freed_act"] if k % 2 else S["act_seq"], 1)
                return fn
            units("ra", 4, logistic_gate(r_f, "lru_b_a"))
            act.wait_ge(S["pool_done"], 1)
            units("rx", 4, logistic_gate(i_f, "lru_b_x"))
            act.wait_ge(S["freed_act"], evacuated(UNIT["ra"] + 3)[1])
            act.wait_ge(S["act_seq"], 8)
            act.wait_ge(S["lam_done"], 1)
            for k in range(KT):
                nc.scalar.activation(a_f[:, k, :], r_f[:, k, :], ACT.Exp, scale=lam_c[:, k:k + 1])\
                    .then_inc(S["decay_done"], 1)
                nc.scalar.activation(b_f[:, k, :], r_f[:, k, :], ACT.Tanh, scale=lam_c[:, k:k + 1])\
                    .then_inc(S["decay_done"], 1)
            for j in range(4):
                evacuate("gelu", j, lambda j, b: nc.scalar.activation(
                    gelu_f[:, 2 * j:2 * j + 2, :], two(b), ACT.Copy).then_inc(S["freed_act"], 1))
                weights_after("gelu", j)
                if j == 1:
                    act.wait_ge(S["inner_done"], 1)
                    nc.scalar.activation(b_f, b_f, ACT.Sqrt, scale=-1.0).then_inc(S["mult_done"], 1)
            act.wait_ge(S["scan_done"], KT)
            for j in range(4):
                evacuate("ga", j, lambda j, b: nc.scalar.activation(
                    siga_f[:, 2 * j:2 * j + 2, :], two(b), ACT.Sigmoid).then_inc(S["freed_act"], 1))
                weights_after("ga", j)
                if j == 1:
                    act.wait_ge(S["gelu_arg"], 1)
                    nc.scalar.activation(gtmp_f, gtmp_f, ACT.Sigmoid, scale=2.0 * 0.7978845608028654)\
                        .then_inc(S["gelu_sig"], 1)
            act.wait_ge(S["freed_dve"], evacuated(UNIT["grp"] + 3)[1])
            for j in range(4):
                if j == 3:
                    act.wait_ge(S["unit_done"], UNIT["gb"] + 4)
                    for i in range(4):
                        high_of(pool_f, i)
                evacuate("gb", j, lambda j, b: nc.scalar.activation(
                    sigb_f[:, 2 * j:2 * j + 2, :], two(b), ACT.Sigmoid).then_inc(S["freed_act"], 1))
                weights_after("gb", j)
            weights_after("pp", 2)
            act.wait_ge(S["yb_done"], 1)
            act.wait_ge(S["unit_done"], UNIT["pp"] + 4)
            for j in range(4):
                high_of(hs_f, j)
            weights_after("pp", 3)
            weights_after("lp", 2)
            act.wait_ge(S["unit_done"], UNIT["lp"] + 4)
            for j in range(4):
                act.wait_ge(S["m_done"], j + 1)
                high_of(m_f, j)
            weights_after("lp", 3)
            weights_after("mix", 2)
            act.wait_ge(S["freed_dve"], evacuated(UNIT["mix"] + 3)[1])
            squares(2, res, xn_rows)
            weights_after("mix", 3)
            high_from_psum("x1T", "norm_xattn")
            weights_after("q", 3)

            def exps(j, b):
                act.wait_ge(S["rowmax"], j + 1)
                for q in range(TT):
                    ins = nc.scalar.activation(prob[:, j, q, :], b[:, q * T:(q + 1) * T], ACT.Exp, scale=HD ** -0.5,
                                               bias=snegm[:, 2 * j + q:2 * j + q + 1],
                                               accum_out=ssm[:, 2 * j + q:2 * j + q + 1])
                    ins.then_inc(S["freed_act"] if q else S["act_seq"], 1)
            units("score", 4, exps)
            units("pT", 4, lambda j, b: nc.scalar.activation(
                probT[:, j, :, :], b.rearrange("p (m q) -> p m q", q=T), ACT.Copy).then_inc(S["freed_act"], 1))
            high_from_psum("oT", None)
            weights_after("o", 3)
            act.wait_ge(S["freed_dve"], evacuated(UNIT["o"] + 3)[1])
            squares(3, res, xn_rows)
            act.wait_ge(S["normed"], 8)
            nc.scalar.activation(xpart[0], xn_rows, ACT.Copy).then_inc(S["part_hi"], 1)
            for n in (1, 2):
                act.wait_ge(S["part_rest"], n)
                nc.scalar.activation(xpart[n], rest_rows, ACT.Copy).then_inc(S["part_hi"], 1)
            act.wait_ge(S["gate_in"], 1)
            for t in range(TT):
                nc.scalar.activation(gates[:, TOPK * t:TOPK * (t + 1)], top8[:, 8 * t:8 * t + TOPK], ACT.Exp,
                                     bias=negtop[:, t:t + 1], accum_out=gsum[:, t:t + 1]).then_inc(S["gate_exp"], 1)
            act.preload_act_table(ACT.Sigmoid)

            def split(r, e, i):
                act.wait_ge(loaded[place(i) % RAW], fills(r, e, i) * 16)
                act.wait_ge(S["chunk_used"], number(r, e, i) - (SPL - 1))
                nc.scalar.activation(whi[:, place(i) % SPL, :], raw[:, place(i) % RAW, 0:SPLIT], ACT.Copy)\
                    .then_inc(S["whi_ready"], 1)

            def x_high(r, e):
                act.wait_ge(S["x_ready"], r * BLOCKS + e + 1)
                nc.scalar.activation(xpair[:, :, 0:SLOTS], x32[:, :, 0:SLOTS], ACT.Copy).then_inc(S["xhi_ready"], 1)

            def rows_out(r, e, i):
                act.wait_ge(S["chunk_used"], number(r, e, i))
                for b in range(4):
                    nc.scalar.activation(gated[:, b * BANK:(b + 1) * BANK], ps[:, b, :], ACT.Copy)\
                        .then_inc(S["gated_out"], 1)

            def low_rows(r, e, k):
                act.wait_ge(S["chunk_used"], number(r, e, 0))
                act.wait_ge(S["drow_ready"], r * BLOCKS + k + 1)
                nc.scalar.activation(dlow, ps[SLOTS:2 * SLOTS, 4:6, :].rearrange("p b n -> p (b n)"), ACT.Copy)\
                    .then_inc(S["dlow_out"], 1)

            def gate_sigmoid(count):
                act.wait_ge(S["gate_ready"], count)
                nc.scalar.activation(sig, gate, ACT.Sigmoid, scale=ALPHA).then_inc(S["sig_ready"], 1)

            def h_high(count):
                act.wait_ge(S["h_ready"], count)
                nc.scalar.activation(hpair[:, :, 0:SLOTS], h32[:, :, 0:SLOTS], ACT.Copy).then_inc(S["hhi_ready"], 1)

            act.sem_inc(S["gated_out"], 4)
            n = needed_rounds(act)
            with act.Fori(0, n) as r:
                x_high(r, 0)
                for i in range(DN_CHUNKS, PER_EXPERT - 1):
                    split(r, 0, i)
                split(r, 0, PER_EXPERT - 1)
                rows_out(r, 0, PER_EXPERT)
                x_high(r, 1)
                with act.Fori(1, EXPERTS) as e:
                    done = r * EXPERTS + e
                    for i in range(PER_EXPERT):
                        if i == 4:
                            low_rows(r, e, e - 1)
                        if i == 5:
                            gate_sigmoid(done)
                        if i == 6:
                            h_high(done)
                        if i == 11:
                            rows_out(r, e, GU_CHUNKS)
                            x_high(r, e + 1)
                        split(r, e, i)
                low_rows(r, EXPERTS, EXPERTS - 1)
                gate_sigmoid((r + 1) * EXPERTS)
                for i in range(DN_CHUNKS):
                    split(r, EXPERTS, i)
                    if i == 0:
                        h_high((r + 1) * EXPERTS)
                act.wait_ge(S["chunk_used"], number(r, EXPERTS, DN_CHUNKS))
                low_rows(r, EXPERTS, EXPERTS)
            for t in range(TT):
                act.wait_ge(S["fin_sum"], 1)
                nc.scalar.activation(xs_rows[:, t, :], res[:, t, :], ACT.Square,
                                     accum_out=ssum[:, 8 + t:9 + t]).then_inc(S["fin_sq"], 1)
                act.wait_ge(S["fin_sq"], t + 1)
                nc.scalar.activation(root[:, 8 + t:9 + t], ssum[:, 8 + t:9 + t], ACT.Sqrt, scale=1.0 / D,
                                     bias=EPS).then_inc(S["fin_root"], 1)

        @block.vector
        def _(dve):
            V = nc.vector
            seq = [0]

            def link(ins):
                seq[0] += 1
                ins.then_inc(S["dve_seq"], 1)
                dve.wait_ge(S["dve_seq"], seq[0])

            def units(name, n, fn):
                for j in range(n):
                    u = UNIT[name] + j
                    dve.wait_ge(S["unit_done"], u + 1)
                    fn(j, ps[:, u % 8, :])

            two = lambda b: b.rearrange("p (k t) -> p k t", t=T)

            def normalise(n, src, dst):
                dve.wait_ge(S["rooted"], n + 1)
                link(V.reciprocal(rstd[:, 2 * n:2 * n + 2], root[:, 2 * n:2 * n + 2]))
                for t in range(TT):
                    V.tensor_scalar(dst[:, t, :], src[:, t, :], rstd[:, 2 * n + t:2 * n + t + 1], None, ALU.mult)\
                        .then_inc(S["normed"], 1)

            def gained(dst, gain):
                def fn(j, b):
                    V.tensor_scalar(dst[:, 2 * j, :], b[:, 0:T], p_(gain, 2 * j), None, ALU.mult)\
                        .then_inc(S["dve_seq"], 1)
                    seq[0] += 1
                    V.tensor_scalar(dst[:, 2 * j + 1, :], b[:, T:2 * T], p_(gain, 2 * j + 1), None, ALU.mult)\
                        .then_inc(S["freed_dve"], 1)
                return fn

            def copied(dst):
                return lambda j, b: V.tensor_copy(dst[:, 2 * j:2 * j + 2, :], two(b)).then_inc(S["freed_dve"], 1)

            def low_from_psum(name, operand, gain):
                def fn(j, b):
                    dve.wait_ge(S["hi_done"], split_tiles(operand, 2 * j + 1))
                    for k in (2 * j, 2 * j + 1):
                        V.scalar_tensor_tensor(act_lo[:, k, :], b[:, (k % 2) * T:(k % 2 + 1) * T],
                                               p_(gain, k) if gain else 1.0, act_hi[:, k, :].bitcast(F32), ALU.mult,
                                               ALU.subtract).then_inc(S["lo_done"], 1)
                units(name, 4, fn)

            def low_of(src, operand, j):
                dve.wait_ge(S["hi_done"], split_tiles(operand, 2 * j + 1))
                V.tensor_tensor(act_lo[:, 2 * j:2 * j + 2, :], src[:, 2 * j:2 * j + 2, :],
                                act_hi[:, 2 * j:2 * j + 2, :].bitcast(F32), ALU.subtract).then_inc(S["lo_done"], 2)

            dve.wait_ge(S["in_cst"], 32)
            lam0 = col[:, COL["lru_lambda"]:COL["lru_lambda"] + KT]
            link(V.scalar_tensor_tensor(lam_mag, lam0, -1.0, lam0, ALU.mult, ALU.max))
            dve.sem_inc(S["lam_abs"], 1)
            V.memset(u_pool[:, :, 0:PAD], 0.0).then_inc(S["pads_zero"], 1)
            V.tensor_copy(mat16[:, :, :], cst[:, CONST["before"][0]:CONST["ones"][1]].rearrange(
                "p (a b) -> p a b", a=2)).then_inc(S["dve_seq"], 1)
            seq[0] += 1
            normalise(0, mem_rows, mem_rows)
            low_from_psum("memT", "mem", "norm_mem")
            normalise(1, res, xs_rows)
            dve.wait_ge(S["lam_exp"], 1)
            link(V.tensor_scalar(lam_s, lam_y, 2.0, None, ALU.add))
            link(V.reciprocal(lam_s, lam_s))
            link(V.tensor_tensor(lam_s, lam_s, lam_y, ALU.mult))
            link(V.tensor_tensor(lam_z, lam_s, lam_s, ALU.mult))
            link(V.tensor_scalar(lam_p, lam_z, 1.0 / 19, None, ALU.mult))
            for odd in range(17, 1, -2):
                link(V.scalar_tensor_tensor(lam_p, lam_p, 1.0 / odd, lam_z, ALU.add, ALU.mult))
            link(V.scalar_tensor_tensor(lam_p, lam_p, 1.0, lam_s, ALU.add, ALU.mult))
            link(V.tensor_scalar(lam_z, lam0, 0.0, 8.0, ALU.min, ALU.mult))
            link(V.scalar_tensor_tensor(lam_c, lam_p, -16.0, lam_z, ALU.mult, ALU.add))
            dve.sem_inc(S["lam_done"], 1)
            units("k", 4, copied(k_f))
            low_from_psum("xT", "h", "norm_mix")
            link(V.memset(u_lru[:, :, 0:PAD], 0.0))
            units("lrux", 4, lambda j, b: V.tensor_copy(
                u_lru[:, 2 * j:2 * j + 2, PAD:], two(b)).then_inc(S["freed_dve"], 1))
            dve.wait_ge(S["freed_dve"], evacuated(UNIT["lrux"] + 3)[1])
            for tap in range(CONV):
                shift = PAD - (CONV - 1) + tap
                for k in range(KT):
                    w = col[:, COL["conv_w"] + KT * tap + k:COL["conv_w"] + KT * tap + k + 1]
                    if tap == 0:
                        ins = V.tensor_scalar(xr_f[:, k, :], u_lru[:, k, shift:shift + T], w, p_("conv_b", k),
                                              ALU.mult, ALU.add)
                    else:
                        ins = V.scalar_tensor_tensor(xr_f[:, k, :], u_lru[:, k, shift:shift + T], w, xr_f[:, k, :],
                                                     ALU.mult, ALU.add)
                    if tap == CONV - 1:
                        ins.then_inc(S["xr_done"], 1)
                    else:
                        ins.then_inc(S["dve_seq"], 1)
                        seq[0] += 1
                if tap < CONV - 1:
                    dve.wait_ge(S["dve_seq"], seq[0])
            dve.wait_ge(S["xr_done"], KT)
            dve.wait_ge(S["freed_act"], evacuated(UNIT["pool"] + 3)[1])
            end = PAD + T
            link(V.tensor_tensor(win_a[:, 0:8, 2:end], u_pool[:, 0:8, 2:end], u_pool[:, 0:8, 1:end - 1], ALU.add))
            link(V.tensor_tensor(win_b[:, 2:8, 4:end], win_a[:, 2:8, 4:end], win_a[:, 2:8, 2:end - 2], ALU.add))
            link(V.tensor_tensor(win_a[:, 4:8, 8:end], win_b[:, 4:8, 8:end], win_b[:, 4:8, 4:end - 4], ALU.add))
            link(V.tensor_tensor(win_b[:, 6:8, 16:end], win_a[:, 6:8, 16:end], win_a[:, 6:8, 8:end - 8], ALU.add))
            for g, w in enumerate(WINDOWS):
                src = (win_a, win_b)[g % 2]
                early = src[:, 2 * g:2 * g + 2, PAD:2 * PAD]
                inv = c_("inv")[:, PAD * g:PAD * (g + 1)].unsqueeze(1).broadcast_to([P, 2, PAD])
                link(V.tensor_tensor(early, early, inv, ALU.mult))
                link(V.scalar_tensor_tensor(pool_f[:, 2 * g:2 * g + 2, :], src[:, 2 * g:2 * g + 2, PAD:], 1.0 / w,
                                            u_pool[:, 2 * g:2 * g + 2, PAD:], ALU.mult, ALU.subtract))
            dve.sem_inc(S["pool_done"], 1)

            def scaled(j, b):
                for k in (2 * j, 2 * j + 1):
                    V.tensor_scalar(pool_f[:, k, :], b[:, (k % 2) * T:(k % 2 + 1) * T], p_("pool_scale", k), None,
                                    ALU.mult).then_inc(S["freed_dve"] if k % 2 else S["dve_seq"], 1)
                seq[0] += 1
            units("grp", 4, scaled)

            dve.wait_ge(S["decay_done"], 2 * KT)
            link(V.tensor_tensor(r_f, a_f, a_f, ALU.mult))
            link(V.scalar_tensor_tensor(b_f, r_f, 1.0, b_f, ALU.add, ALU.mult))
            V.tensor_scalar(b_f, b_f, 0.0, None, ALU.min).then_inc(S["inner_done"], 1)
            dve.wait_ge(S["freed_act"], evacuated(UNIT["rx"] + 3)[1])
            dve.wait_ge(S["mult_done"], 1)
            link(V.memset(b_f[:, :, 0:1], 1.0))
            link(V.tensor_tensor(b_f, b_f, i_f, ALU.mult))
            link(V.tensor_tensor(b_f, b_f, xr_f, ALU.mult))
            for k in range(KT):
                V.tensor_tensor_scan(hs_f[:, k, :], a_f[:, k, :], b_f[:, k, :], 0.0, ALU.mult, ALU.add)\
                    .then_inc(S["scan_done"], 1)
            dve.wait_ge(S["freed_act"], evacuated(UNIT["gelu"] + 3)[1])
            link(V.tensor_tensor(gtmp_f, gelu_f, gelu_f, ALU.mult))
            link(V.tensor_scalar(gtmp_f, gtmp_f, 0.044715, 1.0, ALU.mult, ALU.add))
            V.tensor_tensor(gtmp_f, gtmp_f, gelu_f, ALU.mult).then_inc(S["gelu_arg"], 1)
            dve.wait_ge(S["scan_done"], KT)
            link(V.tensor_tensor(hs_f, hs_f, gelu_f, ALU.mult))
            dve.wait_ge(S["gelu_sig"], 1)
            V.tensor_tensor(hs_f, hs_f, gtmp_f, ALU.mult).then_inc(S["yb_done"], 1)
            for j in range(4):
                low_of(pool_f, "pool", j)
            dve.wait_ge(S["freed_act"], evacuated(UNIT["gb"] + 3)[1])
            units("pp", 4, lambda j, b: V.tensor_tensor(
                m_f[:, 2 * j:2 * j + 2, :], siga_f[:, 2 * j:2 * j + 2, :], two(b), ALU.mult)
                .then_inc(S["freed_dve"], 1))

            for j in range(4):
                low_of(hs_f, "lru", j)

            def merge(j, b):
                t2 = sigb_f[:, 2 * j:2 * j + 2, :]
                V.tensor_tensor(t2, t2, two(b), ALU.mult).then_inc(S["freed_dve"], 1)
                dve.wait_ge(S["freed_dve"], evacuated(UNIT["lp"] + j)[1])
                V.tensor_tensor(m_f[:, 2 * j:2 * j + 2, :], m_f[:, 2 * j:2 * j + 2, :], t2, ALU.add)\
                    .then_inc(S["m_done"], 1)
            units("lp", 4, merge)
            for j in range(4):
                low_of(m_f, "merged", j)

            def onto_residual(j, b):
                part = res[:, j // 2, (j % 2) * BANK:(j % 2 + 1) * BANK]
                V.tensor_tensor(part, part, b, ALU.add).then_inc(S["freed_dve"], 1)
            units("mix", 4, onto_residual)
            normalise(2, res, xn_rows)
            low_from_psum("x1T", "xn", "norm_xattn")
            units("q", 4, copied(q_f))

            def maxima(j, b):
                link(V.tensor_reduce(smax[:, 2 * j:2 * j + 2], two(b), AX.X, ALU.max))
                V.tensor_scalar(snegm[:, 2 * j:2 * j + 2], smax[:, 2 * j:2 * j + 2], -(HD ** -0.5), None, ALU.mult)\
                    .then_inc(S["rowmax"], 1)
            units("score", 4, maxima)
            for j in range(HEADS):
                dve.wait_ge(S["freed_act"], evacuated(UNIT["score"] + j)[1])
                dve.wait_ge(S["act_seq"], 8 + j + 1)
                link(V.reciprocal(srec[:, 2 * j:2 * j + 2], ssm[:, 2 * j:2 * j + 2]))
                for q in range(TT):
                    V.tensor_scalar(prob[:, j, q, :], prob[:, j, q, :], srec[:, 2 * j + q:2 * j + q + 1], None,
                                    ALU.mult).then_inc(S["prob_done"], 1)
            low_from_psum("oT", "attn", None)
            units("o", 4, onto_residual)
            normalise(3, res, xn_rows)
            units("xnT", 4, gained(xn_f, "norm_moe"))
            for n in range(2):
                dve.wait_ge(S["part_hi"], n + 1)
                V.tensor_tensor(rest_rows, (xn_rows, rest_rows)[n], xpart[n], ALU.subtract)\
                    .then_inc(S["part_rest"], 1)

            dve.wait_ge(S["in_router"], 48)
            u = UNIT["logit"]
            dve.wait_ge(S["unit_done"], u + 1)
            bias = router_b.unsqueeze(1).broadcast_to([P, TT, EXPERTS])
            V.tensor_tensor(logit, ps[:, u % 8, 0:TT * EXPERTS].rearrange("p (t e) -> p t e", e=EXPERTS), bias, ALU.add)\
                .then_inc(S["freed_dve"], 1)
            dve.wait_ge(S["freed_dve"], evacuated(u)[1])
            tops = lambda v, t, j: v[:, 8 * t + j:8 * t + j + 1]
            for t in range(TT):
                link(V.max(top8[:, 8 * t:8 * t + 8], logit[:, t, :]))
                link(V.max_index(idx8[:, 8 * t:8 * t + 8], top8[:, 8 * t:8 * t + 8], logit[:, t, :]))
                link(V.tensor_scalar(negtop[:, t:t + 1], tops(top8, t, 0), -1.0, None, ALU.mult))
            dve.sem_inc(S["gate_in"], 1)
            link(V.tensor_copy(idxf, idx8[:]))
            places = iota[:, 0:EXPERTS]
            for t in range(TT):
                link(V.tensor_scalar(pick[:, t, :], places, tops(idxf, t, 0), None, ALU.is_equal))
                for j in range(1, TOPK):
                    link(V.scalar_tensor_tensor(pick[:, t, :], places, tops(idxf, t, j), pick[:, t, :], ALU.is_equal,
                                                ALU.add))
            V.tensor_copy(pick16[:], pick).then_inc(S["picked"], 1)
            dve.wait_ge(S["gate_exp"], TT)
            link(V.reciprocal(grec, gsum))
            for t in range(TT):
                mine = gates[:, TOPK * t:TOPK * (t + 1)]
                link(V.tensor_scalar(mine, mine, grec[:, t:t + 1], None, ALU.mult))
                for j in range(TOPK):
                    g = gates[:, TOPK * t + j:TOPK * t + j + 1]
                    dst = gmat[:, t, :] if j == 0 else tmp[:, t, :]
                    link(V.tensor_scalar(dst, places, tops(idxf, t, j), g, ALU.is_equal, ALU.mult))
                    if j:
                        link(V.tensor_tensor(gmat[:, t, :], gmat[:, t, :], tmp[:, t, :], ALU.add))
            dve.sem_inc(S["gmat_done"], 1)
            u = UNIT["rank"]
            dve.wait_ge(S["unit_done"], u + 1)
            got = ps[:, u % 8, 0:3 * EXPERTS].rearrange("p (t e) -> p t e", e=EXPERTS)
            link(V.tensor_copy(rankp, got[:, 0:TT, :]))
            V.tensor_reduce(cntmax, got[:, TT, :], AX.X, ALU.max).then_inc(S["freed_dve"], 1)
            dve.wait_ge(S["freed_dve"], evacuated(u)[1])
            link(V.tensor_scalar(nround, cntmax, float(SLOTS), 1.0, ALU.is_gt, ALU.add))
            for n in range(2, ROUNDS):
                link(V.scalar_tensor_tensor(nround, cntmax, float(SLOTS * n), nround, ALU.is_gt, ALU.add))
            link(V.tensor_copy(nround_i[:], nround))
            link(V.memset(rank_or_no, 0.0))
            link(V.scalar_tensor_tensor(rank_or_no[:, :, 0:EXPERTS], rankp, 1.0, pick, ALU.add, ALU.mult))
            link(V.tensor_scalar(rank_or_no, rank_or_no, -1.0, None, ALU.add))
            dve.sem_inc(S["route_done"], 1)
            link(V.tensor_scalar(rowid, places.unsqueeze(1).broadcast_to([P, TT, EXPERTS]), float(SLOTS), float(SLOTS),
                                 ALU.mult, ALU.add))
            link(V.tensor_tensor(rowid, rowid, rankp, ALU.add))
            link(V.tensor_scalar(roundid, rankp, float(SLOTS), None, ALU.is_ge))
            for n in range(2, ROUNDS):
                link(V.scalar_tensor_tensor(roundid, rankp, float(SLOTS * n), roundid, ALU.is_ge, ALU.add))
            link(V.scalar_tensor_tensor(rowid, roundid, -float(SLOTS), rowid, ALU.mult, ALU.add))
            for dst, table in ((slotf, rowid), (chosen_round, roundid)):
                for t in range(TT):
                    for j in range(TOPK):
                        link(V.scalar_tensor_tensor(tmp[:, t, :], places, tops(idxf, t, j), table[:, t, :],
                                                    ALU.is_equal, ALU.mult,
                                                    accum_out=dst[:, TOPK * t + j:TOPK * t + j + 1]))
            link(V.tensor_copy(sloti[:], slotf))
            u = UNIT["gT"]
            dve.wait_ge(S["unit_done"], u + 1)
            V.tensor_copy(gT[:], ps[0:EXPERTS, u % 8, 0:T]).then_inc(S["freed_dve"], 1)
            units("bd", 4, onto_residual)

            def split(r, e, i):
                dve.wait_ge(S["whi_ready"], number(r, e, i) - (CHUNKS_0 - 1))
                V.tensor_tensor(wlo[:, place(i) % SPL, :], raw[:, place(i) % RAW, 0:SPLIT],
                                whi[:, place(i) % SPL, :].bitcast(F32), ALU.subtract).then_inc(S["wlo_ready"], 1)

            def select(r, e):
                for t in range(TT):
                    V.tensor_scalar(onehot[:, t, :], iota[:, bass.ds(r * SLOTS, SLOTS)],
                                    rank_or_no[:, t, bass.ds(e, 1)], None, ALU.is_equal)\
                        .then_inc(S["onehot_ready"], 1)

            gain = col[:, COL["norm_moe"]:COL["norm_moe"] + KT].unsqueeze(2).broadcast_to([P, KT, SLOTS])

            def x_whole(r, e):
                dve.wait_ge(S["sel_done"], r * BLOCKS + e + 1)
                V.tensor_tensor(x32[:, :, 0:SLOTS], ps[:, 6, :].rearrange("p (k c) -> p k c", c=SLOTS), gain,
                                ALU.mult).then_inc(S["x_ready"], 1)

            def x_low(r, e):
                dve.wait_ge(S["xhi_ready"], r * BLOCKS + e + 1)
                V.tensor_tensor(xpair[:, :, SLOTS:], x32[:, :, 0:SLOTS], xpair[:, :, 0:SLOTS].bitcast(F32),
                                ALU.subtract).then_inc(S["xlo_ready"], 1)

            dve.wait_ge(S["in_bgu"], 16)

            def add_bias(r, e, count):
                dve.wait_ge(S["turned"], count)
                for n, (dst, name) in enumerate(((gate, "gate_biased"), (up, "up_biased"))):
                    b = bgu_sb[:, bass.ds(e, 1), KT * n:KT * (n + 1)].rearrange("p o k -> p (o k)").unsqueeze(2)
                    V.tensor_tensor(dst, ps[:, 6 + n, :].rearrange("p (k c) -> p k c", c=SLOTS),
                                    b.broadcast_to([P, KT, SLOTS]), ALU.add).then_inc(S[name], 1)
                dve.wait_ge(S["gate_biased"], count)
                V.tensor_scalar(gate, gate, LIMIT, None, ALU.min).then_inc(S["gate_ready"], 1)

            def swiglu(count):
                dve.wait_ge(S["up_biased"], count)
                V.tensor_scalar(up, up, LIMIT, -LIMIT, ALU.min, ALU.max).then_inc(S["up_ready"], 1)
                dve.wait_ge(S["up_ready"], count)
                dve.wait_ge(S["gate_ready"], count)
                V.scalar_tensor_tensor(lin, up, 1.0, gate, ALU.add, ALU.mult).then_inc(S["lin_ready"], 1)
                dve.wait_ge(S["lin_ready"], count)
                dve.wait_ge(S["sig_ready"], count)
                V.tensor_tensor(h32[:, :, 0:SLOTS], sig, lin, ALU.mult).then_inc(S["h_ready"], 1)

            def h_low(count):
                dve.wait_ge(S["hhi_ready"], count)
                V.tensor_tensor(hpair[:, :, SLOTS:], h32[:, :, 0:SLOTS], hpair[:, :, 0:SLOTS].bitcast(F32),
                                ALU.subtract).then_inc(S["hlo_ready"], 1)

            def sum_rows(r, k):
                dve.wait_ge(S["dlow_out"], r * BLOCKS + k + 1)
                dve.wait_ge(S["drow_free"], r * BLOCKS + k + 1)
                V.tensor_tensor(drow, ps[0:SLOTS, 4:6, :].rearrange("p b n -> p (b n)"), dlow, ALU.add)\
                    .then_inc(S["drow_ready"], 1)

            link(V.memset(x32[:, :, SLOTS:], 0.0))
            link(V.memset(h32[:, :, SLOTS:], 0.0))
            dve.sem_inc(S["drow_ready"], 1)
            n = needed_rounds(dve)
            with dve.Fori(0, n) as r:
                select(r, 0)
                x_whole(r, 0)
                x_low(r, 0)
                for i in range(DN_CHUNKS, PER_EXPERT):
                    if i == DN_CHUNKS + 1:
                        dve.wait_ge(S["sel_done"], r * BLOCKS + 1)
                        select(r, 1)
                    split(r, 0, i)
                dve.wait_ge(S["chunk_used"], number(r, 0, PER_EXPERT))
                x_whole(r, 1)
                x_low(r, 1)
                with dve.Fori(1, EXPERTS) as e:
                    done = r * EXPERTS + e
                    for i in range(PER_EXPERT):
                        if i == 4:
                            add_bias(r, e - 1, done)
                        if i == 5:
                            swiglu(done)
                        if i == 6:
                            sum_rows(r, e - 1)
                        if i == 7:
                            h_low(done)
                            dve.wait_ge(S["sel_done"], r * BLOCKS + e + 1)
                            select(r, e + 1)
                        if i == 11:
                            dve.wait_ge(S["chunk_used"], number(r, e, GU_CHUNKS))
                            x_whole(r, e + 1)
                        split(r, e, i)
                    x_low(r, e + 1)
                add_bias(r, EXPERTS - 1, (r + 1) * EXPERTS)
                split(r, EXPERTS, 0)
                swiglu((r + 1) * EXPERTS)
                sum_rows(r, EXPERTS - 1)
                split(r, EXPERTS, 1)
                h_low((r + 1) * EXPERTS)
                split(r, EXPERTS, 2)
                split(r, EXPERTS, 3)
                sum_rows(r, EXPERTS)
                V.scalar_tensor_tensor(weight, chosen_round, iota[:, bass.ds(r, 1)], gates, ALU.is_equal, ALU.mult)\
                    .then_inc(S["weighed"], 1)
                dve.wait_ge(S["weighed"], r + 1)
                for j in range(TOPK):
                    for t in range(TT):
                        i = TOPK * t + j
                        dve.wait_ge(gathered[i], (r + 1) * 16)
                        if j:
                            dve.wait_ge(S["summed"], r * (TT * TOPK) + (TT * (j - 1) + t + 1))
                        V.scalar_tensor_tensor(res[:, t, :], gather[i], weight[:, i:i + 1], res[:, t, :], ALU.mult,
                                               ALU.add).then_inc(S["summed"], 1)
                dve.wait_ge(S["summed"], (r + 1) * (TT * TOPK))
            dve.sem_inc(S["fin_sum"], 1)
            dve.wait_ge(S["in_fin"], 16)
            for t in range(TT):
                dve.wait_ge(S["fin_root"], t + 1)
                link(V.reciprocal(rstd[:, 8 + t:9 + t], root[:, 8 + t:9 + t]))
                V.scalar_tensor_tensor(res[:, t, :], res[:, t, :], rstd[:, 8 + t:9 + t], fin_g, ALU.mult, ALU.mult)\
                    .then_inc(S["result"], 1)

        @block.tensor
        def _(pe):
            def begin(u):
                if u >= 8:
                    eng, count = evacuated(u - 8)
                    pe.wait_ge(freed[eng], count)
                return ps[:, u % 8, :]

            def chunk(name, j):
                n = DENSE[name] + j
                pe.wait_ge(loaded[n % RAW], 16 * (n // RAW + 1))
                return raw[:, n % RAW, :]

            def transposed(name, src):
                for j in range(KT // 2):
                    b = begin(UNIT[name] + j)
                    for k in (2 * j, 2 * j + 1):
                        for t in range(TT):
                            at = (k % 2) * T + t * P
                            last = nc.tensor.transpose(b[:, at:at + P], src[:, t, k * P:(k + 1) * P], ident)
                    last.then_inc(S["unit_done"], 1)

            def parts(name, j):
                m = SPLIT_CHUNKS.index(DENSE[name] + j)
                pe.wait_ge(S["dense_hi_ready"], m + 1)
                pe.wait_ge(S["dense_lo_ready"], m + 1)
                return dense_hi[:, m % DSPL, :], dense_lo[:, m % DSPL, :]

            def tiles_ready(operand, k):
                pe.wait_ge(S["hi_done"], split_tiles(operand, k))
                pe.wait_ge(S["lo_done"], split_tiles(operand, k))

            def feature_major(name, operand):
                for j in range(KT // 2):
                    w_hi, w_lo = (w.rearrange("p (k n) -> p k n", n=2 * P) for w in parts(name, j))
                    b = begin(UNIT[name] + j)
                    for n in range(2):
                        cut = slice(n * P, (n + 1) * P)
                        for k in range(KT):
                            if j == 0 and n == 0:
                                tiles_ready(operand, k)
                            o = b[:, n * T:(n + 1) * T]
                            nc.tensor.matmul(o, w_hi[:, k, cut], act_hi[:, k, :], start=k == 0, stop=False)
                            nc.tensor.matmul(o, w_hi[:, k, cut], act_lo[:, k, :], start=False, stop=False)
                            last = nc.tensor.matmul(o, w_lo[:, k, cut], act_hi[:, k, :], start=False,
                                                    stop=k == KT - 1)
                    last.then_inc(S["unit_done"], 1)

            def token_major(name, operand):
                banks = [begin(UNIT[name] + i) for i in range(4)]
                for j in range(KT // 2):
                    w_hi, w_lo = (w.rearrange("p (k n) -> p k n", n=D) for w in parts(name, j))
                    for kk in range(2):
                        k = 2 * j + kk
                        tiles_ready(operand, k)
                        for t in range(TT):
                            mine = slice(t * P, (t + 1) * P)
                            for h in range(2):
                                b, cut = banks[2 * t + h], slice(h * BANK, (h + 1) * BANK)
                                nc.tensor.matmul(b, act_hi[:, k, mine], w_hi[:, kk, cut], start=k == 0, stop=False)
                                nc.tensor.matmul(b, act_hi[:, k, mine], w_lo[:, kk, cut], start=False, stop=False)
                                last = nc.tensor.matmul(b, act_lo[:, k, mine], w_hi[:, kk, cut], start=False,
                                                        stop=k == KT - 1)
                                if k == KT - 1:
                                    last.then_inc(S["unit_done"], 1)
                    if j < KT // 2 - 1:
                        last.then_inc(S["chunk_used"], 1)

            def per_head(name, act_f):
                w = chunk(name, 0).rearrange("p (h k n) -> p h k n", h=HEADS, k=2)
                for h in range(HEADS):
                    b = begin(UNIT[name] + h)
                    for n in range(2):
                        for k in range(2):
                            last = nc.tensor.matmul(b[:, n * T:(n + 1) * T], w[:, h, k, n * P:(n + 1) * P],
                                                    act_f[:, 2 * h + k, :], start=k == 0, stop=k == 1)
                    last.then_inc(S["unit_done"], 1)

            pe.wait_ge(S["in_cst"], 32)
            pe.wait_ge(S["normed"], 2)
            transposed("memT", mem_rows)
            feature_major("k", "mem")
            token_major("v", "mem")
            pe.wait_ge(S["normed"], 4)
            transposed("xT", xs_rows)
            feature_major("lrux", "h")
            feature_major("pool", "h")
            pe.wait_ge(S["xr_done"], KT)
            per_head("ra", xr_f)
            per_head("rx", xr_f)
            pe.wait_ge(S["pool_done"], 1)
            per_head("grp", pool_f)
            for name in ("gelu", "ga", "gb"):
                feature_major(name, "h")
            feature_major("pp", "pool")
            feature_major("lp", "lru")
            token_major("mix", "merged")
            pe.wait_ge(S["normed"], 6)
            transposed("x1T", xn_rows)
            feature_major("q", "xn")
            pe.wait_ge(S["freed_dve"], evacuated(UNIT["q"] + 3)[1])
            for h in range(HEADS):
                b = begin(UNIT["score"] + h)
                for q in range(TT):
                    for k in range(2):
                        last = nc.tensor.matmul(b[:, q * T:(q + 1) * T], q_f[:, 2 * h + k, q * P:(q + 1) * P],
                                                k_f[:, 2 * h + k, :], start=k == 0, stop=k == 1)
                last.then_inc(S["unit_done"], 1)
            for h in range(HEADS):
                pe.wait_ge(S["prob_done"], TT * (h + 1))
                b = begin(UNIT["pT"] + h)
                for m in range(TT):
                    for q in range(TT):
                        at = m * T + q * P
                        last = nc.tensor.transpose(b[:, at:at + P], prob[:, h, q, m * P:(m + 1) * P], ident)
                last.then_inc(S["unit_done"], 1)
            for h in range(HEADS):
                pe.wait_ge(S["freed_act"], evacuated(UNIT["pT"] + h)[1])
                b = begin(UNIT["oT"] + h)
                for n in range(2):
                    for m in range(TT):
                        at = h * HD + n * P
                        last = nc.tensor.matmul(b[:, n * T:(n + 1) * T], v_rows[:, m, at:at + P], probT[:, h, m, :],
                                                start=m == 0, stop=m == TT - 1)
                last.then_inc(S["unit_done"], 1)
            token_major("o", "attn")
            pe.wait_ge(S["normed"], 8)
            transposed("xnT", xn_rows)
            pe.wait_ge(S["in_router"], 48)
            pe.wait_ge(S["freed_dve"], evacuated(UNIT["xnT"] + 3)[1])
            b = begin(UNIT["logit"])
            for t in range(TT):
                for k in range(KT):
                    last = nc.tensor.matmul(b[:, t * EXPERTS:(t + 1) * EXPERTS], xn_f[:, k, t * P:(t + 1) * P],
                                            router_w[:, k, :], start=k == 0, stop=k == KT - 1)
            last.then_inc(S["unit_done"], 1)
            pe.wait_ge(S["picked"], 1)
            b = begin(UNIT["rank"])
            lower, whole = mat16[:, 0, :], mat16[:, 1, :]
            for n, terms in enumerate((((lower, 0),), ((whole, 0), (lower, 1)), ((whole, 0), (whole, 1)))):
                for i, (m, t) in enumerate(terms):
                    last = nc.tensor.matmul(b[:, n * EXPERTS:(n + 1) * EXPERTS], m, pick16[:, t, :], start=i == 0,
                                            stop=i == len(terms) - 1)
            last.then_inc(S["unit_done"], 1)
            pe.wait_ge(S["gmat_done"], 1)
            b = begin(UNIT["gT"])
            for t in range(TT):
                last = nc.tensor.transpose(b[0:EXPERTS, t * P:(t + 1) * P], gmat[:, t, :], ident)
            last.then_inc(S["unit_done"], 1)
            pe.wait_ge(S["freed_dve"], evacuated(UNIT["gT"])[1])
            for i in range(4):
                b = begin(UNIT["bd"] + i)
                t, h = i // 2, i % 2
                nc.tensor.matmul(b, gT[:, t * P:(t + 1) * P], bdown_sb[:, h * BANK:(h + 1) * BANK], start=True,
                                 stop=True).then_inc(S["unit_done"], 1)

            def chunk_products(r, e, i, pair, whole32, tiles, bank, opens, closes):
                n = number(r, e, i) - CHUNKS_0
                pe.wait_ge(loaded[place(i) % RAW], fills(r, e, i) * 16)
                pe.wait_ge(S["whi_ready"], n + 1)
                pe.wait_ge(S["wlo_ready"], n + 1)
                for b in range(4):
                    out_ = ps[:, bank(b), :]
                    start, stop = b < opens, b >= 4 - closes
                    k = tiles[b]
                    if b < 3:
                        cut = slice(b * BANK, (b + 1) * BANK)
                        nc.tensor.matmul(out_, pair[:, k, :], whi[:, place(i) % SPL, cut], start=start, stop=False)
                        ins = nc.tensor.matmul(out_, pair[:, k, :], wlo[:, place(i) % SPL, cut], start=False, stop=stop)
                    else:
                        ins = nc.tensor.matmul(out_, whole32[:, k, :], raw[:, place(i) % RAW, SPLIT:], start=start,
                                               stop=stop)
                ins.then_inc(S["chunk_used"], 1)

            def gate_up(r, e, i, k):
                chunk_products(r, e, i, xpair, x32, [k] * 4, lambda b: b, 4 * (k == 0), 4 * (k == KT - 1))

            def down(r, e, i, j):
                chunk_products(r, e, i, hpair, h32, [2 * j, 2 * j, 2 * j + 1, 2 * j + 1], lambda b: 4 + b % 2,
                               2 * (j == 0), 2 * (j == DN_CHUNKS - 1))

            def select(r, e):
                pe.wait_ge(S["onehot_ready"], (r * BLOCKS + e + 1) * TT)
                for k in range(KT):
                    for n in range(3):
                        for t in range(TT):
                            last = nc.tensor.matmul(ps[:, 6, k * SLOTS:(k + 1) * SLOTS],
                                                    xpart[n][:, t, k * P:(k + 1) * P], onehot[:, t, :],
                                                    start=n == 0 and t == 0, stop=n == 2 and t == TT - 1)
                last.then_inc(S["sel_done"], 1)

            def input_ready(r, e):
                pe.wait_ge(S["x_ready"], r * BLOCKS + e + 1)
                pe.wait_ge(S["xhi_ready"], r * BLOCKS + e + 1)
                pe.wait_ge(S["xlo_ready"], r * BLOCKS + e + 1)
                pe.wait_ge(S["gated_out"], (r * EXPERTS + e) * 4 + 4)

            def hidden_ready(r, e, count):
                pe.wait_ge(S["h_ready"], count)
                pe.wait_ge(S["hhi_ready"], count)
                pe.wait_ge(S["hlo_ready"], count)
                pe.wait_ge(S["drow_ready"], r * BLOCKS + e + 1)

            def turn(r, e):
                pe.wait_ge(S["gated_out"], (r * EXPERTS + e) * 4 + 8)
                pe.wait_ge(S["x_ready"], r * BLOCKS + e + 2)
                for j in range(2 * KT):
                    last = nc.tensor.matmul(ps[:, 6 + j // KT, (j % KT) * SLOTS:(j % KT + 1) * SLOTS],
                                            gated[:, j * P:(j + 1) * P], fold, start=True, stop=True)
                last.then_inc(S["turned"], 1)

            pe.wait_ge(S["freed_dve"], evacuated(NUNIT - 1)[1])
            pe.wait_ge(S["part_hi"], 3)
            n = needed_rounds(pe)
            with pe.Fori(0, n) as r:
                select(r, 0)
                input_ready(r, 0)
                for k in range(GU_CHUNKS):
                    gate_up(r, 0, DN_CHUNKS + k, k)
                select(r, 1)
                turn(r, 0)
                with pe.Fori(1, EXPERTS) as e:
                    done = r * EXPERTS + e
                    input_ready(r, e)
                    for k in range(GU_CHUNKS):
                        gate_up(r, e, k, k)
                    pe.wait_ge(S["up_biased"], done)
                    select(r, e + 1)
                    hidden_ready(r, e, done)
                    for j in range(DN_CHUNKS):
                        down(r, e, GU_CHUNKS + j, j)
                    turn(r, e)
                hidden_ready(r, EXPERTS, (r + 1) * EXPERTS)
                for j in range(DN_CHUNKS):
                    down(r, EXPERTS, j, j)


INPUTS = ("x", "mem", "cols", "consts", "dense", "bgu", "b_router", "w_router", "norm_final", "w_gate_up", "w_down",
          "b_down")


def kernel(x, mem, norm_mix, w_in, w_pool_group, pool_scale, w_pool_proj, conv_w, conv_b, lru_w_a, lru_b_a, lru_w_x,
           lru_b_x, lru_lambda, w_lru_proj, w_mix_out, norm_xattn, norm_mem, w_q, w_kv, w_o, norm_moe, w_router,
           b_router, w_gate_up, b_gate_up, w_down, b_down, norm_final):
    import numpy as np
    import concourse.bacc as bacc
    from concourse.bass_utils import run_bass_kernel_spmd

    a = {k: np.asarray(v) for k, v in locals().items() if k not in ("np", "bacc", "run_bass_kernel_spmd")}
    one = lambda name: a[name][0]
    tiles = lambda v: v.reshape(-1, P).T
    cols = np.concatenate([tiles(one(n)) for n in COLS[:-1]] + [tiles(one("conv_w").reshape(-1))], 1)
    consts = np.zeros((P, NCONST), np.float32)
    part = lambda name: consts[:, CONST[name][0]:CONST[name][1]]
    part("ident")[:] = np.eye(P)
    part("fold")[:] = np.concatenate([np.eye(SLOTS)] * 2)
    part("before")[:] = np.triu(np.ones((P, P)), 1)
    part("ones")[:] = 1
    part("iota")[:] = np.arange(T)
    part("inv")[:] = np.concatenate([w / np.minimum(np.arange(PAD) + 1, w) for w in WINDOWS])

    def by_columns(w):
        return w.reshape(KT, P, -1, 2 * P).transpose(2, 1, 0, 3).reshape(-1, P, CHUNK)

    def by_rows(w):
        return w.reshape(KT // 2, 2, P, D).transpose(0, 2, 1, 3).reshape(-1, P, CHUNK)

    def by_heads(w):
        return w.reshape(HEADS, 2, P, HD).transpose(2, 0, 1, 3).reshape(1, P, CHUNK)

    w_in_ = one("w_in")
    kv = one("w_kv")
    section = lambda i: by_columns(w_in_[:, i * D:(i + 1) * D])
    stages = {"k": by_columns(kv[:, :D]), "v": by_rows(kv[:, D:]), "lrux": section(1), "pool": section(0),
              "ra": by_heads(one("lru_w_a")), "rx": by_heads(one("lru_w_x")), "grp": by_heads(one("w_pool_group")),
              "gelu": section(2), "ga": section(3), "gb": section(4), "pp": by_columns(one("w_pool_proj")),
              "lp": by_columns(one("w_lru_proj")), "mix": by_rows(one("w_mix_out")), "q": by_columns(one("w_q")),
              "o": by_rows(one("w_o"))}
    dense = np.concatenate([stages[n] for n in DENSE], 0)
    arrays = {"x": a["x"][0], "mem": a["mem"][0], "cols": cols, "consts": consts, "dense": dense,
              "bgu": one("b_gate_up").reshape(EXPERTS, 2 * KT, P).transpose(2, 0, 1),
              "b_router": np.broadcast_to(one("b_router"), (P, EXPERTS)), "w_router": one("w_router"),
              "norm_final": np.broadcast_to(a["norm_final"], (P, D)),
              "w_gate_up": one("w_gate_up").reshape(EXPERTS * D, 2 * D), "w_down": one("w_down").reshape(EXPERTS * D, D),
              "b_down": one("b_down")}
    arrays = {k: np.ascontiguousarray(arrays[k]) for k in INPUTS}
    nc = bacc.Bacc("TRN2", target_bir_lowering=False, num_devices=1)
    args = {k: nc.dram_tensor(f"in_{k}", v.shape, mybir.dt.from_np(v.dtype), kind="ExternalInput").ap()
            for k, v in arrays.items()}
    args["out"] = nc.dram_tensor("out", (T, D), F32, kind="ExternalOutput").ap()
    build(nc, **args)
    r = run_bass_kernel_spmd(nc, [{f"in_{k}": v for k, v in arrays.items()}], core_ids=[0])
    return r.results[0]["out"].reshape(1, T, D)
```

```python
from contextlib import ExitStack

import concourse.bass as bass
from concourse import mybir

F32 = mybir.dt.float32
F32R = mybir.dt.float32r
BF16 = mybir.dt.bfloat16
I32 = mybir.dt.int32
U32 = mybir.dt.uint32
ALU = mybir.AluOpType
ACT = mybir.ActivationFunctionType
AX = mybir.AxisListType

P = 128
D = 1024
KT = D // P
T = 256
TT = T // P
HEADS = 4
HD = D // HEADS
WINDOWS = (2, 4, 8, 16)
PAD = max(WINDOWS)
CONV = 4
EPS = 1e-6
EXPERTS = 32
TOPK = 4
LIMIT = 7.0
ALPHA = 1.702
CHUNK = 2048
BANK = 512

SLOTS = 64
ROUNDS = T // SLOTS
GU_CHUNKS = KT
DN_CHUNKS = KT // 2
PER_EXPERT = GU_CHUNKS + DN_CHUNKS
RAW = 6
SPL = 3
BLOCKS = EXPERTS + 1
DVE_COLS = 1280

COLS = ["norm_mix", "norm_mem", "norm_xattn", "norm_moe", "pool_scale", "conv_b", "lru_b_a", "lru_b_x",
        "lru_lambda", "conv_w"]
COL = {name: KT * i for i, name in enumerate(COLS)}
NCOL = KT * (len(COLS) - 1 + CONV)

CONST = {}
_at = 0
for _name, _n in (("ident", P), ("fold", SLOTS), ("before", P), ("ones", P), ("iota", T), ("inv", len(WINDOWS) * PAD)):
    CONST[_name] = (_at, _at + _n)
    _at += _n
NCONST = _at

DENSE = {}
_at = 0
for _name, _n in (("k", 4), ("v", 4), ("lrux", 4), ("pool", 4), ("ra", 1), ("rx", 1), ("grp", 1), ("gelu", 4),
                  ("ga", 4), ("gb", 4), ("pp", 4), ("lp", 4), ("mix", 4), ("q", 4), ("o", 4)):
    DENSE[_name] = _at
    _at += _n
NDENSE = _at

PER_HEAD = ("ra", "rx", "grp")
SPLIT_CHUNKS = [n for n in range(NDENSE) if n not in [DENSE[name] for name in PER_HEAD]]

OPERANDS = ("mem", "h", "pool", "lru", "merged", "xn", "attn")

UNIT, EVAC = {}, []
for _name, _n, _eng in (("memT", 4, ["lo"]), ("k", 4, ["dve"]), ("v", 4, ["act"]), ("xT", 4, ["lo"]),
                        ("lrux", 4, ["dve"]), ("pool", 4, ["act"]), ("ra", 4, ["act"]), ("rx", 4, ["act"]),
                        ("grp", 4, ["dve"]), ("gelu", 4, ["act"]), ("ga", 4, ["act"]), ("gb", 4, ["act"]),
                        ("pp", 4, ["dve"]), ("lp", 4, ["dve"]), ("mix", 4, ["dve"]), ("x1T", 4, ["lo"]),
                        ("q", 4, ["dve"]), ("score", 4, ["act"]), ("pT", 4, ["act"]), ("oT", 4, ["lo"]),
                        ("o", 4, ["dve"]), ("xnT", 4, ["dve", "act"]), ("logit", 1, ["dve"]),
                        ("rank", 1, ["dve"])):
    UNIT[_name] = len(EVAC)
    EVAC += list(_eng) * (_n // len(_eng))
NUNIT = len(EVAC)


def evacuated(unit):
    if EVAC[unit] == "lo":
        for name, operand in (("memT", "mem"), ("xT", "h"), ("x1T", "xn"), ("oT", "attn")):
            if 0 <= unit - UNIT[name] < 4:
                return "lo", split_tiles(operand, 2 * (unit - UNIT[name]) + 1)
    return EVAC[unit], EVAC[: unit + 1].count(EVAC[unit])


def split_tiles(operand, k):
    return KT * OPERANDS.index(operand) + k + 1


TOKEN_MAJOR = ("v", "mix", "o")
CHUNKS_0 = len(TOKEN_MAJOR) * (KT // 2 - 1)


def dense_used():
    used, partial = [], 0
    names = list(DENSE)
    for i, name in enumerate(names):
        count = (DENSE[names[i + 1]] if i + 1 < len(names) else NDENSE) - DENSE[name]
        for j in range(count):
            if name in TOKEN_MAJOR and j < count - 1:
                partial += 1
                used.append(("chunk_used", partial))
            elif name in TOKEN_MAJOR or count == 1:
                used.append(("unit_done", UNIT[name] + 4))
            else:
                used.append(("unit_done", UNIT[name] + j + 1))
    return used


USED = dense_used()


def build(nc, x, mem, cols, consts, dense, bgu, b_router, w_router, norm_final, w_gate_up, w_down, b_down, out):
    ctx = ExitStack()
    sb = lambda name, shape, dt=F32: ctx.enter_context(nc.sbuf_tensor(name, shape, dt))
    sem = lambda name: ctx.enter_context(nc.semaphore(name))
    with ctx:
        raw = sb("raw", [P, RAW, CHUNK])
        whi = sb("whi", [P, SPL, CHUNK], F32R)
        wlo = sb("wlo", [P, SPL, CHUNK], F32R)
        act_hi_all = sb("act_hi", [P, KT * T], F32R)
        act_lo_all = sb("act_lo", [P, KT * T], F32R)
        act_hi, act_lo = (a[:, :].rearrange("p (k t) -> p k t", t=T) for a in (act_hi_all, act_lo_all))
        pair = lambda i: act_lo_all[:, i * D:(i + 1) * D].rearrange("p (k c) -> p k c", c=2 * SLOTS)
        xpair, hpair = pair(0), pair(1)
        res = sb("res", [P, TT, D])
        cst = sb("cst", [P, NCONST])
        col = sb("col", [P, NCOL])
        bgu_sb = sb("bgu_sb", [P, EXPERTS, 2 * KT])
        wide = KT * (PAD + T)
        plain = KT * T
        s0, s2, s3, s7, s8, s9 = (sb(f"s{i}", [P, plain]) for i in (0, 2, 3, 7, 8, 9))
        s1, s5, s6 = (sb(f"s{i}", [P, wide]) for i in (1, 5, 6))
        ps = ctx.enter_context(nc.psum_tensor("ps", [P, 8, BANK], F32))

        feat = lambda s: s[:, 0:plain].rearrange("p (k t) -> p k t", t=T)
        rows = lambda s: s[:, 0:plain].rearrange("p (t d) -> p t d", d=D)
        padded = lambda s: s[:, 0:wide].rearrange("p (k t) -> p k t", t=PAD + T)
        c_ = lambda name: cst[:, CONST[name][0]:CONST[name][1]]
        p_ = lambda name, k: col[:, COL[name] + k:COL[name] + k + 1]
        ident, fold, iota = c_("ident"), c_("fold"), c_("iota")

        mem_rows, k_f, v_rows = rows(s0), feat(s2), rows(s3)
        xs_rows = rows(s7)
        u_lru, xr_f = padded(s1), feat(s0)
        u_pool, win_a, win_b, pool_f = padded(s5), padded(s1), padded(s6), feat(s7)
        r_f, i_f, a_f, b_f = feat(s8), feat(s6), feat(s1), feat(s5)
        hs_f, gelu_f, gtmp_f = feat(s8), feat(s9), feat(s0)
        siga_f, sigb_f, m_f = feat(s6), feat(s1), feat(s5)
        xn_rows, q_f = rows(s0), feat(s6)
        xn_f = feat(s6)
        prob = s1[:, 0:plain].rearrange("p (h q m) -> p h q m", h=HEADS, q=TT)
        probT = s5[:, 0:plain].rearrange("p (h m q) -> p h m q", h=HEADS, m=TT)
        half = [s[:, :].bitcast(BF16) for s in (s2, s3)]
        n16 = TT * D
        xpart = [v.rearrange("p (t d) -> p t d", d=D)
                 for v in (half[0][:, 0:n16], half[0][:, n16:2 * n16], half[1][:, 0:n16])]
        onehot = half[1][:, n16:n16 + TT * SLOTS].rearrange("p (t c) -> p t c", c=SLOTS)
        rest_rows = rows(s8)
        gated = s5[:, 0:2 * D]
        x32, h32 = (s6[:, i * BANK:(i + 1) * BANK].rearrange("p (k c) -> p k c", c=SLOTS) for i in range(2))
        gate, up, sig, lin = (s8[:, BANK * i:BANK * (i + 1)].rearrange("p (k c) -> p k c", c=SLOTS) for i in range(4))
        y_rows = s7[:, 0:D]
        wone = s7[:, D:D + TT * P].rearrange("p (t two c) -> p t two c", t=TT, two=2)
        wturned = s7[:, D + TT * P:D + 2 * TT * P].rearrange("p (t q) -> p t q", t=TT)
        router_w = s9[:, 0:KT * EXPERTS].rearrange("p (k e) -> p k e", e=EXPERTS)
        router_b = s9[:, KT * EXPERTS:(KT + 1) * EXPERTS]
        bdown_sb = s9[0:EXPERTS, BANK:BANK + D]
        fin_g = s0[:, 0:D]

        router = sb("router", [P, 1000])
        at = [0]

        def carve(n):
            at[0] += n
            assert at[0] <= 1000
            return router[:, at[0] - n:at[0]]

        ssum, root, rstd = carve(10), carve(10), carve(10)
        smax, snegm, ssm, srec = carve(8), carve(8), carve(8), carve(8)
        lam_mag, lam_y, lam_s, lam_z, lam_p, lam_c = (carve(KT) for _ in range(6))
        logit, pick, rankp, term = (carve(TT * EXPERTS).rearrange("p (t e) -> p t e", e=EXPERTS) for _ in range(4))
        rank_or_no, gmat = (carve(TT * (EXPERTS + 2)).rearrange("p (t e) -> p t e", e=EXPERTS + 2) for _ in range(2))
        top8, idxf = carve(8 * TT), carve(8 * TT)
        gates, gsum, grec, negtop = carve(TOPK * TT), carve(TT), carve(TT), carve(TT)
        cntmax, nround = carve(1), carve(1)
        idx8 = sb("idx8", [P, 8 * TT], U32)
        pick16 = sb("pick16", [P, TT, EXPERTS], BF16)
        mat16 = sb("mat16", [P, 2, P], BF16)
        nround_i = sb("nround_i", [P, 1], I32)
        gT = sb("gT", [EXPERTS, T])

        loaded = [sem(f"loaded{i}") for i in range(RAW)]
        names = """in_x in_cst in_bgu in_router in_fin
            dense_hi_ready dense_lo_ready hi_done lo_done
            chunk_used unit_done freed_dve freed_act squared rooted normed dve_seq act_seq
            lam_abs lam_exp pads_zero xr_done pool_done decay_done inner_done mult_done scan_done
            gelu_arg gelu_sig yb_done m_done lam_done rowmax prob_done part_hi part_rest
            gate_in gate_exp picked gmat_done gT_turned gT_out bd_done bd_added route_done grec_done pool_seq
            onehot_ready sel_done x_ready xhi_ready xlo_ready whi_ready wlo_ready low_cols_ready gated_out turned
            gate_biased up_biased gate_ready up_ready lin_ready sig_ready h_ready hhi_ready hlo_ready
            y_ready wone_ready wone_turned wturned_ready out_first out_done added fin_sq fin_root result
            written""".split()
        S = {n: sem(n) for n in names}
        in_mem = [sem(f"in_mem{t}") for t in range(TT)]
        freed = {"dve": S["freed_dve"], "act": S["freed_act"], "lo": S["lo_done"]}

        block = ctx.enter_context(nc.Block())

        PER_ROUND = PER_EXPERT * EXPERTS

        def number(r, e, i):
            return r * PER_ROUND + e * PER_EXPERT + (CHUNKS_0 - DN_CHUNKS + i)

        def place(i):
            return NDENSE - DN_CHUNKS + i

        def fills(r, e, i):
            return r * (PER_ROUND // RAW) + e * (PER_EXPERT // RAW) + (place(i) // RAW + 1)

        def needed_rounds(eng):
            eng.wait_ge(S["route_done"], 1)
            return eng.value_load(nround_i[0:1, 0:1], min_val=1, max_val=ROUNDS)

        @block.sync
        def _(sp):
            for t in range(TT):
                sp.dma_start(mem_rows[:, t, :], mem[t * P:(t + 1) * P, :]).then_inc(in_mem[t], 16)

            def slot_free(n):
                if n in SPLIT_CHUNKS:
                    sp.wait_ge(S["dense_lo_ready"], SPLIT_CHUNKS.index(n) + 1)
                else:
                    sp.wait_ge(S[USED[n][0]], USED[n][1])

            for n in range(NDENSE):
                if n >= RAW:
                    slot_free(n - RAW)
                sp.dma_start(raw[:, n % RAW, :], dense[n]).then_inc(loaded[n % RAW], 16)
                if n == 1:
                    sp.dma_start(res[:], x.rearrange("(t p) d -> p t d", p=P)).then_inc(S["in_x"], 16)

            def split_before(count):
                sp.wait_ge(S["wlo_ready"], count)
                sp.wait_ge(S["low_cols_ready"], count)

            def gate_up_chunk(r, e, i, k):
                split_before(number(r, e, i) - (CHUNKS_0 + RAW - 1))
                sp.dma_start(raw[:, place(i) % RAW, :], w_gate_up[bass.ds(e * D + k * P, P), :])\
                    .then_inc(loaded[place(i) % RAW], 16)

            def down_chunk(r, e, i, k):
                split_before(number(r, e, i) - (CHUNKS_0 + RAW - 1))
                rows2 = w_down[bass.ds((e - 1) * D + k * 2 * P, 2 * P), :]
                sp.dma_start(raw[:, place(i) % RAW, :].rearrange("p (f d) -> p f d", d=D),
                             rows2.rearrange("(f p) d -> p f d", p=P)).then_inc(loaded[place(i) % RAW], 16)

            for k in range(RAW):
                slot_free(NDENSE - RAW + k)
                sp.dma_start(raw[:, (NDENSE + k) % RAW, :], w_gate_up[k * P:(k + 1) * P, :])\
                    .then_inc(loaded[(NDENSE + k) % RAW], 16)
            sp.wait_ge(S["part_rest"], 2)
            sp.wait_ge(S["unit_done"], UNIT["xnT"] + 4)
            sp.dma_start(fin_g, norm_final).then_inc(S["in_fin"], 16)
            n = needed_rounds(sp)
            with sp.Fori(0, n) as r:
                for k in range(RAW, GU_CHUNKS):
                    gate_up_chunk(r, 0, DN_CHUNKS + k, k)
                with sp.Fori(1, EXPERTS) as e:
                    for k in range(GU_CHUNKS):
                        gate_up_chunk(r, e, k, k)
                    for k in range(DN_CHUNKS):
                        down_chunk(r, e, GU_CHUNKS + k, k)
                for k in range(DN_CHUNKS):
                    down_chunk(r, EXPERTS, k, k)
                with sp.If(r + 1 < n):
                    for k in range(RAW):
                        gate_up_chunk(r + 1, 0, DN_CHUNKS + k, k)
            for t in range(TT):
                sp.wait_ge(S["result"], t + 1)
                sp.dma_start(out[t * P:(t + 1) * P, :], res[:, t, :]).then_inc(S["written"], 16)
            sp.wait_ge(S["written"], 16 * TT)

        @block.gpsimd
        def _(pool):
            pool.dma_start(bgu_sb[:], bgu).then_inc(S["in_bgu"], 16)
            for m, n in enumerate(SPLIT_CHUNKS):
                if m == 0:
                    continue
                if m == 1:
                    pool.wait_ge(S["dense_lo_ready"], 1)
                pool.wait_ge(S["dense_hi_ready"], m + 1)
                nc.gpsimd.tensor_tensor(wlo[:, m % SPL, :], raw[:, n % RAW, :],
                                        whi[:, m % SPL, :].bitcast(F32), ALU.subtract)\
                    .then_inc(S["dense_lo_ready"], 1)
            pool.wait_ge(S["yb_done"], 1)
            pool.dma_start(router_w, w_router.rearrange("(k p) e -> p k e", p=P)).then_inc(S["in_router"], 16)
            pool.dma_start(router_b, b_router).then_inc(S["in_router"], 16)
            pool.dma_start(bdown_sb, b_down).then_inc(S["in_router"], 16)
            pool.wait_ge(S["part_hi"], 2)
            nc.gpsimd.tensor_tensor(rest_rows, rest_rows, xpart[1], ALU.subtract).then_inc(S["part_rest"], 1)

            seq = [0]

            def link(*instructions):
                for ins in instructions:
                    seq[0] += 1
                    ins.then_inc(S["pool_seq"], 1)
                pool.wait_ge(S["pool_seq"], seq[0])

            link(nc.gpsimd.memset(gmat, 0.0))
            pool.wait_ge(S["picked"], 1)
            pool.wait_ge(S["gate_exp"], TT)
            places = iota[:, 0:EXPERTS]
            mine = [gmat[:, t, 1:EXPERTS + 1] for t in range(TT)]
            for j in range(TOPK):
                link(*[nc.gpsimd.tensor_scalar(mine[t] if j == 0 else term[:, t, :], places,
                                               idxf[:, 8 * t + j:8 * t + j + 1],
                                               gates[:, TOPK * t + j:TOPK * t + j + 1], ALU.is_equal, ALU.mult)
                       for t in range(TT)])
                if j:
                    link(*[nc.gpsimd.tensor_tensor(mine[t], mine[t], term[:, t, :], ALU.add) for t in range(TT)])
            pool.wait_ge(S["grec_done"], 1)
            for t in range(TT):
                nc.gpsimd.tensor_scalar(mine[t], mine[t], grec[:, t:t + 1], None, ALU.mult)\
                    .then_inc(S["gmat_done"], 1)

            n = needed_rounds(pool)
            with pool.Fori(0, n) as r:
                with pool.Fori(0, EXPERTS) as e:
                    for q in range(PER_EXPERT):
                        i = DN_CHUNKS + q
                        pool.wait_ge(S["whi_ready"], number(r, e, i) - (CHUNKS_0 - 1))
                        nc.gpsimd.tensor_tensor(wlo[:, place(i) % SPL, DVE_COLS:],
                                                raw[:, place(i) % RAW, DVE_COLS:],
                                                whi[:, place(i) % SPL, DVE_COLS:].bitcast(F32), ALU.subtract)\
                            .then_inc(S["low_cols_ready"], 1)

        @block.scalar
        def _(act):
            act.dma_start(cst[:], consts).then_inc(S["in_cst"], 16)
            act.dma_start(col[:], cols).then_inc(S["in_cst"], 16)

            def squares(n, src, junk, there):
                act.preload_act_table(ACT.Sqrt)
                for t in range(TT):
                    act.wait_ge(*there(t))
                    i = 2 * n + t
                    nc.scalar.activation(junk[:, t, :], src[:, t, :], ACT.Square, accum_out=ssum[:, i:i + 1])\
                        .then_inc(S["squared"], 1)
                    act.wait_ge(S["squared"], i + 1)
                    nc.scalar.activation(root[:, i:i + 1], ssum[:, i:i + 1], ACT.Sqrt, scale=1.0 / D, bias=EPS)\
                        .then_inc(S["rooted"], 1)

            def units(name, n, fn):
                for j in range(n):
                    u = UNIT[name] + j
                    act.wait_ge(S["unit_done"], u + 1)
                    fn(j, ps[:, u % 8, :])

            two = lambda b: b.rearrange("p (k t) -> p k t", t=T)

            next_split = [0]

            def weights_after(name, j):
                while next_split[0] < len(SPLIT_CHUNKS):
                    m = next_split[0]
                    if m >= SPL:
                        if SPLIT_CHUNKS[m - SPL] > DENSE[name] + j:
                            break
                        who, count = USED[SPLIT_CHUNKS[m - SPL]]
                        act.wait_ge(S[who], count)
                    elif m > j + SPL:
                        break
                    n = SPLIT_CHUNKS[m]
                    act.wait_ge(loaded[n % RAW], 16 * (n // RAW + 1))
                    nc.scalar.activation(whi[:, m % SPL, :], raw[:, n % RAW, :], ACT.Copy)\
                        .then_inc(S["dense_hi_ready"], 1)
                    next_split[0] += 1

            def high_from_psum(name, gain):
                def fn(j, b):
                    for k in (2 * j, 2 * j + 1):
                        nc.scalar.activation(act_hi[:, k, :], b[:, (k % 2) * T:(k % 2 + 1) * T], ACT.Copy,
                                             scale=p_(gain, k) if gain else 1.0).then_inc(S["hi_done"], 1)
                units(name, 4, fn)

            def high_of(src, j):
                nc.scalar.activation(act_hi[:, 2 * j:2 * j + 2, :], src[:, 2 * j:2 * j + 2, :], ACT.Copy)\
                    .then_inc(S["hi_done"], 2)

            def evacuate(name, j, fn):
                u = UNIT[name] + j
                act.wait_ge(S["unit_done"], u + 1)
                fn(j, ps[:, u % 8, :])

            squares(0, mem_rows, rows(s9), lambda t: (in_mem[t], 16))
            weights_after("k", -3)
            act.wait_ge(S["in_cst"], 32)
            high_from_psum("memT", "norm_mem")
            weights_after("k", 0)
            squares(1, res, xs_rows, lambda t: (S["in_x"], 16))
            act.wait_ge(S["lam_abs"], 1)
            nc.scalar.activation(lam_y, lam_mag, ACT.Exp, scale=-1.0).then_inc(S["lam_exp"], 1)
            weights_after("k", 3)
            weights_after("v", 2)
            units("v", 4, lambda j, b: nc.scalar.activation(
                v_rows[:, j // 2, (j % 2) * BANK:(j % 2 + 1) * BANK], b, ACT.Copy).then_inc(S["freed_act"], 1))
            high_from_psum("xT", "norm_mix")
            weights_after("v", 3)
            weights_after("lrux", 3)
            act.wait_ge(S["pads_zero"], 1)
            for j in range(4):
                evacuate("pool", j, lambda j, b: nc.scalar.activation(
                    u_pool[:, 2 * j:2 * j + 2, PAD:], two(b), ACT.Copy).then_inc(S["freed_act"], 1))
                weights_after("pool", j)

            def logistic_gate(dst, bias):
                def fn(j, b):
                    for k in (2 * j, 2 * j + 1):
                        ins = nc.scalar.activation(dst[:, k, :], b[:, (k % 2) * T:(k % 2 + 1) * T], ACT.Sigmoid,
                                                   bias=p_(bias, k))
                        ins.then_inc(S["freed_act"] if k % 2 else S["act_seq"], 1)
                return fn
            units("ra", 4, logistic_gate(r_f, "lru_b_a"))
            act.wait_ge(S["pool_done"], 1)
            units("rx", 4, logistic_gate(i_f, "lru_b_x"))
            act.wait_ge(S["freed_act"], evacuated(UNIT["ra"] + 3)[1])
            act.wait_ge(S["act_seq"], 8)
            act.wait_ge(S["lam_done"], 1)
            for k in range(KT):
                nc.scalar.activation(a_f[:, k, :], r_f[:, k, :], ACT.Exp, scale=lam_c[:, k:k + 1])\
                    .then_inc(S["decay_done"], 1)
                nc.scalar.activation(b_f[:, k, :], r_f[:, k, :], ACT.Tanh, scale=lam_c[:, k:k + 1])\
                    .then_inc(S["decay_done"], 1)
            for j in range(4):
                evacuate("gelu", j, lambda j, b: nc.scalar.activation(
                    gelu_f[:, 2 * j:2 * j + 2, :], two(b), ACT.Copy).then_inc(S["freed_act"], 1))
                weights_after("gelu", j)
                if j == 1:
                    act.wait_ge(S["inner_done"], 1)
                    nc.scalar.activation(b_f, b_f, ACT.Sqrt, scale=-1.0).then_inc(S["mult_done"], 1)
            act.wait_ge(S["scan_done"], KT)
            for j in range(4):
                evacuate("ga", j, lambda j, b: nc.scalar.activation(
                    siga_f[:, 2 * j:2 * j + 2, :], two(b), ACT.Sigmoid).then_inc(S["freed_act"], 1))
                weights_after("ga", j)
                if j == 1:
                    act.wait_ge(S["gelu_arg"], 1)
                    nc.scalar.activation(gtmp_f, gtmp_f, ACT.Sigmoid, scale=2.0 * 0.7978845608028654)\
                        .then_inc(S["gelu_sig"], 1)
            act.wait_ge(S["freed_dve"], evacuated(UNIT["grp"] + 3)[1])
            for j in range(4):
                if j == 3:
                    act.wait_ge(S["unit_done"], UNIT["gb"] + 4)
                    for i in range(4):
                        high_of(pool_f, i)
                evacuate("gb", j, lambda j, b: nc.scalar.activation(
                    sigb_f[:, 2 * j:2 * j + 2, :], two(b), ACT.Sigmoid).then_inc(S["freed_act"], 1))
                weights_after("gb", j)
            weights_after("pp", 2)
            act.wait_ge(S["yb_done"], 1)
            act.wait_ge(S["unit_done"], UNIT["pp"] + 4)
            for j in range(4):
                high_of(hs_f, j)
            weights_after("pp", 3)
            weights_after("lp", 2)
            act.wait_ge(S["unit_done"], UNIT["lp"] + 4)
            for j in range(4):
                act.wait_ge(S["m_done"], j + 1)
                high_of(m_f, j)
            weights_after("lp", 3)
            weights_after("mix", 2)
            squares(2, res, xn_rows, lambda t: (S["freed_dve"], evacuated(UNIT["mix"] + 2 * t + 1)[1]))
            weights_after("mix", 3)
            high_from_psum("x1T", "norm_xattn")
            weights_after("q", 3)

            def exps(j, b):
                act.wait_ge(S["rowmax"], j + 1)
                for q in range(TT):
                    ins = nc.scalar.activation(prob[:, j, q, :], b[:, q * T:(q + 1) * T], ACT.Exp, scale=HD ** -0.5,
                                               bias=snegm[:, 2 * j + q:2 * j + q + 1],
                                               accum_out=ssm[:, 2 * j + q:2 * j + q + 1])
                    ins.then_inc(S["freed_act"] if q else S["act_seq"], 1)
            units("score", 4, exps)
            units("pT", 4, lambda j, b: nc.scalar.activation(
                probT[:, j, :, :], b.rearrange("p (m q) -> p m q", q=T), ACT.Copy).then_inc(S["freed_act"], 1))
            high_from_psum("oT", None)
            weights_after("o", 3)
            squares(3, res, xn_rows, lambda t: (S["freed_dve"], evacuated(UNIT["o"] + 2 * t + 1)[1]))

            def gained(j, b):
                for k in (2 * j, 2 * j + 1):
                    nc.scalar.activation(xn_f[:, k, :], b[:, (k % 2) * T:(k % 2 + 1) * T], ACT.Copy,
                                         scale=p_("norm_moe", k)).then_inc(S["freed_act" if k % 2 else "act_seq"], 1)
            evacuate("xnT", 1, gained)
            evacuate("xnT", 3, gained)
            act.wait_ge(S["normed"], 8)
            nc.scalar.activation(xpart[0], xn_rows, ACT.Copy).then_inc(S["part_hi"], 1)
            act.wait_ge(S["part_rest"], 1)
            nc.scalar.activation(xpart[1], rest_rows, ACT.Copy).then_inc(S["part_hi"], 1)
            act.wait_ge(S["gate_in"], 1)
            for t in range(TT):
                nc.scalar.activation(gates[:, TOPK * t:TOPK * (t + 1)], top8[:, 8 * t:8 * t + TOPK], ACT.Exp,
                                     bias=negtop[:, t:t + 1], accum_out=gsum[:, t:t + 1]).then_inc(S["gate_exp"], 1)
            act.wait_ge(S["part_rest"], 2)
            nc.scalar.activation(xpart[2], rest_rows, ACT.Copy).then_inc(S["part_hi"], 1)
            act.preload_act_table(ACT.Sigmoid)

            def split(r, e, i):
                act.wait_ge(loaded[place(i) % RAW], fills(r, e, i) * 16)
                act.wait_ge(S["chunk_used"], number(r, e, i) - (SPL - 1))
                nc.scalar.activation(whi[:, place(i) % SPL, :], raw[:, place(i) % RAW, :], ACT.Copy)\
                    .then_inc(S["whi_ready"], 1)

            def x_high(r, e):
                act.wait_ge(S["x_ready"], r * BLOCKS + e + 1)
                nc.scalar.activation(xpair[:, :, 0:SLOTS], x32, ACT.Copy).then_inc(S["xhi_ready"], 1)

            def rows_out(r, e, i):
                act.wait_ge(S["chunk_used"], number(r, e, i))
                for b in range(4):
                    nc.scalar.activation(gated[:, b * BANK:(b + 1) * BANK], ps[:, b, :], ACT.Copy)\
                        .then_inc(S["gated_out"], 1)

            def rows_copied(r, e, chunks=PER_EXPERT):
                act.wait_ge(S["chunk_used"], number(r, e - 1, chunks))
                act.wait_ge(S["out_done"], r * BLOCKS + e)
                nc.scalar.activation(y_rows, ps[:, 4:6, :].rearrange("p b n -> p (b n)"), ACT.Copy)\
                    .then_inc(S["y_ready"], 1)

            def gate_sigmoid(count):
                act.wait_ge(S["gate_ready"], count)
                nc.scalar.activation(sig, gate, ACT.Sigmoid, scale=ALPHA).then_inc(S["sig_ready"], 1)

            def h_high(count):
                act.wait_ge(S["h_ready"], count)
                nc.scalar.activation(hpair[:, :, 0:SLOTS], h32, ACT.Copy).then_inc(S["hhi_ready"], 1)

            act.sem_inc(S["gated_out"], 4)
            n = needed_rounds(act)
            with act.Fori(0, n) as r:
                for i in range(DN_CHUNKS, PER_EXPERT):
                    if i == DN_CHUNKS + 2:
                        x_high(r, 0)
                    split(r, 0, i)
                rows_out(r, 0, PER_EXPERT)
                x_high(r, 1)
                with act.Fori(1, EXPERTS) as e:
                    done = r * EXPERTS + e
                    for i in range(PER_EXPERT):
                        if i == 2:
                            rows_copied(r, e)
                        if i == 5:
                            gate_sigmoid(done)
                        if i == 6:
                            h_high(done)
                        if i == 10:
                            rows_out(r, e, GU_CHUNKS)
                        if i == 11:
                            x_high(r, e + 1)
                        split(r, e, i)
                for i in range(DN_CHUNKS):
                    split(r, EXPERTS, i)
                    if i == 0:
                        gate_sigmoid((r + 1) * EXPERTS)
                        rows_copied(r, EXPERTS)
                        h_high((r + 1) * EXPERTS)
                rows_copied(r, EXPERTS + 1, DN_CHUNKS)
            act.preload_act_table(ACT.Sqrt)
            for t in range(TT):
                act.wait_ge(S["added"], n * (2 * BLOCKS) + (1 + 2 + t - TT))
                nc.scalar.activation(rest_rows[:, t, :], res[:, t, :], ACT.Square,
                                     accum_out=ssum[:, 8 + t:9 + t]).then_inc(S["fin_sq"], 1)
                act.wait_ge(S["fin_sq"], t + 1)
                nc.scalar.activation(root[:, 8 + t:9 + t], ssum[:, 8 + t:9 + t], ACT.Sqrt, scale=1.0 / D,
                                     bias=EPS).then_inc(S["fin_root"], 1)

        @block.vector
        def _(dve):
            V = nc.vector
            seq = [0]

            def link(*instructions):
                for ins in instructions:
                    seq[0] += 1
                    ins.then_inc(S["dve_seq"], 1)
                dve.wait_ge(S["dve_seq"], seq[0])

            def evacuate(name, j, fn):
                u = UNIT[name] + j
                dve.wait_ge(S["unit_done"], u + 1)
                fn(j, ps[:, u % 8, :])

            def units(name, n, fn):
                for j in range(n):
                    evacuate(name, j, fn)

            two = lambda b: b.rearrange("p (k t) -> p k t", t=T)

            def normalise(n, src, dst):
                for t in range(TT):
                    i = 2 * n + t
                    dve.wait_ge(S["rooted"], i + 1)
                    link(V.reciprocal(rstd[:, i:i + 1], root[:, i:i + 1]))
                    V.tensor_scalar(dst[:, t, :], src[:, t, :], rstd[:, i:i + 1], None, ALU.mult)\
                        .then_inc(S["normed"], 1)

            def gained(dst, gain):
                def fn(j, b):
                    V.tensor_scalar(dst[:, 2 * j, :], b[:, 0:T], p_(gain, 2 * j), None, ALU.mult)\
                        .then_inc(S["dve_seq"], 1)
                    seq[0] += 1
                    V.tensor_scalar(dst[:, 2 * j + 1, :], b[:, T:2 * T], p_(gain, 2 * j + 1), None, ALU.mult)\
                        .then_inc(S["freed_dve"], 1)
                return fn

            def copied(dst):
                return lambda j, b: V.tensor_copy(dst[:, 2 * j:2 * j + 2, :], two(b)).then_inc(S["freed_dve"], 1)

            def low_from_psum(name, operand, gain):
                def fn(j, b):
                    dve.wait_ge(S["hi_done"], split_tiles(operand, 2 * j + 1))
                    for k in (2 * j, 2 * j + 1):
                        V.scalar_tensor_tensor(act_lo[:, k, :], b[:, (k % 2) * T:(k % 2 + 1) * T],
                                               p_(gain, k) if gain else 1.0, act_hi[:, k, :].bitcast(F32), ALU.mult,
                                               ALU.subtract).then_inc(S["lo_done"], 1)
                units(name, 4, fn)

            def low_of(src, operand, j):
                dve.wait_ge(S["hi_done"], split_tiles(operand, 2 * j + 1))
                V.tensor_tensor(act_lo[:, 2 * j:2 * j + 2, :], src[:, 2 * j:2 * j + 2, :],
                                act_hi[:, 2 * j:2 * j + 2, :].bitcast(F32), ALU.subtract).then_inc(S["lo_done"], 2)

            dve.wait_ge(S["in_cst"], 32)
            lam0 = col[:, COL["lru_lambda"]:COL["lru_lambda"] + KT]
            link(V.scalar_tensor_tensor(lam_mag, lam0, -1.0, lam0, ALU.mult, ALU.max))
            dve.sem_inc(S["lam_abs"], 1)
            V.memset(u_pool[:, :, 0:PAD], 0.0).then_inc(S["pads_zero"], 1)
            V.tensor_copy(mat16[:, :, :], cst[:, CONST["before"][0]:CONST["ones"][1]].rearrange(
                "p (a b) -> p a b", a=2)).then_inc(S["dve_seq"], 1)
            seq[0] += 1
            normalise(0, mem_rows, mem_rows)
            dve.wait_ge(S["dense_hi_ready"], 1)
            V.tensor_tensor(wlo[:, 0, :], raw[:, 0, :], whi[:, 0, :].bitcast(F32), ALU.subtract)\
                .then_inc(S["dense_lo_ready"], 1)
            low_from_psum("memT", "mem", "norm_mem")
            normalise(1, res, xs_rows)
            dve.wait_ge(S["lam_exp"], 1)
            link(V.tensor_scalar(lam_s, lam_y, 2.0, None, ALU.add))
            link(V.reciprocal(lam_s, lam_s))
            link(V.tensor_tensor(lam_s, lam_s, lam_y, ALU.mult))
            link(V.tensor_tensor(lam_z, lam_s, lam_s, ALU.mult))
            link(V.tensor_scalar(lam_p, lam_z, 1.0 / 19, None, ALU.mult))
            for odd in range(17, 1, -2):
                link(V.scalar_tensor_tensor(lam_p, lam_p, 1.0 / odd, lam_z, ALU.add, ALU.mult))
            link(V.scalar_tensor_tensor(lam_p, lam_p, 1.0, lam_s, ALU.add, ALU.mult))
            link(V.tensor_scalar(lam_z, lam0, 0.0, 8.0, ALU.min, ALU.mult))
            link(V.scalar_tensor_tensor(lam_c, lam_p, -16.0, lam_z, ALU.mult, ALU.add))
            dve.sem_inc(S["lam_done"], 1)
            units("k", 4, copied(k_f))
            low_from_psum("xT", "h", "norm_mix")
            link(V.memset(u_lru[:, :, 0:PAD], 0.0))
            units("lrux", 4, lambda j, b: V.tensor_copy(
                u_lru[:, 2 * j:2 * j + 2, PAD:], two(b)).then_inc(S["freed_dve"], 1))
            dve.wait_ge(S["freed_dve"], evacuated(UNIT["lrux"] + 3)[1])
            for tap in range(CONV):
                shift = PAD - (CONV - 1) + tap
                for k in range(KT):
                    w = col[:, COL["conv_w"] + KT * tap + k:COL["conv_w"] + KT * tap + k + 1]
                    if tap == 0:
                        ins = V.tensor_scalar(xr_f[:, k, :], u_lru[:, k, shift:shift + T], w, p_("conv_b", k),
                                              ALU.mult, ALU.add)
                    else:
                        ins = V.scalar_tensor_tensor(xr_f[:, k, :], u_lru[:, k, shift:shift + T], w, xr_f[:, k, :],
                                                     ALU.mult, ALU.add)
                    if tap == CONV - 1:
                        ins.then_inc(S["xr_done"], 1)
                    else:
                        ins.then_inc(S["dve_seq"], 1)
                        seq[0] += 1
                if tap < CONV - 1:
                    dve.wait_ge(S["dve_seq"], seq[0])
            dve.wait_ge(S["xr_done"], KT)
            dve.wait_ge(S["freed_act"], evacuated(UNIT["pool"] + 3)[1])
            end = PAD + T
            link(V.tensor_tensor(win_a[:, 0:8, 2:end], u_pool[:, 0:8, 2:end], u_pool[:, 0:8, 1:end - 1], ALU.add))
            link(V.tensor_tensor(win_b[:, 2:8, 4:end], win_a[:, 2:8, 4:end], win_a[:, 2:8, 2:end - 2], ALU.add))
            link(V.tensor_tensor(win_a[:, 4:8, 8:end], win_b[:, 4:8, 8:end], win_b[:, 4:8, 4:end - 4], ALU.add))
            link(V.tensor_tensor(win_b[:, 6:8, 16:end], win_a[:, 6:8, 16:end], win_a[:, 6:8, 8:end - 8], ALU.add))
            for g, w in enumerate(WINDOWS):
                src = (win_a, win_b)[g % 2]
                early = src[:, 2 * g:2 * g + 2, PAD:2 * PAD]
                inv = c_("inv")[:, PAD * g:PAD * (g + 1)].unsqueeze(1).broadcast_to([P, 2, PAD])
                link(V.tensor_tensor(early, early, inv, ALU.mult))
                link(V.scalar_tensor_tensor(pool_f[:, 2 * g:2 * g + 2, :], src[:, 2 * g:2 * g + 2, PAD:], 1.0 / w,
                                            u_pool[:, 2 * g:2 * g + 2, PAD:], ALU.mult, ALU.subtract))
            dve.sem_inc(S["pool_done"], 1)

            def scaled(j, b):
                for k in (2 * j, 2 * j + 1):
                    V.tensor_scalar(pool_f[:, k, :], b[:, (k % 2) * T:(k % 2 + 1) * T], p_("pool_scale", k), None,
                                    ALU.mult).then_inc(S["freed_dve"] if k % 2 else S["dve_seq"], 1)
                seq[0] += 1
            units("grp", 4, scaled)

            dve.wait_ge(S["decay_done"], 2 * KT)
            link(V.tensor_tensor(r_f, a_f, a_f, ALU.mult))
            link(V.scalar_tensor_tensor(b_f, r_f, 1.0, b_f, ALU.add, ALU.mult))
            V.tensor_scalar(b_f, b_f, 0.0, None, ALU.min).then_inc(S["inner_done"], 1)
            dve.wait_ge(S["freed_act"], evacuated(UNIT["rx"] + 3)[1])
            dve.wait_ge(S["mult_done"], 1)
            link(V.memset(b_f[:, :, 0:1], 1.0))
            link(V.tensor_tensor(b_f, b_f, i_f, ALU.mult))
            link(V.tensor_tensor(b_f, b_f, xr_f, ALU.mult))
            for k in range(KT):
                V.tensor_tensor_scan(hs_f[:, k, :], a_f[:, k, :], b_f[:, k, :], 0.0, ALU.mult, ALU.add)\
                    .then_inc(S["scan_done"], 1)
            dve.wait_ge(S["freed_act"], evacuated(UNIT["gelu"] + 3)[1])
            link(V.tensor_tensor(gtmp_f, gelu_f, gelu_f, ALU.mult))
            link(V.tensor_scalar(gtmp_f, gtmp_f, 0.044715, 1.0, ALU.mult, ALU.add))
            V.tensor_tensor(gtmp_f, gtmp_f, gelu_f, ALU.mult).then_inc(S["gelu_arg"], 1)
            dve.wait_ge(S["scan_done"], KT)
            link(V.tensor_tensor(hs_f, hs_f, gelu_f, ALU.mult))
            dve.wait_ge(S["gelu_sig"], 1)
            V.tensor_tensor(hs_f, hs_f, gtmp_f, ALU.mult).then_inc(S["yb_done"], 1)
            for j in range(4):
                low_of(pool_f, "pool", j)
            dve.wait_ge(S["freed_act"], evacuated(UNIT["gb"] + 3)[1])
            units("pp", 4, lambda j, b: V.tensor_tensor(
                m_f[:, 2 * j:2 * j + 2, :], siga_f[:, 2 * j:2 * j + 2, :], two(b), ALU.mult)
                .then_inc(S["freed_dve"], 1))

            for j in range(4):
                low_of(hs_f, "lru", j)

            def merge(j, b):
                t2 = sigb_f[:, 2 * j:2 * j + 2, :]
                V.tensor_tensor(t2, t2, two(b), ALU.mult).then_inc(S["freed_dve"], 1)
                dve.wait_ge(S["freed_dve"], evacuated(UNIT["lp"] + j)[1])
                V.tensor_tensor(m_f[:, 2 * j:2 * j + 2, :], m_f[:, 2 * j:2 * j + 2, :], t2, ALU.add)\
                    .then_inc(S["m_done"], 1)
            units("lp", 4, merge)
            for j in range(4):
                low_of(m_f, "merged", j)

            def onto_residual(j, b):
                part = res[:, j // 2, (j % 2) * BANK:(j % 2 + 1) * BANK]
                V.tensor_tensor(part, part, b, ALU.add).then_inc(S["freed_dve"], 1)
            units("mix", 4, onto_residual)
            normalise(2, res, xn_rows)
            low_from_psum("x1T", "xn", "norm_xattn")
            units("q", 4, copied(q_f))

            def maxima(j, b):
                link(V.tensor_reduce(smax[:, 2 * j:2 * j + 2], two(b), AX.X, ALU.max))
                V.tensor_scalar(snegm[:, 2 * j:2 * j + 2], smax[:, 2 * j:2 * j + 2], -(HD ** -0.5), None, ALU.mult)\
                    .then_inc(S["rowmax"], 1)
            units("score", 4, maxima)
            for j in range(HEADS):
                dve.wait_ge(S["freed_act"], evacuated(UNIT["score"] + j)[1])
                dve.wait_ge(S["act_seq"], 8 + j + 1)
                link(V.reciprocal(srec[:, 2 * j:2 * j + 2], ssm[:, 2 * j:2 * j + 2]))
                for q in range(TT):
                    V.tensor_scalar(prob[:, j, q, :], prob[:, j, q, :], srec[:, 2 * j + q:2 * j + q + 1], None,
                                    ALU.mult).then_inc(S["prob_done"], 1)
            low_from_psum("oT", "attn", None)
            units("o", 4, onto_residual)
            normalise(3, res, xn_rows)
            evacuate("xnT", 0, gained(xn_f, "norm_moe"))
            evacuate("xnT", 2, gained(xn_f, "norm_moe"))

            dve.wait_ge(S["part_hi"], 1)
            V.tensor_tensor(rest_rows, xn_rows, xpart[0], ALU.subtract).then_inc(S["part_rest"], 1)

            dve.wait_ge(S["in_router"], 48)
            u = UNIT["logit"]
            dve.wait_ge(S["unit_done"], u + 1)
            bias = router_b.unsqueeze(1).broadcast_to([P, TT, EXPERTS])
            V.tensor_tensor(logit, ps[:, u % 8, 0:TT * EXPERTS].rearrange("p (t e) -> p t e", e=EXPERTS), bias,
                            ALU.add)\
                .then_inc(S["freed_dve"], 1)
            dve.wait_ge(S["freed_dve"], evacuated(u)[1])
            tops = lambda v, t, j: v[:, 8 * t + j:8 * t + j + 1]
            both = range(TT)
            link(*[V.max(top8[:, 8 * t:8 * t + 8], logit[:, t, :]) for t in both])
            link(*[V.max_index(idx8[:, 8 * t:8 * t + 8], top8[:, 8 * t:8 * t + 8], logit[:, t, :]) for t in both])
            link(V.tensor_copy(idxf, idx8[:]))
            places = iota[:, 0:EXPERTS]
            link(*[V.tensor_scalar(pick[:, t, :], places, tops(idxf, t, 0), None, ALU.is_equal) for t in both])
            for j in range(1, TOPK):
                link(*[V.scalar_tensor_tensor(pick[:, t, :], places, tops(idxf, t, j), pick[:, t, :], ALU.is_equal,
                                              ALU.add) for t in both])
            V.tensor_copy(pick16[:], pick).then_inc(S["picked"], 1)
            link(*[V.tensor_scalar(negtop[:, t:t + 1], tops(top8, t, 0), -1.0, None, ALU.mult) for t in both])
            dve.sem_inc(S["gate_in"], 1)
            link(V.memset(rank_or_no, 0.0))
            u = UNIT["rank"]
            dve.wait_ge(S["unit_done"], u + 1)
            got = ps[:, u % 8, 0:3 * EXPERTS].rearrange("p (t e) -> p t e", e=EXPERTS)
            V.tensor_copy(rankp, got[:, 0:TT, :]).then_inc(S["dve_seq"], 1)
            seq[0] += 1
            V.tensor_reduce(cntmax, got[:, TT, :], AX.X, ALU.max).then_inc(S["freed_dve"], 1)
            dve.wait_ge(S["freed_dve"], evacuated(u)[1])
            dve.wait_ge(S["dve_seq"], seq[0])
            link(V.tensor_scalar(nround, cntmax, float(SLOTS), 1.0, ALU.is_gt, ALU.add),
                 V.scalar_tensor_tensor(rank_or_no[:, :, 1:EXPERTS + 1], rankp, 1.0, pick, ALU.add, ALU.mult))
            link(V.scalar_tensor_tensor(nround, cntmax, float(SLOTS * 2), nround, ALU.is_gt, ALU.add),
                 V.tensor_scalar(rank_or_no, rank_or_no, -1.0, None, ALU.add))
            for n in range(3, ROUNDS):
                link(V.scalar_tensor_tensor(nround, cntmax, float(SLOTS * n), nround, ALU.is_gt, ALU.add))
            link(V.tensor_copy(nround_i[:], nround))
            dve.sem_inc(S["route_done"], 1)
            dve.wait_ge(S["gate_exp"], TT)
            link(V.reciprocal(grec, gsum))
            dve.sem_inc(S["grec_done"], 1)

            def split(r, e, i):
                dve.wait_ge(S["whi_ready"], number(r, e, i) - (CHUNKS_0 - 1))
                V.tensor_tensor(wlo[:, place(i) % SPL, 0:DVE_COLS], raw[:, place(i) % RAW, 0:DVE_COLS],
                                whi[:, place(i) % SPL, 0:DVE_COLS].bitcast(F32), ALU.subtract)\
                    .then_inc(S["wlo_ready"], 1)

            def select(r, e):
                for t in range(TT):
                    V.tensor_scalar(onehot[:, t, :], iota[:, bass.ds(r * SLOTS, SLOTS)],
                                    rank_or_no[:, t, bass.ds(e + 1, 1)], None, ALU.is_equal)\
                        .then_inc(S["onehot_ready"], 1)

            gain = col[:, COL["norm_moe"]:COL["norm_moe"] + KT].unsqueeze(2).broadcast_to([P, KT, SLOTS])

            def x_whole(r, e):
                dve.wait_ge(S["sel_done"], r * BLOCKS + e + 1)
                V.tensor_tensor(x32, ps[:, 6, :].rearrange("p (k c) -> p k c", c=SLOTS), gain,
                                ALU.mult).then_inc(S["x_ready"], 1)

            def x_low(r, e):
                dve.wait_ge(S["xhi_ready"], r * BLOCKS + e + 1)
                V.tensor_tensor(xpair[:, :, SLOTS:], x32, xpair[:, :, 0:SLOTS].bitcast(F32),
                                ALU.subtract).then_inc(S["xlo_ready"], 1)

            dve.wait_ge(S["in_bgu"], 16)

            def add_bias(r, e, count):
                dve.wait_ge(S["turned"], count)
                for n, (dst, name) in enumerate(((gate, "gate_biased"), (up, "up_biased"))):
                    b = bgu_sb[:, bass.ds(e, 1), KT * n:KT * (n + 1)].rearrange("p o k -> p (o k)").unsqueeze(2)
                    V.tensor_tensor(dst, ps[:, 6 + n, :].rearrange("p (k c) -> p k c", c=SLOTS),
                                    b.broadcast_to([P, KT, SLOTS]), ALU.add).then_inc(S[name], 1)
                dve.wait_ge(S["gate_biased"], count)
                V.tensor_scalar(gate, gate, LIMIT, None, ALU.min).then_inc(S["gate_ready"], 1)

            def swiglu(count):
                dve.wait_ge(S["up_biased"], count)
                V.tensor_scalar(up, up, LIMIT, -LIMIT, ALU.min, ALU.max).then_inc(S["up_ready"], 1)
                dve.wait_ge(S["up_ready"], count)
                dve.wait_ge(S["gate_ready"], count)
                V.scalar_tensor_tensor(lin, up, 1.0, gate, ALU.add, ALU.mult).then_inc(S["lin_ready"], 1)
                dve.wait_ge(S["lin_ready"], count)
                dve.wait_ge(S["sig_ready"], count)
                V.tensor_tensor(h32, sig, lin, ALU.mult).then_inc(S["h_ready"], 1)

            def h_low(count):
                dve.wait_ge(S["hhi_ready"], count)
                V.tensor_tensor(hpair[:, :, SLOTS:], h32, hpair[:, :, 0:SLOTS].bitcast(F32),
                                ALU.subtract).then_inc(S["hlo_ready"], 1)

            def weighted_onehot(r, e):
                dve.wait_ge(S["gmat_done"], TT)
                dve.wait_ge(S["wone_turned"], r * BLOCKS + e)
                for t in range(TT):
                    V.tensor_scalar(wone[:, t, :, :],
                                    iota[:, bass.ds(r * SLOTS, SLOTS)].unsqueeze(1).broadcast_to([P, 2, SLOTS]),
                                    rank_or_no[:, t, bass.ds(e - 1, 1)], gmat[:, t, bass.ds(e - 1, 1)], ALU.is_equal,
                                    ALU.mult).then_inc(S["wone_ready"], 1)

            def onehot_turned(r, e, bank=4):
                dve.wait_ge(S["wone_turned"], r * BLOCKS + e + 1)
                dve.wait_ge(S["out_done"], r * BLOCKS + e)
                V.tensor_copy(wturned, ps[:, bank, 0:TT * P].rearrange("p (t q) -> p t q", t=TT))\
                    .then_inc(S["wturned_ready"], 1)

            def add_rows(r, e, t, bank=4):
                dve.wait_ge(S["out_done"] if t else S["out_first"], r * BLOCKS + e + t)
                dve.wait_ge(S["added"], 2 * (r * BLOCKS + e) + t)
                V.tensor_tensor(res[:, t, :], res[:, t, :],
                                ps[:, bank + 2 * t:bank + 2 + 2 * t, :].rearrange("p b n -> p (b n)"), ALU.add)\
                    .then_inc(S["added"], 1)

            dve.sem_inc(S["wone_turned"], 1)
            dve.sem_inc(S["out_done"], 1)
            dve.sem_inc(S["added"], 2)
            n = needed_rounds(dve)
            with dve.Fori(0, n) as r:
                select(r, 0)
                for i in range(DN_CHUNKS, PER_EXPERT):
                    if i == DN_CHUNKS + 1:
                        x_whole(r, 0)
                        x_low(r, 0)
                        dve.wait_ge(S["sel_done"], r * BLOCKS + 1)
                        select(r, 1)
                    split(r, 0, i)
                dve.wait_ge(S["chunk_used"], number(r, 0, PER_EXPERT))
                x_whole(r, 1)
                x_low(r, 1)
                with dve.Fori(1, EXPERTS) as e:
                    done = r * EXPERTS + e
                    for i in range(PER_EXPERT):
                        if i == 1:
                            weighted_onehot(r, e)
                        if i == 3:
                            add_bias(r, e - 1, done)
                        if i == 4:
                            onehot_turned(r, e)
                        if i == 5:
                            swiglu(done)
                        if i == 6:
                            h_low(done)
                        if i == 7:
                            add_rows(r, e, 0)
                            dve.wait_ge(S["sel_done"], r * BLOCKS + e + 1)
                            select(r, e + 1)
                        if i == 9:
                            add_rows(r, e, 1)
                        if i == 10:
                            dve.wait_ge(S["chunk_used"], number(r, e, GU_CHUNKS))
                            x_whole(r, e + 1)
                        split(r, e, i)
                    x_low(r, e + 1)
                weighted_onehot(r, EXPERTS)
                add_bias(r, EXPERTS - 1, (r + 1) * EXPERTS)
                swiglu((r + 1) * EXPERTS)
                split(r, EXPERTS, 0)
                onehot_turned(r, EXPERTS, 2)
                h_low((r + 1) * EXPERTS)
                split(r, EXPERTS, 1)
                split(r, EXPERTS, 2)
                weighted_onehot(r, EXPERTS + 1)
                for t in range(TT):
                    add_rows(r, EXPERTS, t, 0)
                with dve.If(r < 1):
                    dve.wait_ge(S["gT_turned"], 1)
                    V.tensor_copy(gT[:], ps[0:EXPERTS, 7, 0:T]).then_inc(S["gT_out"], 1)
                split(r, EXPERTS, 3)
                onehot_turned(r, EXPERTS + 1, 0)
                with dve.If(r < 1):
                    for t, bank in enumerate((6, 2)):
                        dve.wait_ge(S["bd_done"], t + 1)
                        dve.wait_ge(S["added"], 2 * EXPERTS + 2)
                        V.tensor_tensor(res[:, t, :], res[:, t, :],
                                        ps[:, bank:bank + 2, :].rearrange("p b n -> p (b n)"), ALU.add)\
                            .then_inc(S["bd_added"], 1)
                dve.wait_ge(S["bd_added"], TT)
                for t in range(TT):
                    add_rows(r, EXPERTS + 1, t)
                dve.wait_ge(S["added"], 2 * (r + 1) * BLOCKS + 2)
            dve.wait_ge(S["in_fin"], 16)
            for t in range(TT):
                dve.wait_ge(S["fin_root"], t + 1)
                link(V.reciprocal(rstd[:, 8 + t:9 + t], root[:, 8 + t:9 + t]))
                V.scalar_tensor_tensor(res[:, t, :], res[:, t, :], rstd[:, 8 + t:9 + t], fin_g, ALU.mult, ALU.mult)\
                    .then_inc(S["result"], 1)

        @block.tensor
        def _(pe):
            def begin(u):
                if u >= 8:
                    eng, count = evacuated(u - 8)
                    pe.wait_ge(freed[eng], count)
                return ps[:, u % 8, :]

            def chunk(name, j):
                n = DENSE[name] + j
                pe.wait_ge(loaded[n % RAW], 16 * (n // RAW + 1))
                return raw[:, n % RAW, :]

            def transposed(name, src, n):
                banks = [begin(UNIT[name] + j) for j in range(KT // 2)]
                for t in range(TT):
                    pe.wait_ge(S["normed"], TT * n + t + 1)
                    for k in range(KT):
                        at = (k % 2) * T + t * P
                        last = nc.tensor.transpose(banks[k // 2][:, at:at + P], src[:, t, k * P:(k + 1) * P], ident)
                        if t == TT - 1 and k % 2:
                            last.then_inc(S["unit_done"], 1)

            def parts(name, j):
                m = SPLIT_CHUNKS.index(DENSE[name] + j)
                pe.wait_ge(S["dense_hi_ready"], m + 1)
                pe.wait_ge(S["dense_lo_ready"], m + 1)
                return whi[:, m % SPL, :], wlo[:, m % SPL, :]

            def tiles_ready(operand, k):
                pe.wait_ge(S["hi_done"], split_tiles(operand, k))
                pe.wait_ge(S["lo_done"], split_tiles(operand, k))

            def feature_major(name, operand):
                for j in range(KT // 2):
                    w_hi, w_lo = (w.rearrange("p (k n) -> p k n", n=2 * P) for w in parts(name, j))
                    b = begin(UNIT[name] + j)
                    for n in range(2):
                        cut = slice(n * P, (n + 1) * P)
                        for k in range(KT):
                            if j == 0 and n == 0:
                                tiles_ready(operand, k)
                            o = b[:, n * T:(n + 1) * T]
                            nc.tensor.matmul(o, w_hi[:, k, cut], act_hi[:, k, :], start=k == 0, stop=False)
                            nc.tensor.matmul(o, w_hi[:, k, cut], act_lo[:, k, :], start=False, stop=False)
                            last = nc.tensor.matmul(o, w_lo[:, k, cut], act_hi[:, k, :], start=False,
                                                    stop=k == KT - 1)
                    last.then_inc(S["unit_done"], 1)

            def token_major(name, operand):
                banks = [begin(UNIT[name] + i) for i in range(4)]
                for j in range(KT // 2):
                    w_hi, w_lo = (w.rearrange("p (k n) -> p k n", n=D) for w in parts(name, j))
                    tiles_ready(operand, 2 * j + 1)
                    for t in range(TT):
                        mine = slice(t * P, (t + 1) * P)
                        for kk in range(2):
                            k = 2 * j + kk
                            for h in range(2):
                                b, cut = banks[2 * t + h], slice(h * BANK, (h + 1) * BANK)
                                nc.tensor.matmul(b, act_hi[:, k, mine], w_hi[:, kk, cut], start=k == 0, stop=False)
                                nc.tensor.matmul(b, act_hi[:, k, mine], w_lo[:, kk, cut], start=False, stop=False)
                                last = nc.tensor.matmul(b, act_lo[:, k, mine], w_hi[:, kk, cut], start=False,
                                                        stop=k == KT - 1)
                                if k == KT - 1:
                                    last.then_inc(S["unit_done"], 1)
                    if j < KT // 2 - 1:
                        last.then_inc(S["chunk_used"], 1)

            def per_head(name, act_f):
                w = chunk(name, 0).rearrange("p (h k n) -> p h k n", h=HEADS, k=2)
                for h in range(HEADS):
                    b = begin(UNIT[name] + h)
                    for n in range(2):
                        for k in range(2):
                            last = nc.tensor.matmul(b[:, n * T:(n + 1) * T], w[:, h, k, n * P:(n + 1) * P],
                                                    act_f[:, 2 * h + k, :], start=k == 0, stop=k == 1)
                    last.then_inc(S["unit_done"], 1)

            pe.wait_ge(S["in_cst"], 32)
            transposed("memT", mem_rows, 0)
            feature_major("k", "mem")
            token_major("v", "mem")
            transposed("xT", xs_rows, 1)
            feature_major("lrux", "h")
            feature_major("pool", "h")
            pe.wait_ge(S["xr_done"], KT)
            per_head("ra", xr_f)
            per_head("rx", xr_f)
            pe.wait_ge(S["pool_done"], 1)
            per_head("grp", pool_f)
            for name in ("gelu", "ga", "gb"):
                feature_major(name, "h")
            feature_major("pp", "pool")
            feature_major("lp", "lru")
            token_major("mix", "merged")
            transposed("x1T", xn_rows, 2)
            feature_major("q", "xn")
            pe.wait_ge(S["freed_dve"], evacuated(UNIT["q"] + 3)[1])
            for h in range(HEADS):
                b = begin(UNIT["score"] + h)
                for q in range(TT):
                    for k in range(2):
                        last = nc.tensor.matmul(b[:, q * T:(q + 1) * T], q_f[:, 2 * h + k, q * P:(q + 1) * P],
                                                k_f[:, 2 * h + k, :], start=k == 0, stop=k == 1)
                last.then_inc(S["unit_done"], 1)
            for h in range(HEADS):
                pe.wait_ge(S["prob_done"], TT * (h + 1))
                b = begin(UNIT["pT"] + h)
                for m in range(TT):
                    for q in range(TT):
                        at = m * T + q * P
                        last = nc.tensor.transpose(b[:, at:at + P], prob[:, h, q, m * P:(m + 1) * P], ident)
                last.then_inc(S["unit_done"], 1)
            for h in range(HEADS):
                pe.wait_ge(S["freed_act"], evacuated(UNIT["pT"] + h)[1])
                b = begin(UNIT["oT"] + h)
                for n in range(2):
                    for m in range(TT):
                        at = h * HD + n * P
                        last = nc.tensor.matmul(b[:, n * T:(n + 1) * T], v_rows[:, m, at:at + P], probT[:, h, m, :],
                                                start=m == 0, stop=m == TT - 1)
                last.then_inc(S["unit_done"], 1)
            token_major("o", "attn")
            transposed("xnT", xn_rows, 3)
            pe.wait_ge(S["in_router"], 48)
            for j in (2, 3):
                eng, count = evacuated(UNIT["xnT"] + j)
                pe.wait_ge(freed[eng], count)
            b = begin(UNIT["logit"])
            for t in range(TT):
                for k in range(KT):
                    last = nc.tensor.matmul(b[:, t * EXPERTS:(t + 1) * EXPERTS], xn_f[:, k, t * P:(t + 1) * P],
                                            router_w[:, k, :], start=k == 0, stop=k == KT - 1)
            last.then_inc(S["unit_done"], 1)
            pe.wait_ge(S["picked"], 1)
            b = begin(UNIT["rank"])
            lower, whole = mat16[:, 0, :], mat16[:, 1, :]
            for n, terms in enumerate((((lower, 0),), ((whole, 0), (lower, 1)), ((whole, 0), (whole, 1)))):
                for i, (m, t) in enumerate(terms):
                    last = nc.tensor.matmul(b[:, n * EXPERTS:(n + 1) * EXPERTS], m, pick16[:, t, :], start=i == 0,
                                            stop=i == len(terms) - 1)
            last.then_inc(S["unit_done"], 1)
            def chunk_products(r, e, i, pair, tiles, bank, opens, closes):
                n = number(r, e, i) - CHUNKS_0
                pe.wait_ge(S["whi_ready"], n + 1)
                pe.wait_ge(S["wlo_ready"], n + 1)
                pe.wait_ge(S["low_cols_ready"], n + 1)
                for b in range(4):
                    start, stop = b < opens, b >= 4 - closes
                    w = slice(b * BANK, (b + 1) * BANK)
                    nc.tensor.matmul(ps[:, bank(b), :], pair[:, tiles[b], :], whi[:, place(i) % SPL, w], start=start,
                                     stop=False)
                    ins = nc.tensor.matmul(ps[:, bank(b), :], pair[:, tiles[b], :], wlo[:, place(i) % SPL, w],
                                           start=False, stop=stop)
                ins.then_inc(S["chunk_used"], 1)

            def gate_up(r, e, i, k):
                chunk_products(r, e, i, xpair, [k] * 4, lambda b: b, 4 * (k == 0), 4 * (k == KT - 1))

            def down(r, e, i, j):
                chunk_products(r, e, i, hpair, [2 * j, 2 * j, 2 * j + 1, 2 * j + 1], lambda b: 4 + b % 2,
                               2 * (j == 0), 2 * (j == DN_CHUNKS - 1))

            def select(r, e, outputs):
                pe.wait_ge(S["onehot_ready"], (r * BLOCKS + e + 1) * TT)
                pe.wait_ge(S["added"], 2 * (r * BLOCKS + outputs) + 2)
                for k in range(KT):
                    for n in range(3):
                        for t in range(TT):
                            last = nc.tensor.matmul(ps[:, 6, k * SLOTS:(k + 1) * SLOTS],
                                                    xpart[n][:, t, k * P:(k + 1) * P], onehot[:, t, :],
                                                    start=n == 0 and t == 0, stop=n == 2 and t == TT - 1)
                last.then_inc(S["sel_done"], 1)

            def input_ready(r, e):
                pe.wait_ge(S["x_ready"], r * BLOCKS + e + 1)
                pe.wait_ge(S["xhi_ready"], r * BLOCKS + e + 1)
                pe.wait_ge(S["xlo_ready"], r * BLOCKS + e + 1)
                pe.wait_ge(S["gated_out"], (r * EXPERTS + e) * 4 + 4)

            def turn_weights(r, e, bank=4):
                pe.wait_ge(S["wone_ready"], TT * (r * BLOCKS + e))
                for t in range(TT):
                    last = nc.tensor.transpose(ps[:, bank, t * P:(t + 1) * P],
                                               wone[:, t, :, :].rearrange("p two c -> p (two c)"), ident)
                last.then_inc(S["wone_turned"], 1)

            def output(r, e, t, bank=4):
                if t == 0:
                    pe.wait_ge(S["wturned_ready"], r * BLOCKS + e)
                for h in range(2):
                    last = nc.tensor.matmul(ps[:, bank + 2 * t + h, :], wturned[:, t, :],
                                            y_rows[:, h * BANK:(h + 1) * BANK], start=True, stop=True)
                last.then_inc(S["out_done"] if t else S["out_first"], 1)

            def hidden_ready(count):
                pe.wait_ge(S["h_ready"], count)
                pe.wait_ge(S["hhi_ready"], count)
                pe.wait_ge(S["hlo_ready"], count)

            def turn(r, e):
                pe.wait_ge(S["gated_out"], (r * EXPERTS + e) * 4 + 8)
                pe.wait_ge(S["x_ready"], r * BLOCKS + e + 2)
                for j in range(2 * KT):
                    last = nc.tensor.matmul(ps[:, 6 + j // KT, (j % KT) * SLOTS:(j % KT + 1) * SLOTS],
                                            gated[:, j * P:(j + 1) * P], fold, start=True, stop=True)
                last.then_inc(S["turned"], 1)

            pe.wait_ge(S["freed_dve"], evacuated(NUNIT - 1)[1])
            pe.wait_ge(S["part_hi"], 3)
            n = needed_rounds(pe)
            with pe.Fori(0, n) as r:
                select(r, 0, 0)
                input_ready(r, 0)
                for k in range(GU_CHUNKS):
                    gate_up(r, 0, DN_CHUNKS + k, k)
                select(r, 1, 0)
                turn(r, 0)
                with pe.Fori(1, EXPERTS) as e:
                    done = r * EXPERTS + e
                    input_ready(r, e)
                    for k in range(GU_CHUNKS):
                        if k == 2:
                            pe.wait_ge(S["y_ready"], r * BLOCKS + e)
                            turn_weights(r, e)
                        if k == 4:
                            output(r, e, 0)
                        if k == 6:
                            pe.wait_ge(S["up_biased"], done)
                            output(r, e, 1)
                        gate_up(r, e, k, k)
                    select(r, e + 1, e)
                    pe.wait_ge(S["added"], 2 * (r * BLOCKS + e) + 1)
                    hidden_ready(done)
                    for j in range(DN_CHUNKS):
                        if j == 2:
                            turn(r, e)
                        down(r, e, GU_CHUNKS + j, j)
                turn_weights(r, EXPERTS, 2)

                def weighted_biases(t, bank):
                    for h in range(2):
                        last = nc.tensor.matmul(ps[:, bank + h, :], gT[:, t * P:(t + 1) * P],
                                                bdown_sb[:, h * BANK:(h + 1) * BANK], start=True, stop=True)
                    last.then_inc(S["bd_done"], 1)

                pe.wait_ge(S["y_ready"], r * BLOCKS + EXPERTS)
                output(r, EXPERTS, 0, 0)
                hidden_ready((r + 1) * EXPERTS)
                down(r, EXPERTS, 0, 0)
                output(r, EXPERTS, 1, 0)
                down(r, EXPERTS, 1, 1)
                pe.wait_ge(S["up_biased"], (r + 1) * EXPERTS)
                with pe.If(r < 1):
                    pe.wait_ge(S["gmat_done"], TT)
                    pe.wait_ge(S["in_router"], 48)
                    for t in range(TT):
                        last = nc.tensor.transpose(ps[0:EXPERTS, 7, t * P:(t + 1) * P], gmat[:, t, 1:EXPERTS + 1],
                                                   ident)
                    last.then_inc(S["gT_turned"], 1)
                down(r, EXPERTS, 2, 2)
                pe.wait_ge(S["added"], 2 * (r * BLOCKS + EXPERTS) + 2)
                turn_weights(r, EXPERTS + 1, 0)
                with pe.If(r < 1):
                    pe.wait_ge(S["gT_out"], 1)
                    weighted_biases(0, 6)
                down(r, EXPERTS, 3, 3)
                with pe.If(r < 1):
                    weighted_biases(1, 2)
                pe.wait_ge(S["y_ready"], r * BLOCKS + EXPERTS + 1)
                pe.wait_ge(S["wturned_ready"], r * BLOCKS + EXPERTS + 1)
                pe.wait_ge(S["bd_added"], 1)
                for t in range(TT):
                    output(r, EXPERTS + 1, t)


INPUTS = ("x", "mem", "cols", "consts", "dense", "bgu", "b_router", "w_router", "norm_final", "w_gate_up", "w_down",
          "b_down")


def kernel(x, mem, norm_mix, w_in, w_pool_group, pool_scale, w_pool_proj, conv_w, conv_b, lru_w_a, lru_b_a, lru_w_x,
           lru_b_x, lru_lambda, w_lru_proj, w_mix_out, norm_xattn, norm_mem, w_q, w_kv, w_o, norm_moe, w_router,
           b_router, w_gate_up, b_gate_up, w_down, b_down, norm_final):
    import numpy as np
    import concourse.bacc as bacc
    from concourse.bass_utils import run_bass_kernel_spmd

    a = {k: np.asarray(v) for k, v in locals().items() if k not in ("np", "bacc", "run_bass_kernel_spmd")}
    one = lambda name: a[name][0]
    tiles = lambda v: v.reshape(-1, P).T
    cols = np.concatenate([tiles(one(n)) for n in COLS[:-1]] + [tiles(one("conv_w").reshape(-1))], 1)
    consts = np.zeros((P, NCONST), np.float32)
    part = lambda name: consts[:, CONST[name][0]:CONST[name][1]]
    part("ident")[:] = np.eye(P)
    part("fold")[:] = np.concatenate([np.eye(SLOTS)] * 2)
    part("before")[:] = np.triu(np.ones((P, P)), 1)
    part("ones")[:] = 1
    part("iota")[:] = np.arange(T)
    part("inv")[:] = np.concatenate([w / np.minimum(np.arange(PAD) + 1, w) for w in WINDOWS])

    def by_columns(w):
        return w.reshape(KT, P, -1, 2 * P).transpose(2, 1, 0, 3).reshape(-1, P, CHUNK)

    def by_rows(w):
        return w.reshape(KT // 2, 2, P, D).transpose(0, 2, 1, 3).reshape(-1, P, CHUNK)

    def by_heads(w):
        return w.reshape(HEADS, 2, P, HD).transpose(2, 0, 1, 3).reshape(1, P, CHUNK)

    w_in_ = one("w_in")
    kv = one("w_kv")
    section = lambda i: by_columns(w_in_[:, i * D:(i + 1) * D])
    stages = {"k": by_columns(kv[:, :D]), "v": by_rows(kv[:, D:]), "lrux": section(1), "pool": section(0),
              "ra": by_heads(one("lru_w_a")), "rx": by_heads(one("lru_w_x")), "grp": by_heads(one("w_pool_group")),
              "gelu": section(2), "ga": section(3), "gb": section(4), "pp": by_columns(one("w_pool_proj")),
              "lp": by_columns(one("w_lru_proj")), "mix": by_rows(one("w_mix_out")), "q": by_columns(one("w_q")),
              "o": by_rows(one("w_o"))}
    dense = np.concatenate([stages[n] for n in DENSE], 0)
    arrays = {"x": a["x"][0], "mem": a["mem"][0], "cols": cols, "consts": consts, "dense": dense,
              "bgu": one("b_gate_up").reshape(EXPERTS, 2 * KT, P).transpose(2, 0, 1),
              "b_router": np.broadcast_to(one("b_router"), (P, EXPERTS)), "w_router": one("w_router"),
              "norm_final": np.broadcast_to(a["norm_final"], (P, D)),
              "w_gate_up": one("w_gate_up").reshape(EXPERTS * D, 2 * D),
              "w_down": one("w_down").reshape(EXPERTS * D, D),
              "b_down": one("b_down")}
    arrays = {k: np.ascontiguousarray(arrays[k]) for k in INPUTS}
    nc = bacc.Bacc("TRN2", target_bir_lowering=False, num_devices=1)
    args = {k: nc.dram_tensor(f"in_{k}", v.shape, mybir.dt.from_np(v.dtype), kind="ExternalInput").ap()
            for k, v in arrays.items()}
    args["out"] = nc.dram_tensor("out", (T, D), F32, kind="ExternalOutput").ap()
    build(nc, **args)
    r = run_bass_kernel_spmd(nc, [{f"in_{k}": v for k, v in arrays.items()}], core_ids=[0])
    return r.results[0]["out"].reshape(1, T, D)
```
